# Optimizing a Trainium2 kernel written in Bass

```python
import jax, jax.numpy as jnp
from jax import lax
import numpy as np
import math

D_MODEL = 1024
BATCH = 1
SEQ = 512
DEPTH = 2

GRID_W = 64
CTX_LEN = 256
EPS = 1e-6
POOL_WINDOWS = (2, 4, 8, 16)
POOL_GROUPS = len(POOL_WINDOWS)
POOL_GROUP_DIM = D_MODEL // 8
POOL_WIDTH = POOL_GROUPS * POOL_GROUP_DIM
SGU_HEADS = 4
SGU_HEAD_DIM = D_MODEL // 8
SGU_WIDTH = SGU_HEADS * SGU_HEAD_DIM
CHUNK = 128
AB_IN = 2 * POOL_WIDTH + 3 * SGU_WIDTH
AB_MIX = POOL_WIDTH + SGU_WIDTH
FNET_HEADS = 4
FNET_HEAD_DIM = D_MODEL // 8
FNET_WIDTH = FNET_HEADS * FNET_HEAD_DIM
MLA_HEADS = 8
QK_NOPE = 64
QK_ROPE = 32
V_DIM = 64
Q_LORA = D_MODEL // 4
KV_LORA = D_MODEL // 8
MLA_WIDTH = MLA_HEADS * V_DIM
CD_IN = 2 * FNET_WIDTH + Q_LORA + KV_LORA + QK_ROPE + MLA_WIDTH
CD_MIX = FNET_WIDTH + MLA_WIDTH
ROPE_AXIS = QK_ROPE // 2
ROPE_BASE = 10000.0
Q_BLOCK = 128
ALPHA = (2 * DEPTH) ** 0.25
BETA = (8 * DEPTH) ** -0.25
N_EVEN = (DEPTH + 1) // 2
N_ODD = DEPTH // 2


def _layer_norm(x, g, b):
    xf = x.astype(jnp.float32)
    mu = jnp.mean(xf, axis=-1, keepdims=True)
    var = jnp.mean(jnp.square(xf - mu), axis=-1, keepdims=True)
    return ((xf - mu) * lax.rsqrt(var + EPS) * g + b).astype(x.dtype)

def _rms_norm(x, g):
    xf = x.astype(jnp.float32)
    y = xf * lax.rsqrt(jnp.mean(jnp.square(xf), axis=-1, keepdims=True) + EPS)
    return (y * g).astype(x.dtype)

def _adaln(cond, w_mod, b_mod):
    m = jax.nn.silu(cond) @ w_mod + b_mod
    return jnp.split(m, 3, axis=-1)

def _post_norm(x, y, gate, g, b):
    return _layer_norm(ALPHA * x + gate * y, g, b)

def _multiscale_pool(a, pool_w, pool_scale):
    bn, L, _ = a.shape
    cs = jnp.cumsum(a.astype(jnp.float32), axis=1)
    cs = jnp.pad(cs, ((0, 0), (1, 0), (0, 0)))
    t = jnp.arange(L)
    outs = []
    for g, w in enumerate(POOL_WINDOWS):
        lo = jnp.clip(t - w // 2, 0, L)
        hi = jnp.clip(t + w - w // 2, 0, L)
        seg = cs[:, :, g * POOL_GROUP_DIM:(g + 1) * POOL_GROUP_DIM]
        s = jnp.take(seg, hi, axis=1) - jnp.take(seg, lo, axis=1)
        outs.append(s / (hi - lo).astype(jnp.float32)[None, :, None])
    pooled = jnp.concatenate(outs, axis=-1).astype(a.dtype)
    d = (pooled - a).reshape(bn, L, POOL_GROUPS, POOL_GROUP_DIM)
    y = jnp.einsum('blgc,gcd->blgd', d, pool_w).reshape(bn, L, POOL_WIDTH)
    return y * pool_scale

def _chunk_sgu(u, v, w_s, b_s):
    bn, L, _ = v.shape
    nc = L // CHUNK
    vh = v.reshape(bn, L, SGU_HEADS, SGU_HEAD_DIM).astype(jnp.float32)
    mu = jnp.mean(vh, axis=-1, keepdims=True)
    var = jnp.mean(jnp.square(vh - mu), axis=-1, keepdims=True)
    vn = ((vh - mu) * lax.rsqrt(var + EPS)).astype(v.dtype)
    vn = vn.reshape(bn, nc, CHUNK, SGU_HEADS, SGU_HEAD_DIM)
    f = jnp.einsum('hij,bnjhc->bnihc', w_s, vn) + jnp.swapaxes(b_s, 0, 1)[:, :, None]
    return u * f.reshape(bn, L, SGU_WIDTH)

def _ab_mixer(h, w_in, pool_w, pool_scale, sgu_w, sgu_b, w_out):
    z = h @ w_in
    a, ga, u, v, gb = jnp.split(z, [POOL_WIDTH, 2 * POOL_WIDTH, 2 * POOL_WIDTH + SGU_WIDTH,
                                    2 * POOL_WIDTH + 2 * SGU_WIDTH], axis=-1)
    ya = _multiscale_pool(a, pool_w, pool_scale) * jax.nn.silu(ga)
    yb = _chunk_sgu(u, v, sgu_w, sgu_b) * jax.nn.silu(gb)
    return jnp.concatenate([ya, yb], axis=-1) @ w_out

def _fourier_mix(f, w_f):
    bn, L, _ = f.shape
    fh = f.reshape(bn, L, FNET_HEADS, FNET_HEAD_DIM).astype(jnp.float32)
    spec = jnp.fft.fft2(fh, axes=(1, 3), norm="ortho").real
    return spec.astype(f.dtype).reshape(bn, L, FNET_WIDTH) @ w_f

def _axial_tables(L, dtype):
    rows = L // GRID_W
    row = jnp.repeat(jnp.arange(rows), GRID_W).astype(jnp.float32)
    col = jnp.tile(jnp.arange(GRID_W), rows).astype(jnp.float32)
    inv = ROPE_BASE ** (-jnp.arange(0, ROPE_AXIS, 2, dtype=jnp.float32) / ROPE_AXIS)
    ang_r = (row[:, None] * inv)[:, None, :]
    ang_c = (col[:, None] * inv)[:, None, :]
    return (jnp.cos(ang_r).astype(dtype), jnp.sin(ang_r).astype(dtype),
            jnp.cos(ang_c).astype(dtype), jnp.sin(ang_c).astype(dtype))

def _rotate(x, cos, sin):
    half = x.shape[-1] // 2
    x1, x2 = x[..., :half], x[..., half:]
    return jnp.concatenate([x1 * cos - x2 * sin, x1 * sin + x2 * cos], axis=-1)

def _axial_rope(x, rope):
    cos_r, sin_r, cos_c, sin_c = rope
    return jnp.concatenate([_rotate(x[..., :ROPE_AXIS], cos_r, sin_r),
                            _rotate(x[..., ROPE_AXIS:], cos_c, sin_c)], axis=-1)

def _split_cd(z):
    o1 = FNET_WIDTH
    o2 = o1 + FNET_WIDTH
    o3 = o2 + Q_LORA
    o4 = o3 + KV_LORA
    o5 = o4 + QK_ROPE
    return jnp.split(z, [o1, o2, o3, o4, o5], axis=-1)

def _mla_q(cq, q_norm, w_q_up, rope):
    bn, L, _ = cq.shape
    q = (_rms_norm(cq, q_norm) @ w_q_up).reshape(bn, L, MLA_HEADS, QK_NOPE + QK_ROPE)
    if rope is not None:
        q = jnp.concatenate([q[..., :QK_NOPE], _axial_rope(q[..., QK_NOPE:], rope)], axis=-1)
    return q

def _mla_kv(ckv, kr, kv_norm, w_kv_up, rope):
    bn, L, _ = ckv.shape
    kv = (_rms_norm(ckv, kv_norm) @ w_kv_up).reshape(bn, L, MLA_HEADS, QK_NOPE + V_DIM)
    k_nope, v = kv[..., :QK_NOPE], kv[..., QK_NOPE:]
    kr = kr[:, :, None, :]
    if rope is not None:
        kr = _axial_rope(kr, rope)
    k = jnp.concatenate([k_nope, jnp.broadcast_to(kr, (bn, L, MLA_HEADS, QK_ROPE))], axis=-1)
    return k, v

def _block_attention(q, k, v):
    bn, L, H, dk = q.shape
    nb = L // Q_BLOCK
    scale = dk ** -0.5
    qb = q.reshape(bn, nb, Q_BLOCK, H, dk).transpose(1, 0, 2, 3, 4)

    def one(qi):
        s = jnp.einsum('bqhd,bkhd->bhqk', qi, k, preferred_element_type=jnp.float32) * scale
        p = jax.nn.softmax(s, axis=-1).astype(v.dtype)
        return jnp.einsum('bhqk,bkhd->bqhd', p, v)

    o = lax.map(one, qb)
    return o.transpose(1, 0, 2, 3, 4).reshape(bn, L, H * V_DIM)

def _cd_out(f_in, f_gate, attn, d_gate, fnet_w, w_out):
    yc = _fourier_mix(f_in, fnet_w) * jax.nn.silu(f_gate)
    yd = attn * jax.nn.silu(d_gate)
    return jnp.concatenate([yc, yd], axis=-1) @ w_out

def first_inputs(seed: int = 0) -> dict:
    key = jax.random.key(seed)
    ks = jax.random.split(key, 32)

    def nrm(k, shape, scale):
        return jax.random.normal(k, shape, jnp.float32) * scale

    D = D_MODEL
    H = MLA_HEADS
    return {
        "x": nrm(ks[0], (BATCH, SEQ, D), 1.0),
        "c": nrm(ks[1], (BATCH, D), 1.0),
        "ctx": nrm(ks[2], (BATCH, CTX_LEN, D), 1.0),
        "c_ctx": nrm(ks[3], (D,), 1.0),
        "ab_w_mod": nrm(ks[4], (N_EVEN, D, 3 * D), 0.5 * D ** -0.5),
        "ab_b_mod": nrm(ks[5], (N_EVEN, 3 * D), 0.01),
        "ab_w_in": nrm(ks[6], (N_EVEN, D, AB_IN), D ** -0.5),
        "ab_pool_w": nrm(ks[7], (N_EVEN, POOL_GROUPS, POOL_GROUP_DIM, POOL_GROUP_DIM), POOL_GROUP_DIM ** -0.5),
        "ab_pool_scale": 1.0 + nrm(ks[8], (N_EVEN, POOL_WIDTH), 0.1),
        "ab_sgu_w": nrm(ks[9], (N_EVEN, SGU_HEADS, CHUNK, CHUNK), CHUNK ** -0.5),
        "ab_sgu_b": 1.0 + nrm(ks[10], (N_EVEN, SGU_HEADS, CHUNK), 0.01),
        "ab_w_out": nrm(ks[11], (N_EVEN, AB_MIX, D), BETA * AB_MIX ** -0.5),
        "ab_ln_g": 1.0 + nrm(ks[12], (N_EVEN, D), 0.1),
        "ab_ln_b": nrm(ks[13], (N_EVEN, D), 0.01),
        "cd_w_mod": nrm(ks[14], (N_ODD, D, 3 * D), 0.5 * D ** -0.5),
        "cd_b_mod": nrm(ks[15], (N_ODD, 3 * D), 0.01),
        "cd_w_in": nrm(ks[16], (N_ODD, D, CD_IN), D ** -0.5),
        "cd_fnet_w": nrm(ks[17], (N_ODD, FNET_WIDTH, FNET_WIDTH), FNET_WIDTH ** -0.5),
        "cd_q_norm": 1.0 + nrm(ks[18], (N_ODD, Q_LORA), 0.1),
        "cd_kv_norm": 1.0 + nrm(ks[19], (N_ODD, KV_LORA), 0.1),
        "cd_w_q_up": nrm(ks[20], (N_ODD, Q_LORA, H * (QK_NOPE + QK_ROPE)), Q_LORA ** -0.5),
        "cd_w_kv_up": nrm(ks[21], (N_ODD, KV_LORA, H * (QK_NOPE + V_DIM)), KV_LORA ** -0.5),
        "cd_w_out": nrm(ks[22], (N_ODD, CD_MIX, D), BETA * CD_MIX ** -0.5),
        "cd_ln_g": 1.0 + nrm(ks[23], (N_ODD, D), 0.1),
        "cd_ln_b": nrm(ks[24], (N_ODD, D), 0.01),
    }

def first_block(x, c, ctx, c_ctx,
              ab_w_mod, ab_b_mod, ab_w_in, ab_pool_w, ab_pool_scale, ab_sgu_w, ab_sgu_b,
              ab_w_out, ab_ln_g, ab_ln_b,
              cd_w_mod, cd_b_mod, cd_w_in, cd_fnet_w, cd_q_norm, cd_kv_norm, cd_w_q_up,
              cd_w_kv_up, cd_w_out, cd_ln_g, cd_ln_b):
    L = x.shape[1]
    rope = _axial_tables(L, x.dtype)
    for i in range(DEPTH):
        last = i == DEPTH - 1
        j = i // 2
        if i % 2 == 0:
            sh, sc, gt = _adaln(c, ab_w_mod[j], ab_b_mod[j])
            h = x * (1.0 + sc[:, None]) + sh[:, None]
            y = _ab_mixer(h, ab_w_in[j], ab_pool_w[j], ab_pool_scale[j], ab_sgu_w[j], ab_sgu_b[j], ab_w_out[j])
            if not last:
                csh, csc, cgt = _adaln(c_ctx, ab_w_mod[j], ab_b_mod[j])
                hc = ctx * (1.0 + csc) + csh
                yc = _ab_mixer(hc, ab_w_in[j], ab_pool_w[j], ab_pool_scale[j], ab_sgu_w[j], ab_sgu_b[j], ab_w_out[j])
                ctx = _post_norm(ctx, yc, cgt, ab_ln_g[j], ab_ln_b[j])
            x = _post_norm(x, y, gt[:, None], ab_ln_g[j], ab_ln_b[j])
        else:
            csh, csc, cgt = _adaln(c_ctx, cd_w_mod[j], cd_b_mod[j])
            hc = ctx * (1.0 + csc) + csh
            fc_in, fc_gate, cq_c, ckv_c, kr_c, dc_gate = _split_cd(hc @ cd_w_in[j])
            k_ctx, v_ctx = _mla_kv(ckv_c, kr_c, cd_kv_norm[j], cd_w_kv_up[j], None)
            sh, sc, gt = _adaln(c, cd_w_mod[j], cd_b_mod[j])
            h = x * (1.0 + sc[:, None]) + sh[:, None]
            f_in, f_gate, cq, ckv, kr, d_gate = _split_cd(h @ cd_w_in[j])
            k_lat, v_lat = _mla_kv(ckv, kr, cd_kv_norm[j], cd_w_kv_up[j], rope)
            q = _mla_q(cq, cd_q_norm[j], cd_w_q_up[j], rope)
            attn = _block_attention(q, jnp.concatenate([k_ctx, k_lat], axis=1),
                                    jnp.concatenate([v_ctx, v_lat], axis=1))
            y = _cd_out(f_in, f_gate, attn, d_gate, cd_fnet_w[j], cd_w_out[j])
            if not last:
                qc = _mla_q(cq_c, cd_q_norm[j], cd_w_q_up[j], None)
                attn_c = _block_attention(qc, k_ctx, v_ctx)
                yc = _cd_out(fc_in, fc_gate, attn_c, dc_gate, cd_fnet_w[j], cd_w_out[j])
                ctx = _post_norm(ctx, yc, cgt, cd_ln_g[j], cd_ln_b[j])
            x = _post_norm(x, y, gt[:, None], cd_ln_g[j], cd_ln_b[j])
    return x


CHUNK_2 = 64
HEAD_DIM = 64
N_HEADS_TOTAL = D_MODEL // HEAD_DIM
N_HEADS_B = N_HEADS_TOTAL // 4
N_HEADS_A = (N_HEADS_TOTAL - N_HEADS_B) // 2
N_HEADS_C = N_HEADS_TOTAL - N_HEADS_A - N_HEADS_B
DIFF_QK_DIM = HEAD_DIM // 2
DIFF_V_DIM = HEAD_DIM
WIDTH_A = N_HEADS_A * HEAD_DIM
WIDTH_B = N_HEADS_B * DIFF_V_DIM
WIDTH_C = N_HEADS_C * HEAD_DIM
B_QK_WIDTH = N_HEADS_B * 2 * DIFF_QK_DIM
D_MIX = WIDTH_A + WIDTH_B + WIDTH_C
IN_COLS = 3 * WIDTH_A + 2 * B_QK_WIDTH + WIDTH_B + 3 * WIDTH_C
LEFT_CHUNKS = 8
BAND = (LEFT_CHUNKS + 1) * CHUNK_2
REL_CLIP = 128
D_FF = 2816
NORM_EPS = 1e-6
NEG_INF = -1e30
FFN_RESIDUAL_WEIGHT = 0.5


def rmsnorm(x, g):
    xf = x.astype(jnp.float32)
    y = xf * lax.rsqrt(jnp.mean(xf * xf, axis=-1, keepdims=True) + NORM_EPS)
    return (y * g.astype(jnp.float32)).astype(x.dtype)

def swiglu(x, w_gate, w_up, w_down):
    return (jax.nn.silu(x @ w_gate) * (x @ w_up)) @ w_down

def chunk_band_attention(q, k, v, rel_bias):
    b, s, h, d = q.shape
    nc = s // CHUNK_2
    qc = q.reshape(b, nc, CHUNK_2, h, d)
    pad = ((0, 0), (LEFT_CHUNKS, 0), (0, 0), (0, 0), (0, 0))
    kp = jnp.pad(k.reshape(b, nc, CHUNK_2, h, d), pad)
    vp = jnp.pad(v.reshape(b, nc, CHUNK_2, h, d), pad)
    kband = jnp.concatenate([kp[:, w:w + nc] for w in range(LEFT_CHUNKS + 1)], axis=2)
    vband = jnp.concatenate([vp[:, w:w + nc] for w in range(LEFT_CHUNKS + 1)], axis=2)
    qi = jnp.arange(CHUNK_2)
    kk = jnp.arange(BAND)
    rel = jnp.clip(qi[:, None] + LEFT_CHUNKS * CHUNK_2 - kk[None, :], -REL_CLIP, REL_CLIP) + REL_CLIP
    bias = rel_bias[:, rel].astype(jnp.float32)
    valid = (jnp.arange(nc)[:, None] - LEFT_CHUNKS + kk[None, :] // CHUNK_2) >= 0
    scores = jnp.einsum('bnqhd,bnkhd->bnhqk', qc, kband).astype(jnp.float32) * (d ** -0.5)
    scores = scores + bias[None, None]
    scores = jnp.where(valid[None, :, None, None, :], scores, NEG_INF)
    p = jax.nn.softmax(scores, axis=-1).astype(v.dtype)
    o = jnp.einsum('bnhqk,bnkhd->bnqhd', p, vband)
    return o.reshape(b, s, h, d)

def diff_attention(q, k, v, lam, subln_g, lambda_init):
    b, s, h, _, dq = q.shape
    scale = dq ** -0.5
    slopes = jnp.exp2(-8.0 * jnp.arange(1, h + 1, dtype=jnp.float32) / h)
    outs = []
    for blk in range(s // Q_BLOCK):
        q0 = blk * Q_BLOCK
        kend = q0 + Q_BLOCK
        tpos = q0 + jnp.arange(Q_BLOCK)
        spos = jnp.arange(kend)
        allowed = (spos[None, :] // CHUNK_2) <= (tpos[:, None] // CHUNK_2)
        dist = jnp.abs(tpos[:, None] - spos[None, :]).astype(jnp.float32)
        alibi = -slopes[:, None, None] * dist[None]
        sc = jnp.einsum('bqhmd,bkhmd->bhmqk', q[:, q0:kend], k[:, :kend]).astype(jnp.float32) * scale
        sc = sc + alibi[None, :, None]
        sc = jnp.where(allowed[None, None, None], sc, NEG_INF)
        p = jax.nn.softmax(sc, axis=-1)
        w = p[:, :, 0] - lam * p[:, :, 1]
        outs.append(jnp.einsum('bhqk,bkhd->bqhd', w.astype(v.dtype), v[:, :kend]))
    o = jnp.concatenate(outs, axis=1)
    return rmsnorm(o, subln_g) * (1.0 - lambda_init)

def stick_breaking_attention(q, k, v):
    b, s, h, d = q.shape
    scale = d ** -0.5
    outs = []
    for blk in range(s // Q_BLOCK):
        q0 = blk * Q_BLOCK
        kend = q0 + Q_BLOCK
        tpos = q0 + jnp.arange(Q_BLOCK)
        spos = jnp.arange(kend)
        strict = spos[None, :] < tpos[:, None]
        z = jnp.einsum('bqhd,bkhd->bhqk', q[:, q0:kend], k[:, :kend]).astype(jnp.float32) * scale
        log_beta = jax.nn.log_sigmoid(z)
        log_one_minus = jnp.where(strict, jax.nn.log_sigmoid(-z), 0.0)
        suffix = lax.cumsum(log_one_minus, axis=3, reverse=True) - log_one_minus
        a = jnp.where(strict, jnp.exp(log_beta + suffix), 0.0)
        outs.append(jnp.einsum('bhqk,bkhd->bqhd', a.astype(v.dtype), v[:, :kend]))
    return jnp.concatenate(outs, axis=1)

def token_mixing(h, w_in, rel_bias, lq1, lk1, lq2, lk2, subln_g, w_out, lambda_init):
    b, s, _ = h.shape
    proj = h @ w_in
    sizes = [WIDTH_A, WIDTH_A, WIDTH_A, B_QK_WIDTH, B_QK_WIDTH, WIDTH_B, WIDTH_C, WIDTH_C, WIDTH_C]
    qa, ka, va, qb, kb, vb, qc, kc, vc = jnp.split(proj, [int(c) for c in np.cumsum(sizes)[:-1]], axis=-1)
    hd_a = (b, s, N_HEADS_A, HEAD_DIM)
    o_a = chunk_band_attention(qa.reshape(hd_a), ka.reshape(hd_a), va.reshape(hd_a), rel_bias)
    lam = (jnp.exp(jnp.sum(lq1.astype(jnp.float32) * lk1.astype(jnp.float32)))
           - jnp.exp(jnp.sum(lq2.astype(jnp.float32) * lk2.astype(jnp.float32))) + lambda_init)
    hd_bqk = (b, s, N_HEADS_B, 2, DIFF_QK_DIM)
    o_b = diff_attention(qb.reshape(hd_bqk), kb.reshape(hd_bqk), vb.reshape(b, s, N_HEADS_B, DIFF_V_DIM),
                         lam, subln_g, lambda_init)
    hd_c = (b, s, N_HEADS_C, HEAD_DIM)
    o_c = stick_breaking_attention(qc.reshape(hd_c), kc.reshape(hd_c), vc.reshape(hd_c))
    y = jnp.concatenate([o_a.reshape(b, s, WIDTH_A), o_b.reshape(b, s, WIDTH_B),
                         o_c.reshape(b, s, WIDTH_C)], axis=-1)
    return y @ w_out

def second_inputs(seed: int = 0) -> dict:
    key = jax.random.key(seed)
    ks = jax.random.split(key, 32)
    f32 = jnp.float32

    def nrm(k, shape, scale):
        return jax.random.normal(k, shape, f32) * scale

    def gain(k, shape):
        return 1.0 + 0.05 * jax.random.normal(k, shape, f32)

    L = DEPTH
    return {
        "x": jax.random.normal(ks[0], (BATCH, SEQ, D_MODEL), f32),
        "ffn1_pre_g": gain(ks[1], (L, D_MODEL)),
        "ffn1_w_gate": nrm(ks[2], (L, D_MODEL, D_FF), D_MODEL ** -0.5),
        "ffn1_w_up": nrm(ks[3], (L, D_MODEL, D_FF), D_MODEL ** -0.5),
        "ffn1_w_down": nrm(ks[4], (L, D_FF, D_MODEL), D_FF ** -0.5),
        "ffn1_post_g": gain(ks[5], (L, D_MODEL)),
        "mix_pre_g": gain(ks[6], (L, D_MODEL)),
        "w_in": nrm(ks[7], (L, D_MODEL, IN_COLS), D_MODEL ** -0.5),
        "rel_bias": nrm(ks[8], (L, N_HEADS_A, 2 * REL_CLIP + 1), 0.2),
        "diff_lambda_q1": nrm(ks[9], (L, DIFF_QK_DIM), 0.1),
        "diff_lambda_k1": nrm(ks[10], (L, DIFF_QK_DIM), 0.1),
        "diff_lambda_q2": nrm(ks[11], (L, DIFF_QK_DIM), 0.1),
        "diff_lambda_k2": nrm(ks[12], (L, DIFF_QK_DIM), 0.1),
        "diff_subln_g": gain(ks[13], (L, DIFF_V_DIM)),
        "w_out": nrm(ks[14], (L, D_MIX, D_MODEL), D_MIX ** -0.5),
        "mix_post_g": gain(ks[15], (L, D_MODEL)),
        "ffn2_pre_g": gain(ks[16], (L, D_MODEL)),
        "ffn2_w_gate": nrm(ks[17], (L, D_MODEL, D_FF), D_MODEL ** -0.5),
        "ffn2_w_up": nrm(ks[18], (L, D_MODEL, D_FF), D_MODEL ** -0.5),
        "ffn2_w_down": nrm(ks[19], (L, D_FF, D_MODEL), D_FF ** -0.5),
        "ffn2_post_g": gain(ks[20], (L, D_MODEL)),
    }

def second_block(x, ffn1_pre_g, ffn1_w_gate, ffn1_w_up, ffn1_w_down, ffn1_post_g,
              mix_pre_g, w_in, rel_bias, diff_lambda_q1, diff_lambda_k1, diff_lambda_q2,
              diff_lambda_k2, diff_subln_g, w_out, mix_post_g,
              ffn2_pre_g, ffn2_w_gate, ffn2_w_up, ffn2_w_down, ffn2_post_g):
    for l in range(DEPTH):
        lambda_init = 0.8 - 0.6 * math.exp(-0.3 * l)
        f = swiglu(rmsnorm(x, ffn1_pre_g[l]), ffn1_w_gate[l], ffn1_w_up[l], ffn1_w_down[l])
        x = x + FFN_RESIDUAL_WEIGHT * rmsnorm(f, ffn1_post_g[l])
        m = token_mixing(rmsnorm(x, mix_pre_g[l]), w_in[l], rel_bias[l],
                         diff_lambda_q1[l], diff_lambda_k1[l], diff_lambda_q2[l], diff_lambda_k2[l],
                         diff_subln_g[l], w_out[l], lambda_init)
        x = x + rmsnorm(m, mix_post_g[l])
        f = swiglu(rmsnorm(x, ffn2_pre_g[l]), ffn2_w_gate[l], ffn2_w_up[l], ffn2_w_down[l])
        x = x + FFN_RESIDUAL_WEIGHT * rmsnorm(f, ffn2_post_g[l])
    return x


def setup_inputs(seed=0):
    out = dict(first_inputs(seed))
    for name, value in second_inputs(seed + 1).items():
        if name != "x":
            out[name + "_2"] = value
    return out


def reference(
    x, c, ctx, c_ctx, ab_w_mod, ab_b_mod, ab_w_in, ab_pool_w, ab_pool_scale, ab_sgu_w, ab_sgu_b,
    ab_w_out, ab_ln_g, ab_ln_b, cd_w_mod, cd_b_mod, cd_w_in, cd_fnet_w, cd_q_norm, cd_kv_norm,
    cd_w_q_up, cd_w_kv_up, cd_w_out, cd_ln_g, cd_ln_b, ffn1_pre_g_2, ffn1_w_gate_2, ffn1_w_up_2,
    ffn1_w_down_2, ffn1_post_g_2, mix_pre_g_2, w_in_2, rel_bias_2, diff_lambda_q1_2,
    diff_lambda_k1_2, diff_lambda_q2_2, diff_lambda_k2_2, diff_subln_g_2, w_out_2, mix_post_g_2,
    ffn2_pre_g_2, ffn2_w_gate_2, ffn2_w_up_2, ffn2_w_down_2, ffn2_post_g_2,
):
    x = first_block(
        x, c, ctx, c_ctx, ab_w_mod, ab_b_mod, ab_w_in, ab_pool_w, ab_pool_scale, ab_sgu_w,
        ab_sgu_b, ab_w_out, ab_ln_g, ab_ln_b, cd_w_mod, cd_b_mod, cd_w_in, cd_fnet_w, cd_q_norm,
        cd_kv_norm, cd_w_q_up, cd_w_kv_up, cd_w_out, cd_ln_g, cd_ln_b,
    )
    return second_block(
        x, ffn1_pre_g_2, ffn1_w_gate_2, ffn1_w_up_2, ffn1_w_down_2, ffn1_post_g_2, mix_pre_g_2,
        w_in_2, rel_bias_2, diff_lambda_q1_2, diff_lambda_k1_2, diff_lambda_q2_2,
        diff_lambda_k2_2, diff_subln_g_2, w_out_2, mix_post_g_2, ffn2_pre_g_2, ffn2_w_gate_2,
        ffn2_w_up_2, ffn2_w_down_2, ffn2_post_g_2,
    )


_drawn_inputs = setup_inputs


def setup_inputs(seed=0):
    import zlib

    import numpy as np

    out = dict(_drawn_inputs(seed))
    spreads = {}
    factors = {'ctx': 8.0,
     'c_ctx': 5.279,
     'ab_b_mod': 8.0,
     'ab_pool_scale': 8.0,
     'ab_sgu_b': 8.0,
     'cd_b_mod': 8.0,
     'cd_q_norm': 8.0,
     'cd_kv_norm': 8.0,
     'cd_w_q_up': 6.632,
     'diff_lambda_k1_2': 8.0,
     'rel_bias_2': 2.681}
    for name, (base, spread) in spreads.items():
        noise = np.random.default_rng([zlib.crc32(name.encode()), seed]).standard_normal(out[name].shape)
        drawn = base * np.exp(spread * noise) if base else spread * noise
        out[name] = __import__('jax').numpy.asarray(drawn.astype(out[name].dtype))
    for name, factor in factors.items():
        out[name] = (out[name] * factor).astype(out[name].dtype)
    return out
```

```python
from contextlib import ExitStack
import math

import numpy as np

import concourse.bass as bass
from concourse import mybir

F32 = mybir.dt.float32
F32R = mybir.dt.float32r
ACT = mybir.ActivationFunctionType
ALU = mybir.AluOpType
AX = mybir.AxisListType

P = 128
D = 1024
KT = D // P
L = 512
LC = 256
LA = L + LC
NT = L // P
NC = LC // P
BANK = 512
EPS = 1e-6
DEPTH = 2
ALPHA = (2 * DEPTH) ** 0.25
POOL_WINDOWS = (2, 4, 8, 16)
HALO = 8
FF = 2816
FT = FF // P
NOPE, ROPE, HEADS = 64, 32, 8
QK = NOPE + ROPE
NEG = -1e30
CW = 256

VECS = [("ab_b_mod", 24), ("cd_b_mod", 24), ("c", 8), ("c_ctx", 8), ("ab_pool_scale", 4),
        ("cd_q_norm", 2), ("cd_kv_norm", 1), ("ffn1_pre_g_2", 16), ("mix_pre_g_2", 16),
        ("ffn2_pre_g_2", 16)]
VOFF = {}
for _n, _k in VECS:
    VOFF[_n] = sum(k for m, k in VECS[:[n for n, _ in VECS].index(_n)])
NVEC = sum(k for _, k in VECS)


class Engine:

    def __init__(self, sem):
        self.sem, self.count, self.queue, self.seen = sem, 0, [], {}

    def wait(self, marks):
        for sem, value in marks:
            if value > self.seen.get(id(sem), 0):
                self.seen[id(sem)] = value
                self.queue.append(lambda eng, s=sem, v=value: eng.wait_ge(s, v))

    def op(self, build, after=(), mark=True):
        self.wait(after)
        if not mark:
            self.queue.append(build)
            return None
        self.count += 1
        self.queue.append(lambda eng, b=build, s=self.sem: b(eng).then_inc(s, 1))
        return (self.sem, self.count)

    def now(self):
        return [(self.sem, self.count)] if self.count else []


class Slot:

    def __init__(self, *tiles):
        self.tiles, self.free = tiles, []


class Ring:
    def __init__(self, slots):
        self.slots, self.at = slots, 0

    def take(self):
        self.at += 1
        return self.slots[(self.at - 1) % len(self.slots)]


def build(nc, A, out):
    ctx = ExitStack()
    names = [0]

    def sem(name):
        return ctx.enter_context(nc.semaphore(name))

    def sb(scope, name, shape, dt=F32):
        names[0] += 1
        return scope.enter_context(nc.sbuf_tensor(f"{name}_{names[0]}", shape, dt))

    with ctx:
        pe, act, dve, pool = (Engine(sem(n)) for n in ("pe_done", "act_done", "dve_done", "pool_done"))
        sp = Engine(None)
        dma_sems = []

        def load(dst, src, after=(), s=None):
            if s is None:
                s = [sem(f"landed_{len(dma_sems)}"), 0]
                dma_sems.append(s)
            s[1] += 16
            sp.wait(after)
            sp.queue.append(lambda eng, s0=s[0]: eng.dma_start(dst, src).then_inc(s0, 16))
            return (s[0], s[1])

        psum = ctx.enter_context(nc.psum_tensor("psum", [P, 8 * BANK], F32))
        bank_free = {b: [] for b in range(8)}

        def bank(b, n=BANK, off=0):
            return psum[:, b * BANK + off:b * BANK + off + n]

        raw_ring = Ring([Slot(sb(ctx, "raw", [P, 2048]), [sem(f"raw_landed_{i}"), 0]) for i in range(2)])
        split_ring = Ring([Slot(sb(ctx, "w_hi", [P, 2048], F32R), sb(ctx, "w_lo", [P, 2048], F32R))
                           for _ in range(2)])
        X = sb(ctx, "X", [P, NT, D])
        cols = sb(ctx, "cols", [P, NVEC])
        ident = sb(ctx, "ident", [P, P])
        ones = sb(ctx, "ones", [P, P])
        half = sb(ctx, "minus_half", [P, 8])
        work_ring = Ring([Slot(sb(ctx, "work", [P, BANK])) for _ in range(4)])
        stat_ring = Ring([Slot(sb(ctx, "stat", [P, 64])) for _ in range(8)])

        def fence():
            marks = pe.now() + act.now() + dve.now() + pool.now()
            for e in (pe, act, dve, pool, sp):
                e.wait([m for m in marks if m[0] is not e.sem])
            for e in (act, dve, pool):
                e.wait(e.now())
            return marks

        plan = []

        def kview(t, nk):
            return t[:, :].rearrange("p (k n) -> p k n", k=nk)

        def add_cols(w, c0, n, split=True):
            plan.append((w[:, c0:c0 + n].rearrange("(k p) n -> p k n", p=P), KT, n, split))

        def add_rows(w, r0):
            plan.append((w[r0:r0 + 2 * P, :].rearrange("(k p) n -> p k n", p=P), 2, D, True))

        def add_down(w, rows):
            for r in range(0, rows, 2 * P):
                add_rows(w, r)

        for c0 in range(0, 3 * D, CW):
            add_cols(A["ab_w_mod"][0], c0, CW, False)
        for c0 in range(0, 2560, CW):
            add_cols(A["ab_w_in"][0], c0, CW)
        add_down(A["ab_w_out"][0], D)
        add_down(A["ab_w_out"][0], D)
        for c0 in range(0, 3 * D, CW):
            add_cols(A["cd_w_mod"][0], c0, CW, False)
        for c0, n in ((0, 256), (256, 256), (512, 256), (768, 256), (1024, 256), (1280, 160), (1440, 256), (1696, 256)):
            add_cols(A["cd_w_in"][0], c0, n)
        for c0 in (0, 256):
            plan.append((A["cd_fnet_w"][0][:, c0:c0 + 256].rearrange("(k p) n -> p k n", p=P), 4, 256, True))
        add_down(A["cd_w_out"][0], D)
        MIX_CHUNKS = [(0, 256), (256, 256), (512, 256), (768, 256), (1024, 128), (1152, 256), (1408, 256),
                      (1664, 256), (1920, 256), (2176, 256), (2432, 256), (2688, 256), (2944, 128)]
        for layer in range(DEPTH):
            for f in (1, 2):
                if f == 2:
                    for c0, n in MIX_CHUNKS:
                        add_cols(A["w_in_2"][layer], c0, n)
                    add_down(A["w_out_2"][layer], D)
                for c0 in range(0, FF, CW):
                    add_cols(A[f"ffn{f}_w_gate_2"][layer], c0, CW)
                    add_cols(A[f"ffn{f}_w_up_2"][layer], c0, CW)
                add_down(A[f"ffn{f}_w_down_2"][layer], FF)

        class Chunk:
            pass

        st = {"loaded": 0, "prepared": 0, "used": 0, "raws": [], "ready": [], "last": None}

        def load_chunk():
            if st["loaded"] >= len(plan):
                return
            src, nk, n, _ = plan[st["loaded"]]
            st["loaded"] += 1
            slot = raw_ring.take()
            dst = slot.tiles[0][:, 0:nk * n].rearrange("p (k n) -> p k n", k=nk)
            st["raws"].append((slot, load(dst, src, slot.free, slot.tiles[1])))

        def prepare_chunk():
            if st["prepared"] >= len(plan):
                return
            _, nk, n, split = plan[st["prepared"]]
            st["prepared"] += 1
            if not st["raws"]:
                load_chunk()
            raw_slot, landed = st["raws"].pop(0)
            raw = raw_slot.tiles[0]
            c = Chunk()
            c.nk, c.n, c.split, c.raw_slot = nk, n, split, raw_slot
            if split:
                slot = split_ring.take()
                hi, lo = slot.tiles
                w = nk * n
                made_hi = act.op(lambda e: e.activation(hi[:, 0:w], raw[:, 0:w], ACT.Copy),
                                 [landed] + slot.free)
                made_lo = dve.op(lambda e: e.tensor_tensor(lo[:, 0:w], raw[:, 0:w], hi[:, 0:w].bitcast(F32),
                                                           ALU.subtract), [landed, made_hi] + slot.free)
                raw_slot.free = [made_lo]
                load_chunk()
                c.slot, c.ready = slot, [made_lo, made_hi]
                c.hi = hi[:, 0:w].rearrange("p (k n) -> p k n", k=nk)
                c.lo = lo[:, 0:w].rearrange("p (k n) -> p k n", k=nk)
            else:
                c.slot, c.ready = raw_slot, [landed]
                c.raw = raw[:, 0:nk * n].rearrange("p (k n) -> p k n", k=nk)
            st["ready"].append(c)

        def next_chunk():
            if st["last"] is not None:
                st["last"].slot.free = pe.now()
                if not st["last"].split:
                    load_chunk()
            if not st["ready"]:
                prepare_chunk()
            c = st["ready"].pop(0)
            st["last"] = c
            if st["prepared"] < len(plan) and (c.split or not plan[st["prepared"]][3]):
                prepare_chunk()
            return c

        load_chunk()
        load_chunk()

        def mm(o, lhsT, rhs, start, stop, after=(), mark=False):
            return pe.op(lambda e: e.matmul(o, lhsT, rhs, start=start, stop=stop, skip_group_check=True), after, mark)

        def mm3(o, st_hi, st_lo, mv_hi, mv_lo, start, stop, after=(), mark=False):
            mm(o, st_hi, mv_hi, start, False, after)
            mm(o, st_hi, mv_lo, False, False)
            return mm(o, st_lo, mv_hi, False, stop, (), mark)

        def tt(eng, o, a, b, op, after=()):
            return eng.op(lambda e: e.tensor_tensor(o, a, b, op), after)

        def ts(o, a, s1, s2, op0, op1, after=()):
            if op1 is None:
                return dve.op(lambda e: e.tensor_scalar(o, a, s1, None, op0), after)
            return dve.op(lambda e: e.tensor_scalar(o, a, s1, s2, op0, op1), after)

        def stt(o, a, s, b, op0, op1, after=()):
            return dve.op(lambda e: e.scalar_tensor_tensor(out=o, in0=a, scalar=s, in1=b, op0=op0, op1=op1), after)

        def actv(o, a, func, after=(), **kw):
            return act.op(lambda e: e.activation(o, a, func, **kw), after)

        def split_pair(hi, lo, src, after):
            made_hi = actv(hi, src, ACT.Copy, after)
            made_lo = tt(dve, lo, src, hi.bitcast(F32), ALU.subtract, [made_hi] + list(after))
            return [made_hi, made_lo]

        def work(n=BANK):
            slot = work_ring.take()
            return slot, slot.tiles[0][:, 0:n]

        def stat():
            slot = stat_ring.take()
            return slot, slot.tiles[0]

        def rsqrt(o, a, n, scale, after):
            biased = ts(a, a, scale, EPS, ALU.mult, ALU.add, after)
            return tt(pool, o, a, half[:, 0:n], ALU.pow, [biased, made_half])

        vec_scope = ExitStack()
        vec_rows = sb(vec_scope, "vec_rows", [NVEC, P])
        vec_landed = [sem("vectors_landed"), 0]
        for name, k in VECS:
            src = A[name]
            while len(src.shape) > 1:
                src = src.rearrange("a b -> (a b)") if len(src.shape) == 2 else src.rearrange("a b c -> (a b c)")
            vecs_in = load(vec_rows[VOFF[name]:VOFF[name] + k, :], src.rearrange("(k p) -> k p", p=P), s=vec_landed)
        ident_in = load(ident[:, :], A["k_ident"])
        x_in = load(X[:, :, :], A["x"][0].rearrange("(t p) d -> p t d", p=P))
        made_ones = pool.op(lambda e: e.memset(ones[:, :], 1.0))
        made_half = pool.op(lambda e: e.memset(half[:, :], -0.5))
        t = pe.op(lambda e: e.transpose(bank(0, NVEC), vec_rows[:, :], ident[0:NVEC, 0:NVEC]),
                  [vecs_in, ident_in])
        cols_in = dve.op(lambda e: e.tensor_copy(cols[:, :], bank(0, NVEC)), [t])
        bank_free[0] = [cols_in]
        fence()
        vec_scope.close()

        def col(name, k, n=1):
            return cols[:, VOFF[name] + k:VOFF[name] + k + n]

        first = ExitStack()
        silu_c = sb(first, "silu_c", [P, KT, 2])
        mod = sb(first, "mod", [P, 24, 2])
        scale1 = sb(first, "one_plus_scale", [P, KT, 2])
        gate_rows = sb(first, "gate_rows", [P, 2, D])

        def adaln(bias_name):
            for s, name in enumerate(("c", "c_ctx")):
                ready = actv(silu_c[:, :, s], col(name, 0, 8), ACT.Silu, [cols_in])
            o = bank(1, 48)
            for ch in range(3 * D // CW):
                c = next_chunk()
                for j in range(CW // P):
                    for k in range(KT):
                        jj = ch * 2 + j
                        m = mm(o[:, 2 * jj:2 * jj + 2], c.raw[:, k, j * P:(j + 1) * P], silu_c[:, k, :],
                               k == 0, k == KT - 1, c.ready + [ready] + bank_free[1], mark=k == KT - 1)
            ov = o.rearrange("p (j s) -> p j s", s=2)
            m = tt(dve, mod[:, :, :], ov, col(bias_name, 0, 24).unsqueeze(2).broadcast_to([P, 24, 2]), ALU.add, [m])
            bank_free[1] = [m]
            return [m, ts(scale1[:, :, :], mod[:, 8:16, :], 1.0, None, ALU.add, None, [m])]

        def gate_row(s, after):
            for h in range(2):
                b = 2 + h
                for j in range(4):
                    slot, diag = work(P)
                    d = ts(diag, ident[:, :], mod[:, 16 + 4 * h + j, s:s + 1], None, ALU.mult, None, list(after) + slot.free)
                    m = mm(bank(b, P, j * P), ones[:, :], diag, True, True, [d, made_ones] + bank_free[b], mark=True)
                    slot.free = [m]
                g = actv(gate_rows[:, s, h * BANK:(h + 1) * BANK], bank(b), ACT.Copy, [m])
                bank_free[b] = [g]
            return g

        rot = Ring(list(range(8)))

        def take1():
            return rot.take()

        def take2():
            if rot.at % 2:
                rot.take()
            b = rot.take()
            rot.take()
            return b

        def turn(src, T, dst_hi, dst_lo, off, scale, shift, after):
            marks = []
            for h in range(2):
                b = take1()
                for k in range(4):
                    m = pe.op(lambda e, k=k, h=h, b=b: e.transpose(bank(b, P, k * P), src[:, (4 * h + k) * P:(4 * h + k + 1) * P],
                                                                  ident[:, :]), list(after) + bank_free[b], mark=k == 3)
                slot, w = work()
                wv = w.rearrange("p (k n) -> p k n", k=4)
                pv = bank(b).rearrange("p (k n) -> p k n", k=4)
                d = tt(dve, wv, pv, scale[:, 4 * h:4 * h + 4].unsqueeze(2).broadcast_to([P, 4, P]), ALU.mult, [m] + slot.free)
                bank_free[b] = [d]
                if shift is not None:
                    d = tt(dve, wv, wv, shift[:, 4 * h:4 * h + 4].unsqueeze(2).broadcast_to([P, 4, P]), ALU.add, [d])
                slot.free = split_pair(dst_hi[:, 4 * h:4 * h + 4, off:off + P], dst_lo[:, 4 * h:4 * h + 4, off:off + P], wv, [d])
                marks += slot.free
            return marks

        def project(c, j, n, hi, lo, ranges, ready, sink):
            for r, (off, width) in enumerate(ranges):
                b = take1()
                for k in range(KT):
                    m = mm3(psum[0:n, b * BANK:b * BANK + width], c.hi[:, k, j:j + n], c.lo[:, k, j:j + n],
                            hi[:, k, off:off + width], lo[:, k, off:off + width], k == 0, k == KT - 1,
                            c.ready + list(ready) + bank_free[b], mark=k == KT - 1)
                bank_free[b] = sink(r, psum[0:n, b * BANK:b * BANK + width], m)

        def project_tokens(c, hi, lo, tiles, ready, sink, banks=None):
            for t_ in tiles:
                b = take1()
                for k in range(KT):
                    m = mm3(bank(b, c.n), hi[:, k, t_ * P:(t_ + 1) * P], lo[:, k, t_ * P:(t_ + 1) * P],
                            c.hi[:, k, :], c.lo[:, k, :], k == 0, k == KT - 1,
                            c.ready + list(ready) + bank_free[b], mark=k == KT - 1)
                bank_free[b] = sink(t_, bank(b, c.n), m)

        def down(nk, hi, lo, offs, ready, sink):
            for ch in range(nk // 2):
                c = next_chunk()
                for i, off in enumerate(offs):
                    for h in range(2):
                        b = 2 * i + h
                        for kk in range(2):
                            k = 2 * ch + kk
                            m = mm3(bank(b), hi[:, k, off:off + P], lo[:, k, off:off + P],
                                    c.hi[:, kk, h * BANK:(h + 1) * BANK], c.lo[:, kk, h * BANK:(h + 1) * BANK],
                                    k == 0, k == nk - 1, c.ready + list(ready) + bank_free[b], mark=kk == 1)
                    if ch == nk // 2 - 1:
                        bank_free[2 * i] = bank_free[2 * i + 1] = sink(i, psum[:, 2 * i * BANK:(2 * i + 2) * BANK], m)
            rot.at = 0

        def residual_layer_norm(dst, y, grow, g_row, b_row, after):
            done = []
            for h in range(2):
                slot, w = work()
                sl = slice(h * BANK, (h + 1) * BANK)
                m = tt(dve, w, y[:, sl], grow[:, sl], ALU.mult, list(after) + slot.free)
                done.append(m)
                m = stt(dst[:, sl], dst[:, sl], ALPHA, w, ALU.mult, ALU.add, [m])
                slot.free = [m]
            slot, s_ = stat()
            for h in range(2):
                st_m = dve.op(lambda e, h=h: e.bn_stats(s_[:, 6 * h:6 * h + 6], dst[:, h * BANK:(h + 1) * BANK]), [m] + slot.free)
            agg = dve.op(lambda e: e.bn_aggr(s_[:, 12:14], s_[:, 0:12]), [st_m])
            r = rsqrt(s_[:, 14:15], s_[:, 13:14], 1, 1.0, [agg])
            n = ts(dst, dst, s_[:, 12:13], s_[:, 14:15], ALU.subtract, ALU.mult, [r, agg])
            slot.free = [n]
            g = tt(dve, dst, dst, g_row, ALU.mult, [n] + rows_ready)
            return done, tt(dve, dst, dst, b_row, ALU.add, [g])

        ctx_scope, ab = ExitStack(), ExitStack()
        h_hi = sb(first, "h_hi", [P, KT, LA], F32R)
        h_lo = sb(first, "h_lo", [P, KT, LA], F32R)
        CTX = sb(ctx_scope, "CTX", [P, NC, D])
        ctx_in = load(CTX[:, :, :], A["ctx"][0].rearrange("(t p) d -> p t d", p=P))
        pooled_in = sb(ab, "pool_in", [P, 4, HALO * 3 + LA])
        silu_ga = sb(ab, "silu_ga", [P, 4, LA])
        u_gated = sb(ab, "u_gated", [P, 4, LA])
        v_norm = sb(ab, "v_norm", [P, 6, BANK])
        pool_w = sb(ab, "pool_w", [P, 4, P])
        sgu_w = sb(ab, "sgu_w", [P, 4, P])
        sgu_wT = sb(ab, "sgu_wT", [P, 4, P])
        sgu_b = sb(ab, "sgu_b", [1, 4 * P])
        RANGES = ((0, L), (L, LC))
        PAD_OFF = (HALO, 2 * HALO + L)
        pool_w_in = load(pool_w[:, :, :], A["ab_pool_w"][0].rearrange("g c d -> c g d"))
        sgu_w_in = load(sgu_w[:, :, :], A["ab_sgu_w"][0].rearrange("h i j -> i h j"))
        sgu_b_in = load(sgu_b[:, :], A["ab_sgu_b"].rearrange("a h i -> a (h i)"))
        zeroed = pool.op(lambda e: e.memset(pooled_in[:, :, :], 0.0))
        for h in range(4):
            m = pe.op(lambda e, h=h: e.transpose(bank(4, P, h * P), sgu_w[:, h, :], ident[:, :]), [sgu_w_in], mark=h == 3)
        sgu_w_ready = dve.op(lambda e: e.tensor_copy(sgu_wT[:, :, :].rearrange("p h i -> p (h i)"), bank(4)), [m])
        bank_free[4] = [sgu_w_ready]

        def modulate(mod_ready, n_ctx_first=0):
            marks = []
            for t_ in range(NT):
                marks += turn(X[:, t_, :], None, h_hi, h_lo, t_ * P, scale1[:, :, 0], mod[:, 0:8, 0], [x_in] + list(mod_ready))
            for t_ in range(NC):
                marks += turn(CTX[:, t_, :], None, h_hi, h_lo, L + t_ * P, scale1[:, :, 1], mod[:, 0:8, 1], [ctx_in] + list(mod_ready))
            return marks

        mod_ready = adaln("ab_b_mod")
        gates_ready = [gate_row(0, mod_ready), gate_row(1, mod_ready)]
        h_ready = modulate(mod_ready)
        a_marks, ga_marks, u_marks, v_marks = [], [], [], []
        for ch in range(10):
            c = next_chunk()
            if ch in (6, 7):
                def v_sink(t_, ps, m, ch=ch):
                    slot, s_ = stat()
                    for j in range(2):
                        o = 20 * j
                        a = dve.op(lambda e, j=j, o=o: e.bn_stats(s_[:, o:o + 6], ps[:, j * P:(j + 1) * P]), [m] + slot.free)
                        a = dve.op(lambda e, o=o: e.bn_aggr(s_[:, o + 6:o + 8], s_[:, o:o + 6]), [a])
                        r = rsqrt(s_[:, o + 8:o + 9], s_[:, o + 7:o + 8], 1, 1.0, [a])
                        hd = 2 * (ch - 6) + j
                        d = ts(v_norm[:, t_, hd * P:(hd + 1) * P], ps[:, j * P:(j + 1) * P], s_[:, o + 6:o + 7],
                               s_[:, o + 8:o + 9], ALU.subtract, ALU.mult, [r, a])
                    slot.free = [d]
                    v_marks.append(d)
                    return [d]
                project_tokens(c, h_hi, h_lo, range(6), h_ready, v_sink)
                continue
            for j in range(2):
                g = 2 * (ch % 2) + j
                if ch < 2:
                    def sink(r, ps, m, g=g):
                        d = actv(pooled_in[:, g, PAD_OFF[r]:PAD_OFF[r] + RANGES[r][1]], ps, ACT.Copy, [m, zeroed])
                        a_marks.append(d)
                        return [d]
                elif ch < 4:
                    def sink(r, ps, m, g=g):
                        o, n = RANGES[r]
                        d = actv(silu_ga[:, g, o:o + n], ps, ACT.Silu, [m])
                        ga_marks.append(d)
                        return [d]
                elif ch < 6:
                    def sink(r, ps, m, g=g):
                        o, n = RANGES[r]
                        d = actv(u_gated[:, g, o:o + n], ps, ACT.Copy, [m])
                        u_marks.append(d)
                        return [d]
                else:
                    def sink(r, ps, m, g=g):
                        o, n = RANGES[r]
                        slot, w = work(n)
                        s_ = actv(w, ps, ACT.Silu, [m] + slot.free)
                        d = tt(dve, u_gated[:, g, o:o + n], u_gated[:, g, o:o + n], w, ALU.mult, [s_] + u_marks)
                        slot.free = [d]
                        u_marks.append(d)
                        return [s_]
                project(c, j * P, P, h_hi, h_lo, RANGES, h_ready, sink)

        h_read = pe.now()
        sums = sb(ab, "window_sums", [P, 2, LA + 3 * HALO])
        inv_cnt = sb(ab, "inv_count", [P, LA])
        cnt_sem = [sem("inv_count_landed"), 0]
        mix_marks, prev = [], []
        for g, w in enumerate(POOL_WINDOWS):
            cnt_in = load(inv_cnt[:, :], A["k_inv_count"][g].partition_broadcast(P), prev, s=cnt_sem)
            src, width, m = pooled_in[:, g, :], LA + 3 * HALO, a_marks + prev
            span = 1
            side = 0
            while span < w:
                width -= span
                dst = sums[:, side, :]
                m = [tt(dve, dst[:, 0:width], src[:, 0:width], src[:, span:span + width], ALU.add, m)]
                src, side, span = dst, 1 - side, 2 * span
            for r, (off, n) in enumerate(RANGES):
                o = PAD_OFF[r] - w // 2
                slot, wk = work(n)
                d = tt(dve, wk, src[:, o:o + n], inv_cnt[:, off:off + n], ALU.mult, m + [cnt_in] + slot.free)
                d = tt(dve, wk, wk, pooled_in[:, g, PAD_OFF[r]:PAD_OFF[r] + n], ALU.subtract, [d])
                b = take1()
                q = mm(bank(b, n), pool_w[:, g, :], wk, True, True, [d, pool_w_in] + bank_free[b], mark=True)
                d = stt(wk, bank(b, n), col("ab_pool_scale", g), silu_ga[:, g, off:off + n], ALU.mult, ALU.mult, [q] + ga_marks)
                bank_free[b] = [d]
                slot.free = split_pair(h_hi[:, g, off:off + n], h_lo[:, g, off:off + n], wk, [d] + h_read)
                mix_marks += slot.free
                prev = [d]
        for hd in range(4):
            for r, (off, n) in enumerate(RANGES):
                b = take1()
                for q in range(n // P):
                    ck = off // P + q
                    mm(bank(b, P, q * P), v_norm[:, ck, hd * P:(hd + 1) * P], sgu_wT[:, hd, :], True, False,
                       v_marks + [sgu_w_ready] + bank_free[b])
                    m = mm(bank(b, P, q * P), ones[0:1, :], sgu_b[0:1, hd * P:(hd + 1) * P], False, True, [sgu_b_in], mark=True)
                slot, wk = work(n)
                d = tt(dve, wk, bank(b, n), u_gated[:, hd, off:off + n], ALU.mult, [m] + u_marks + slot.free)
                bank_free[b] = [d]
                slot.free = split_pair(h_hi[:, 4 + hd, off:off + n], h_lo[:, 4 + hd, off:off + n], wk, [d] + h_read)
                mix_marks += slot.free
        fence()
        ab.close()

        tail = ExitStack()
        g_row = sb(tail, "g_row", [P, D])
        b_row = sb(tail, "b_row", [P, D])
        row_sems = [[sem("g_row_landed"), 0], [sem("b_row_landed"), 0]]
        rows_ready = [load(g_row[:, :], A["ab_ln_g"][0].partition_broadcast(P), pe.now() + dve.now() + act.now(), s=row_sems[0]),
                      load(b_row[:, :], A["ab_ln_b"][0].partition_broadcast(P), s=row_sems[1])]
        x_marks, c_marks = [], []

        def x_sink(i, y, m):
            done, ready = residual_layer_norm(X[:, i, :], y, gate_rows[:, 0, :], g_row[:, :], b_row[:, :], [m] + gates_ready)
            x_marks.append(ready)
            return done

        def c_sink(i, y, m):
            done, ready = residual_layer_norm(CTX[:, i, :], y, gate_rows[:, 1, :], g_row[:, :], b_row[:, :], [m] + gates_ready)
            c_marks.append(ready)
            return done

        down(KT, h_hi, h_lo, [t_ * P for t_ in range(NT)], mix_marks, x_sink)
        down(KT, h_hi, h_lo, [L + t_ * P for t_ in range(NC)], mix_marks, c_sink)
        fence()
        tail.close()

        mod_ready = adaln("cd_b_mod")
        gates_ready = [gate_row(0, mod_ready)]
        h_ready = modulate(list(mod_ready) + x_marks + c_marks)
        fence()
        ctx_scope.close()
        cd = ExitStack()
        silu_dg = sb(cd, "silu_dgate", [P, 4, L])
        cqT = sb(cd, "cqT", [P, 2, L])
        ckvT = sb(cd, "ckvT", [P, LA])
        krT = sb(cd, "krT", [P, LA])
        fourier = ExitStack()
        f_in = sb(fourier, "f_in", [P, 4, L])
        silu_fg = sb(fourier, "silu_fgate", [P, 4, L])
        dft_d = sb(fourier, "dft_d", [P, 2 * P])
        dft_l = sb(fourier, "dft_l", [P, 4, 2, L])
        f_cs = sb(fourier, "f_cs", [P, NT, 2 * P])
        spec_hi, spec_lo = h_hi[:, 4:8, 0:L], h_lo[:, 4:8, 0:L]
        dft_in = [load(dft_d[:, :], A["k_dft_d"], pe.now() + dve.now() + act.now()), load(dft_l[:, :, :, :], A["k_dft_l"].rearrange("(t p) s l -> p t s l", p=P))]
        f_marks, fg_marks, dg_marks, lat_marks = [], [], [], []
        nrm = ExitStack()
        for ch in range(8):
            c = next_chunk()
            if ch == 4:
                def q_sink(t_, ps, m):
                    slot, s_ = stat()
                    ws, w = work(256)
                    sq = actv(w, ps, ACT.Square, [m] + slot.free + ws.free, accum_out=s_[:, 0:1])
                    r = rsqrt(s_[:, 1:2], s_[:, 0:1], 1, 1.0 / 256, [sq])
                    d = ts(w, ps, s_[:, 1:2], None, ALU.mult, None, [r, sq])
                    slot.free = [d]
                    b = take1()
                    for k in range(2):
                        q = pe.op(lambda e, k=k: e.transpose(bank(b, P, k * P), w[:, k * P:(k + 1) * P], ident[:, :]),
                                  [d] + bank_free[b], mark=True)
                    ws.free = [q]
                    for k in range(2):
                        d2 = ts(cqT[:, k, t_ * P:(t_ + 1) * P], bank(b, P, k * P), col("cd_q_norm", k), None, ALU.mult, None, [q])
                    bank_free[b] = [d2]
                    lat_marks.append(d2)
                    return [d]
                project_tokens(c, h_hi, h_lo, range(NT), h_ready, q_sink)
                continue
            if ch == 5:
                def kv_sink(t_, ps, m):
                    slot, s_ = stat()
                    ws, w = work(160)
                    sq = actv(w[:, 0:P], ps[:, 0:P], ACT.Square, [m] + slot.free + ws.free, accum_out=s_[:, 0:1])
                    r = rsqrt(s_[:, 1:2], s_[:, 0:1], 1, 1.0 / P, [sq])
                    d = ts(w[:, 0:P], ps[:, 0:P], s_[:, 1:2], None, ALU.mult, None, [r, sq])
                    d3 = dve.op(lambda e: e.tensor_copy(w[:, P:160], ps[:, P:160]), [m])
                    slot.free = [d]
                    b = take1()
                    pe.op(lambda e: e.transpose(bank(b, P), w[:, 0:P], ident[:, :]), [d, d3] + bank_free[b], mark=False)
                    q = pe.op(lambda e: e.transpose(psum[0:QK, b * BANK + P:b * BANK + 2 * P], w[:, 64:160], ident[:, :]))
                    ws.free = [q]
                    d2 = ts(ckvT[:, t_ * P:(t_ + 1) * P], bank(b, P), col("cd_kv_norm", 0), None, ALU.mult, None, [q])
                    d4 = dve.op(lambda e: e.tensor_copy(krT[0:QK, t_ * P:(t_ + 1) * P], psum[0:QK, b * BANK + P:b * BANK + 2 * P]), [q])
                    bank_free[b] = [d4]
                    lat_marks.extend([d2, d4])
                    return [d3]
                project_tokens(c, h_hi, h_lo, range(6), h_ready, kv_sink)
                continue
            for j in range(2):
                g = 2 * (ch % 2) + j

                def sink(r, ps, m, g=g, ch=ch):
                    if ch < 2:
                        d = actv(f_in[:, g, :], ps, ACT.Copy, [m])
                        f_marks.append(d)
                    elif ch < 4:
                        d = actv(silu_fg[:, g, :], ps, ACT.Silu, [m])
                        fg_marks.append(d)
                    else:
                        d = actv(silu_dg[:, g, :], ps, ACT.Silu, [m])
                        dg_marks.append(d)
                    return [d]
                project(c, j * P, P, h_hi, h_lo, RANGES[:1], h_ready, sink)
        h_read = pe.now()

        mix_marks, spec_marks, cs_free = [], [], []
        for hd in range(4):
            cs_marks = []
            for t_ in range(NT):
                b = take1()
                m = mm(bank(b, 256), f_in[:, hd, t_ * P:(t_ + 1) * P], dft_d[:, :], True, True, f_marks + dft_in + bank_free[b], mark=True)
                d = actv(f_cs[:, t_, :], bank(b, 256), ACT.Copy, [m] + cs_free)
                bank_free[b] = [d]
                cs_marks.append(d)
            b = take1()
            for t_ in range(NT):
                for s in range(2):
                    m = mm(bank(b), f_cs[:, t_, s * P:(s + 1) * P], dft_l[:, t_, s, :], t_ == 0 and s == 0, t_ == 3 and s == 1,
                           cs_marks + bank_free[b], mark=True)
            cs_free = [m]
            bank_free[b] = split_pair(spec_hi[:, hd, :], spec_lo[:, hd, :], bank(b), [m] + h_read)
            spec_marks += bank_free[b]
        for ch in range(2):
            c = next_chunk()
            for j in range(2):
                b = take1()
                for k in range(4):
                    m = mm3(bank(b), c.hi[:, k, j * P:(j + 1) * P], c.lo[:, k, j * P:(j + 1) * P], spec_hi[:, k, :], spec_lo[:, k, :],
                            k == 0, k == 3, c.ready + spec_marks + bank_free[b], mark=k == 3)
                g = 2 * ch + j
                slot, w = work()
                d = tt(dve, w, bank(b), silu_fg[:, g, :], ALU.mult, [m] + fg_marks + slot.free)
                bank_free[b] = [d]
                slot.free = split_pair(h_hi[:, g, 0:L], h_lo[:, g, 0:L], w, [d] + h_read)
                mix_marks += slot.free
        f = fence()
        fourier.close()

        mla = ExitStack()
        q_up = sb(mla, "q_up", [P, 2, HEADS * QK])
        kv_up = sb(mla, "kv_up", [P, D])
        rope_c = sb(mla, "rope_cos", [QK, L])
        rope_s = sb(mla, "rope_sin", [QK, L])
        swap = sb(mla, "rope_swap", [QK, QK])
        v_all = sb(mla, "v_all", [P, 6, HEADS * 64])
        head_ring = Ring([Slot(sb(mla, "kT_head", [QK, LA]), sb(mla, "qT_head", [QK, L])) for _ in range(2)])
        p_ring = Ring([Slot(sb(mla, "probs", [P, LA])) for _ in range(2)])
        pT_ring = Ring([Slot(sb(mla, "probsT", [P, LA])) for _ in range(2)])
        o_tok = sb(mla, "o_tok", [P, NT, HEADS * 64])
        mla_in = [load(q_up[:, :, :], A["cd_w_q_up"][0].rearrange("(k p) n -> p k n", p=P), f),
                  load(kv_up[:, :], A["cd_w_kv_up"][0]), load(rope_c[:, :], A["k_rope_cos"]),
                  load(rope_s[:, :], A["k_rope_sin"]), load(swap[:, :], A["k_rope_swap"])]

        def rope(t_, after):
            b = take1()
            o = psum[0:QK, b * BANK:(b + 1) * BANK]
            m = mm(o, swap[:, :], t_[0:QK, 0:L], True, True, list(after) + mla_in + bank_free[b], mark=True)
            slot, w = work()
            d = tt(dve, w[0:QK, :], o, rope_s[:, :], ALU.mult, [m] + slot.free)
            bank_free[b] = [d]
            d2 = tt(dve, t_[0:QK, 0:L], t_[0:QK, 0:L], rope_c[:, :], ALU.mult, [m])
            d = tt(dve, t_[0:QK, 0:L], t_[0:QK, 0:L], w[0:QK, :], ALU.add, [d, d2])
            slot.free = [d]
            return d

        kr_ready = rope(krT, lat_marks)
        v_marks = []
        v_cols = kv_up[:, :].rearrange("p (h c) -> p h c", h=HEADS)[:, :, NOPE:P]
        for t_ in range(6):
            b = take1()
            m = mm(bank(b).rearrange("p (h c) -> p h c", h=HEADS), ckvT[:, t_ * P:(t_ + 1) * P], v_cols, True, True,
                   lat_marks + mla_in + bank_free[b], mark=True)
            d = actv(v_all[:, t_, :], bank(b), ACT.Copy, [m])
            bank_free[b] = [d]
            v_marks.append(d)
        SC = QK ** -0.5
        o_marks = []

        def head_tensors(hd):
            slot = head_ring.take()
            kT, qT = slot.tiles
            for off, n in RANGES:
                b = take1()
                m = mm(psum[0:NOPE, b * BANK:b * BANK + n], kv_up[:, hd * P:hd * P + NOPE], ckvT[:, off:off + n], True, True,
                       lat_marks + mla_in + bank_free[b], mark=True)
                k_up = actv(kT[0:NOPE, off:off + n], psum[0:NOPE, b * BANK:b * BANK + n], ACT.Copy, [m] + slot.free)
                bank_free[b] = [k_up]
            kr = pool.op(lambda e: e.tensor_copy(kT[NOPE:QK, :], krT[NOPE:QK, :]), [kr_ready] + lat_marks + slot.free)
            b = take1()
            for k in range(2):
                m = mm(psum[0:QK, b * BANK:(b + 1) * BANK], q_up[:, k, hd * QK:(hd + 1) * QK], cqT[:, k, :], k == 0, k == 1,
                       bank_free[b], mark=True)
            q = actv(qT[:, :], psum[0:QK, b * BANK:(b + 1) * BANK], ACT.Copy, [m] + slot.free)
            bank_free[b] = [q]
            q = rope(qT, [q])
            return slot, kT, qT, [k_up, kr, q]

        items = []
        heads = {}

        def mla_scores(hd, t_):
            if t_ == 0:
                heads[hd] = head_tensors(hd)
            slot, kT, qT, ready = heads[hd]
            b = take2()
            for j, (off, n) in enumerate(RANGES):
                m = mm(bank(b + j, n), qT[:, t_ * P:(t_ + 1) * P], kT[:, off:off + n], True, True, ready + bank_free[b + j], mark=True)
            if t_ == NT - 1:
                slot.free = [m]
            s = psum[:, b * BANK:b * BANK + LA]
            sslot, s_ = stat()
            mx = dve.op(lambda e: e.tensor_reduce(s_[:, 0:1], s, AX.X, ALU.max), [m] + sslot.free)
            nm = ts(s_[:, 1:2], s_[:, 0:1], -SC, None, ALU.mult, None, [mx])
            ps = p_ring.take()
            pr = ps.tiles[0]
            ex = actv(pr[:, :], s, ACT.Exp, [nm] + ps.free, bias=s_[:, 1:2], scale=SC, accum_out=s_[:, 2:3])
            bank_free[b] = bank_free[b + 1] = [ex]
            rc = dve.op(lambda e: e.reciprocal(s_[:, 3:4], s_[:, 2:3]), [ex])
            return ps, pr, sslot, s_, ex, rc

        def mla_turn(it):
            ps, pr, sslot, s_, ex, rc = it
            b = take2()
            for k in range(6):
                bb = b + k // 4
                m = pe.op(lambda e, k=k, bb=bb: e.transpose(bank(bb, P, (k % 4) * P), pr[:, k * P:(k + 1) * P], ident[:, :]),
                          [ex] + bank_free[bb], mark=True)
            ps.free = [m]
            pt = pT_ring.take()
            c1 = actv(pt.tiles[0][:, 0:384], psum[:, b * BANK:b * BANK + 384], ACT.Copy, [m] + pt.free)
            c2 = dve.op(lambda e: e.tensor_copy(pt.tiles[0][:, 384:LA], psum[:, b * BANK + 384:b * BANK + LA]), [m, c1] + pt.free)
            bank_free[b] = bank_free[b + 1] = [c1, c2]
            return pt, [c1, c2], sslot, s_, rc

        def mla_values(it, hd, t_):
            pt, ready, sslot, s_, rc = it
            b = take1()
            for k in range(6):
                m = mm(bank(b, 64), pt.tiles[0][:, k * P:(k + 1) * P], v_all[:, k, hd * 64:(hd + 1) * 64], k == 0, k == 5,
                       ready + v_marks + bank_free[b], mark=True)
            pt.free = [m]
            d = ts(o_tok[:, t_, hd * 64:(hd + 1) * 64], bank(b, 64), s_[:, 3:4], None, ALU.mult, None, [m, rc])
            bank_free[b] = [d]
            sslot.free = [d]
            o_marks.append(d)

        seq = [(hd, t_) for hd in range(HEADS) for t_ in range(NT)]
        a1, a2 = {}, {}
        for n in range(len(seq) + 2):
            if n < len(seq):
                a1[n] = mla_scores(*seq[n])
            if 0 <= n - 1 < len(seq):
                a2[n - 1] = mla_turn(a1.pop(n - 1))
            if 0 <= n - 2 < len(seq):
                mla_values(a2.pop(n - 2), *seq[n - 2])
        for t_ in range(NT):
            b = take1()
            for k in range(4):
                m = pe.op(lambda e, k=k, b=b, t_=t_: e.transpose(bank(b, P, k * P), o_tok[:, t_, k * P:(k + 1) * P], ident[:, :]),
                          o_marks + bank_free[b], mark=True)
            slot, w = work()
            wv = w.rearrange("p (k n) -> p k n", k=4)
            d = tt(dve, wv, bank(b).rearrange("p (k n) -> p k n", k=4), silu_dg[:, :, t_ * P:(t_ + 1) * P], ALU.mult, [m] + dg_marks + slot.free)
            bank_free[b] = [d]
            slot.free = split_pair(h_hi[:, 4:8, t_ * P:(t_ + 1) * P], h_lo[:, 4:8, t_ * P:(t_ + 1) * P], wv, [d] + h_read)
            mix_marks += slot.free
        fence()
        mla.close()
        cd.close()
        tail = ExitStack()
        g_row = sb(tail, "g_row", [P, D])
        b_row = sb(tail, "b_row", [P, D])
        free = pe.now() + dve.now() + act.now()
        rows_ready = [load(g_row[:, :], A["cd_ln_g"][0].partition_broadcast(P), free, s=row_sems[0]),
                      load(b_row[:, :], A["cd_ln_b"][0].partition_broadcast(P), s=row_sems[1])]
        x_marks = []
        down(KT, h_hi, h_lo, [t_ * P for t_ in range(NT)], mix_marks, x_sink)
        fence()
        tail.close()
        first.close()

        second = ExitStack()
        h_hi = sb(second, "n_hi", [P, KT, L], F32R)
        h_lo = sb(second, "n_lo", [P, KT, L], F32R)
        row_buf = sb(second, "wide", [P, D])
        post_g = sb(second, "post_g", [P, D])
        post_free = fence()
        wide = Slot(row_buf)

        def rms_turn(g_name, layer, x_ready):
            marks = []
            for t_ in range(NT):
                slot, s_ = stat()
                sq = actv(row_buf[:, :], X[:, t_, :], ACT.Square, [x_ready[t_]] + wide.free + slot.free, accum_out=s_[:, 0:1])
                r = rsqrt(s_[:, 1:2], s_[:, 0:1], 1, 1.0 / D, [sq])
                d = actv(row_buf[:, :], X[:, t_, :], ACT.Copy, [r, sq], scale=s_[:, 1:2])
                slot.free = [d]
                marks += turn(row_buf[:, :], None, h_hi, h_lo, t_ * P, col(g_name, 8 * layer, 8), None, [d])
                wide.free = pe.now()
            return marks

        def residual_rms(weight, g_ready, x_ready):
            def sink(i, y, m):
                slot, s_ = stat()
                sq = actv(row_buf[:, :], y, ACT.Square, [m] + wide.free + slot.free, accum_out=s_[:, 0:1])
                r = rsqrt(s_[:, 1:2], s_[:, 0:1], 1, 1.0 / D, [sq])
                if weight != 1.0:
                    r = ts(s_[:, 1:2], s_[:, 1:2], weight, None, ALU.mult, None, [r])
                d = stt(row_buf[:, :], y, s_[:, 1:2], post_g[:, :], ALU.mult, ALU.mult, [r, sq, g_ready])
                slot.free = [d]
                x_ready[i] = tt(dve, X[:, i, :], X[:, i, :], row_buf[:, :], ALU.add, [d])
                wide.free = [x_ready[i]]
                return [sq, d]
            return sink

        post_sem = [sem("post_g_landed"), 0]
        x_ready = x_marks

        def ffn(f, layer, x_ready, post_free):
            g_ready = load(post_g[:, :], A[f"ffn{f}_post_g_2"][layer].partition_broadcast(P), post_free, s=post_sem)
            ready = rms_turn(f"ffn{f}_pre_g_2", layer, x_ready)
            scope = ExitStack()
            act_hi = sb(scope, "ff_hi", [P, FT, L], F32R)
            act_lo = sb(scope, "ff_lo", [P, FT, L], F32R)
            marks = []
            for ch in range(FF // CW):
                gates = []

                def gate_sink(r, ps, m):
                    slot, w = work()
                    d = actv(w, ps, ACT.Silu, [m] + slot.free)
                    gates.append((slot, w, d))
                    return [d]
                c = next_chunk()
                for j in range(2):
                    project(c, j * P, P, h_hi, h_lo, RANGES[:1], ready, gate_sink)
                c = next_chunk()
                for j in range(2):
                    def up_sink(r, ps, m, j=j, ch=ch):
                        slot, w, s_ = gates[j]
                        d = tt(dve, w, w, ps, ALU.mult, [m, s_])
                        k = 2 * ch + j
                        slot.free = split_pair(act_hi[:, k, :], act_lo[:, k, :], w, [d])
                        marks.extend(slot.free)
                        return [d]
                    project(c, j * P, P, h_hi, h_lo, RANGES[:1], ready, up_sink)
            new = [None] * NT
            down(FT, act_hi, act_lo, [t_ * P for t_ in range(NT)], marks, residual_rms(0.5, g_ready, new))
            free = fence()
            scope.close()
            return new, free

        def mixing(layer, x_ready, post_free):
            lam_init = 0.8 - 0.6 * math.exp(-0.3 * layer)
            g_ready = load(post_g[:, :], A["mix_post_g_2"][layer].partition_broadcast(P), post_free, s=post_sem)
            ready = rms_turn("mix_pre_g_2", layer, x_ready)
            sc = ExitStack()
            q_a, k_a, q_c, k_c = (sb(sc, n, [P, 3, L]) for n in ("q_a", "k_a", "q_c", "k_c"))
            q_b, k_b = (sb(sc, n, [P, 2, L]) for n in ("q_b", "k_b"))
            v_a, v_c = (sb(sc, n, [P, NT, 384]) for n in ("v_a", "v_c"))
            v_b = sb(sc, "v_b", [P, NT, 256])
            far = sb(sc, "far_bias", [P, 6])
            dist = sb(sc, "distance", [P, L])
            strict = sb(sc, "strict", [P, 2, P])
            tri = sb(sc, "suffix_tri", [P, P])
            lam = sb(sc, "lambda", [P, 4, 32])
            lam_s = sb(sc, "lambda_stats", [P, 8])
            sub_g = sb(sc, "subln_g", [P, 64])
            soft_scope, stick_scope = ExitStack(), ExitStack()
            bias = sb(soft_scope, "band_bias", [P, 6, L])
            o_tok = sb(soft_scope, "o_tok", [P, NT, 640])
            score_ring = Ring([Slot(sb(soft_scope, "scores", [P, L])) for _ in range(4)])
            turned_ring = Ring([Slot(sb(soft_scope, "scoresT", [P, L])) for _ in range(2)])
            clear = post_free
            consts = [sem(f"mix_consts_{layer}"), 0]
            for dst, src in ((bias[:, :, 256:512], A["l_band_bias"][layer].rearrange("h q k -> q h k")),
                             (far[:, :], A["l_far_bias"][layer].partition_broadcast(P)),
                             (dist[:, :], A["k_distance"]), (strict[:, :, :], A["k_strict"].rearrange("s p n -> p s n")),
                             (tri[:, :], A["k_tri"]), (sub_g[:, :], A["diff_subln_g_2"][layer].partition_broadcast(P)),
                             (lam[:, 0, :], A["diff_lambda_q1_2"][layer].partition_broadcast(P)),
                             (lam[:, 1, :], A["diff_lambda_k1_2"][layer].partition_broadcast(P)),
                             (lam[:, 2, :], A["diff_lambda_q2_2"][layer].partition_broadcast(P)),
                             (lam[:, 3, :], A["diff_lambda_k2_2"][layer].partition_broadcast(P))):
                in_ = load(dst, src, clear, s=consts)
            for h in range(6):
                bm = actv(bias[:, h, 0:256], bias[:, h, 256:512], ACT.Identity, [in_], scale=0.0, bias=far[:, h:h + 1])
            masked = pool.op(lambda e: e.memset(bias[0:64, :, 448:512], NEG), [in_, bm])
            for i in range(2):
                d = tt(dve, lam[:, 2 * i, :], lam[:, 2 * i, :], lam[:, 2 * i + 1, :], ALU.mult, [in_])
                d = dve.op(lambda e, i=i: e.tensor_reduce(lam_s[:, i:i + 1], lam[:, 2 * i, :], AX.X, ALU.add), [d])
            ex = actv(lam_s[:, 2:4], lam_s[:, 0:2], ACT.Exp, [d])
            d = tt(dve, lam_s[:, 4:5], lam_s[:, 2:3], lam_s[:, 3:4], ALU.subtract, [ex])
            lam_ready = ts(lam_s[:, 5:6], lam_s[:, 4:5], -1.0, -lam_init, ALU.mult, ALU.add, [d])
            g_scaled = ts(sub_g[:, :], sub_g[:, :], 1.0 - lam_init, None, ALU.mult, None, [in_])

            marks = {n: [] for n in "abc"}

            def put(dst, name, scale):
                def sink(r, ps, m):
                    d = actv(dst, ps, ACT.Copy, [m], scale=scale)
                    marks[name].append(d)
                    return [d]
                return sink

            feature = {}
            for i in range(3):
                feature[i * P] = (q_a[:, i, :], "a", 0.125)
                feature[384 + i * P] = (k_a[:, i, :], "a", 1.0)
                feature[1920 + i * P] = (q_c[:, i, :], "c", 0.125)
                feature[2304 + i * P] = (k_c[:, i, :], "c", 1.0)
            for i in range(2):
                feature[1152 + i * P] = (q_b[:, i, :], "b", 1.0)
                feature[1408 + i * P] = (k_b[:, i, :], "b", 1.0)
            values = ((768, 1152, v_a, "a"), (1664, 1920, v_b, "b"), (2688, 3072, v_c, "c"))
            for c0, n in MIX_CHUNKS:
                c = next_chunk()
                v = [x for x in values if x[0] <= c0 < x[1]]
                if v:
                    lo_, _, dst, name = v[0]

                    def v_sink(t_, ps, m):
                        d = actv(dst[:, t_, c0 - lo_:c0 - lo_ + n], ps, ACT.Copy, [m])
                        marks[name].append(d)
                        return [d]
                    project_tokens(c, h_hi, h_lo, range(NT), ready, v_sink)
                else:
                    for j in range(n // P):
                        project(c, j * P, P, h_hi, h_lo, RANGES[:1], ready, put(*feature[c0 + j * P]))
            h_read = pe.now()
            mix_marks, o_marks = [], []

            def softmax(s_ap, width, bias_mult, sslot, s_, o, psb, after):
                pass

            def turn_probs(slot, width, t_, ready):
                b = take1()
                for k in range(t_ + 1):
                    m = pe.op(lambda e, k=k: e.transpose(bank(b, P, k * P), slot.tiles[0][:, k * P:(k + 1) * P], ident[:, :]),
                              list(ready) + bank_free[b], mark=True)
                slot.free = [m]
                pt = turned_ring.take()
                d = actv(pt.tiles[0][:, 0:width], bank(b, width), ACT.Copy, [m] + pt.free)
                bank_free[b] = [d]
                return pt, d

            def apply_values(pt, d, v, c0, t_, name):
                b = take1()
                for k in range(t_ + 1):
                    m = mm(bank(b, 64), pt.tiles[0][:, k * P:(k + 1) * P], v[:, k, c0:c0 + 64], k == 0, k == t_,
                           [d] + marks[name] + bank_free[b], mark=True)
                pt.free = [m]
                return b, m

            def a_scores(h, t_):
                width, p0 = (t_ + 1) * P, 64 * (h % 2)
                b = take1()
                m = mm(bank(b, width), q_a[p0:p0 + 64, h // 2, t_ * P:(t_ + 1) * P], k_a[p0:p0 + 64, h // 2, 0:width], True, True,
                       marks["a"] + bank_free[b], mark=True)
                slot, (sslot, s_) = score_ring.take(), stat()
                w = slot.tiles[0][:, 0:width]
                d = tt(dve, w, bank(b, width), bias[:, h, L - width:L], ALU.add, [m, masked, bm] + slot.free)
                bank_free[b] = [d]
                mx = dve.op(lambda e: e.tensor_reduce(s_[:, 0:1], w, AX.X, ALU.max, negate=True), [d] + sslot.free)
                ex = actv(w, w, ACT.Exp, [mx], bias=s_[:, 0:1], accum_out=s_[:, 1:2])
                rc = dve.op(lambda e: e.reciprocal(s_[:, 2:3], s_[:, 1:2]), [ex])
                return slot, width, [ex], sslot, s_, rc

            def b_scores(h, t_):
                width = (t_ + 1) * P
                sslot, s_ = stat()
                slope = 2.0 ** (-8.0 * (h + 1) / 4)
                sc_ = 32 ** -0.5
                got = []
                for mp in range(2):
                    blk = 2 * h + mp
                    p0 = 32 * (blk % 4)
                    b = take1()
                    m = mm(bank(b, width), q_b[p0:p0 + 32, blk // 4, t_ * P:(t_ + 1) * P], k_b[p0:p0 + 32, blk // 4, 0:width], True, True,
                           marks["b"] + bank_free[b], mark=True)
                    slot = score_ring.take()
                    w = slot.tiles[0][:, 0:width]
                    o = 4 * mp
                    d = stt(w, dist[:, L - width:L], slope / sc_, bank(b, width), ALU.mult, ALU.add, [m, in_] + slot.free)
                    bank_free[b] = [d]
                    mx = dve.op(lambda e, o=o, w=w: e.tensor_reduce(s_[:, o:o + 1], w, AX.X, ALU.max), [d] + sslot.free)
                    mx = ts(s_[:, o + 1:o + 2], s_[:, o:o + 1], -sc_, None, ALU.mult, None, [mx])
                    ex = actv(w, w, ACT.Exp, [mx], bias=s_[:, o + 1:o + 2], scale=sc_, accum_out=s_[:, o + 2:o + 3])
                    rc = dve.op(lambda e, o=o: e.reciprocal(s_[:, o + 3:o + 4], s_[:, o + 2:o + 3]), [ex])
                    got.append((slot, w, rc, ex))
                d = tt(dve, s_[:, 8:9], s_[:, 7:8], lam_s[:, 5:6], ALU.mult, [got[1][2], lam_ready])
                d = ts(got[1][1], got[1][1], s_[:, 8:9], None, ALU.mult, None, [d, got[1][3]])
                d = stt(got[0][1], got[0][1], s_[:, 3:4], got[1][1], ALU.mult, ALU.add, [d, got[0][2], got[0][3]])
                got[1][0].free = [d]
                sslot.free = [d]
                return got[0][0], width, [d], sslot, s_, None

            def finish(it2, kind, h, t_):
                pt, d, sslot, s_, rc = it2
                v, c0 = (v_a, h * 64) if kind == "a" else (v_b, h * 64)
                b, m = apply_values(pt, d, v, c0, t_, kind)
                if kind == "a":
                    o = ts(o_tok[:, t_, c0:c0 + 64], bank(b, 64), s_[:, 2:3], None, ALU.mult, None, [m, rc])
                    sslot.free = [o]
                else:
                    o = actv(o_tok[:, t_, 384 + c0:384 + c0 + 64], bank(b, 64), ACT.Copy, [m])
                bank_free[b] = [o]
                o_marks.append(o)

            seq = [("a", h, t_) for t_ in range(NT) for h in range(6)] + [("b", h, t_) for t_ in range(NT) for h in range(4)]
            s1, s2 = {}, {}
            for n in range(len(seq) + 2):
                if n < len(seq):
                    kind, h, t_ = seq[n]
                    s1[n] = (a_scores if kind == "a" else b_scores)(h, t_)
                if 0 <= n - 1 < len(seq):
                    slot, width, rdy, sslot, s_, rc = s1.pop(n - 1)
                    pt, d = turn_probs(slot, width, seq[n - 1][2], rdy)
                    s2[n - 1] = (pt, d, sslot, s_, rc)
                if 0 <= n - 2 < len(seq):
                    finish(s2.pop(n - 2), *seq[n - 2])

            for t_ in range(NT):
                slot, w = work(256)
                sslot, s_ = stat()
                ob = o_tok[:, t_, 384:640]
                d = tt(dve, w, ob, ob, ALU.mult, o_marks + slot.free + sslot.free)
                d = dve.op(lambda e, s_=s_, w=w: e.tensor_reduce(s_[:, 0:4], w.rearrange("p (h c) -> p h c", h=4), AX.X, ALU.add), [d])
                slot.free = [d]
                r = rsqrt(s_[:, 4:8], s_[:, 0:4], 4, 1.0 / 64, [d])
                ov = ob.rearrange("p (h c) -> p h c", h=4)
                d = tt(dve, ov, ov, s_[:, 4:8].unsqueeze(2).broadcast_to([P, 4, 64]), ALU.mult, [r])
                sslot.free = [d]
                d = tt(dve, ov, ov, sub_g[:, :].unsqueeze(1).broadcast_to([P, 4, 64]), ALU.mult, [d, g_scaled])
                b = take2()
                for k in range(5):
                    bb = b + k // 4
                    m = pe.op(lambda e, k=k, bb=bb, t_=t_: e.transpose(bank(bb, P, (k % 4) * P), o_tok[:, t_, k * P:(k + 1) * P], ident[:, :]),
                              [d] + o_marks + bank_free[bb], mark=True)
                pv = psum[:, b * BANK:b * BANK + 640].rearrange("p (k n) -> p k n", k=5)
                sp_ = split_pair(h_hi[:, 0:5, t_ * P:(t_ + 1) * P], h_lo[:, 0:5, t_ * P:(t_ + 1) * P], pv, [m] + h_read)
                bank_free[b] = bank_free[b + 1] = sp_
                mix_marks += sp_

            fence()
            soft_scope.close()
            soft = sb(stick_scope, "softplus", [P, 1280])
            wts = sb(stick_scope, "stick_weights", [P, 1280])
            starts = {0: 0, 1: 512, 2: 896, 3: 1152}
            soft_free, wts_free = [], []
            for h in range(6):
                p0 = 64 * (h % 2)
                z_done, w_marks = {}, []
                zb = {}
                for kt in range(NT):
                    width = L - kt * P
                    zb[kt] = kt
                    z_done[kt] = mm(bank(kt, width), k_c[p0:p0 + 64, h // 2, kt * P:(kt + 1) * P], q_c[p0:p0 + 64, h // 2, kt * P:L],
                                    True, True, marks["c"] + bank_free[kt], mark=True)
                sp_marks = {}
                for kt in range(NT):
                    width, o = L - kt * P, starts[kt]
                    a_ = actv(soft[:, o:o + width], bank(kt, width), ACT.Abs, [z_done[kt]] + soft_free)
                    a_ = actv(soft[:, o:o + width], soft[:, o:o + width], ACT.Exp, [a_], scale=-1.0)
                    a_ = actv(soft[:, o:o + width], soft[:, o:o + width], ACT.Ln, [a_], bias=1.0)
                    d = stt(soft[:, o:o + width], bank(kt, width), 0.0, soft[:, o:o + width], ALU.max, ALU.add, [a_])
                    sp_marks[kt] = tt(dve, soft[:, o:o + P], soft[:, o:o + P], strict[:, 0, :], ALU.mult, [d, in_])
                for kt in range(NT):
                    width, o = L - kt * P, starts[kt]
                    b = 4 + kt % 2
                    m = mm(bank(b, width), tri[:, :], soft[:, o:o + width], True, kt == 3, [sp_marks[kt]] + bank_free[b], mark=True)
                    for k2 in range(kt + 1, NT):
                        w2, o2 = L - k2 * P, starts[k2]
                        m = mm(bank(b, w2, (k2 - kt) * P), ones[:, :], soft[:, o2:o2 + w2], False, k2 == 3, [sp_marks[k2]], mark=True)
                    soft_free = [m]
                    ws, w = work(width)
                    cz = actv(w, bank(kt, width), ACT.Copy, [z_done[kt], sp_marks[kt]] + ws.free)
                    bank_free[kt] = [cz, sp_marks[kt]]
                    d = tt(dve, w, w, bank(b, width), ALU.subtract, [m, cz])
                    bank_free[b] = [d]
                    d = tt(dve, w[:, 0:P], w[:, 0:P], strict[:, 1, :], ALU.add, [d])
                    e_ = actv(wts[:, o:o + width], w, ACT.Exp, [d] + wts_free)
                    ws.free = [e_]
                    w_marks.append(e_)
                b = 6 + h % 2
                for kt in range(NT):
                    width, o = L - kt * P, starts[kt]
                    m = mm(psum[p0:p0 + 64, b * BANK + kt * P:(b + 1) * BANK], v_c[:, kt, h * 64:(h + 1) * 64], wts[:, o:o + width],
                           kt == 0, kt == 3, w_marks + bank_free[b], mark=True)
                wts_free = [m]
                po = psum[p0:p0 + 64, b * BANK:(b + 1) * BANK]
                k = 5 + h // 2
                sp_ = split_pair(h_hi[p0:p0 + 64, k, :], h_lo[p0:p0 + 64, k, :], po, [m] + h_read)
                bank_free[b] = sp_
                mix_marks += sp_
            new = [None] * NT
            down(KT, h_hi, h_lo, [t_ * P for t_ in range(NT)], mix_marks, residual_rms(1.0, g_ready, new))
            free = fence()
            stick_scope.close()
            sc.close()
            return new, free

        for layer in range(DEPTH):
            x_ready, post_free = ffn(1, layer, x_ready, post_free)
            x_ready, post_free = mixing(layer, x_ready, post_free)
            x_ready, post_free = ffn(2, layer, x_ready, post_free)
        stored = [sem("stored"), 0]
        for t_ in range(NT):
            last = load(out[0, t_ * P:(t_ + 1) * P, :], X[:, t_, :], [x_ready[t_]], s=stored)
        sp.wait([last])
        second.close()

        block = ctx.enter_context(nc.Block())

        def play(engine, eng):
            for step in engine.queue:
                step(eng)

        block.sync(lambda e: play(sp, e))
        block.tensor(lambda e: play(pe, e))
        block.scalar(lambda e: play(act, e))
        block.vector(lambda e: play(dve, e))
        block.gpsimd(lambda e: play(pool, e))


def shape_constants():
    k = {}
    k["k_ident"] = np.eye(P)
    d = 2 * np.pi * (np.outer(np.arange(P), np.arange(P)) % P) / P
    k["k_dft_d"] = np.concatenate([np.cos(d), np.sin(d)], 1)
    a = 2 * np.pi * (np.outer(np.arange(L), np.arange(L)) % L) / L
    k["k_dft_l"] = np.stack([np.cos(a), -np.sin(a)], 1) / np.sqrt(L * P)
    tok = np.arange(L)
    inv = 10000.0 ** (-np.arange(0, 16, 2) / 16)
    ang = [np.outer(inv, tok // 64), np.outer(inv, tok % 64)]
    cos, sin = np.ones((QK, L)), np.zeros((QK, L))
    swap = np.zeros((QK, QK))
    for i in range(2):
        r = NOPE + 16 * i
        cos[r:r + 8] = cos[r + 8:r + 16] = np.cos(ang[i])
        sin[r:r + 8], sin[r + 8:r + 16] = -np.sin(ang[i]), np.sin(ang[i])
        for j in range(8):
            swap[r + 8 + j, r + j] = swap[r + j, r + 8 + j] = 1
    k["k_rope_cos"], k["k_rope_sin"], k["k_rope_swap"] = cos, sin, swap
    rows = []
    for w in POOL_WINDOWS:
        row = []
        for n in (L, LC):
            t = np.arange(n)
            row.append(1.0 / (np.clip(t + w - w // 2, 0, n) - np.clip(t - w // 2, 0, n)))
        rows.append(np.concatenate(row))
    k["k_inv_count"] = np.stack(rows)
    q, c = np.arange(P)[:, None], np.arange(L)[None]
    dist = -np.abs(q + L - P - c).astype(np.float64)
    dist[0:64, L - 64:] = NEG
    k["k_distance"] = dist
    s, t = np.arange(P)[:, None], np.arange(P)[None]
    k["k_strict"] = np.stack([(s < t) * 1.0, np.where(s < t, 0.0, NEG)])
    k["k_tri"] = (s >= t) * 1.0
    return {n: np.ascontiguousarray(v, dtype=np.float32) for n, v in k.items()}


def kernel(**inputs):
    import concourse.bacc as bacc
    from concourse.bass_utils import run_bass_kernel_spmd as run

    nc = bacc.Bacc("TRN2", target_bir_lowering=False, num_devices=1)
    arrays = {n: np.ascontiguousarray(v) for n, v in inputs.items()}
    arrays.update(shape_constants())
    rb = arrays["rel_bias_2"]
    flipped = np.concatenate([np.repeat(rb[:, :, 256:257], P - 1, axis=2), rb[:, :, :0:-1]], axis=2)
    idx = np.arange(256)[None] - np.arange(P)[:, None] + P - 1
    arrays["l_band_bias"] = np.ascontiguousarray(flipped[:, :, idx])
    arrays["l_far_bias"] = np.ascontiguousarray(rb[:, :, 256])
    A = {n: nc.dram_tensor(f"in_{n}", a.shape, mybir.dt.from_np(a.dtype), kind="ExternalInput").ap()
         for n, a in arrays.items()}
    out = nc.dram_tensor("out_x", (1, L, D), F32, kind="ExternalOutput").ap()
    build(nc, A, out)
    r = run(nc, [{f"in_{n}": a for n, a in arrays.items()}], core_ids=[0])
    return r.results[0]["out_x"]
```

```python
from contextlib import ExitStack
import math

import numpy as np

import concourse.bass as bass
from concourse import mybir

F32 = mybir.dt.float32
F32R = mybir.dt.float32r
ACT = mybir.ActivationFunctionType
ALU = mybir.AluOpType
AX = mybir.AxisListType

P = 128
D = 1024
KT = D // P
L = 512
LC = 256
LA = L + LC
NT = L // P
NC = LC // P
BANK = 512
EPS = 1e-6
DEPTH = 2
ALPHA = (2 * DEPTH) ** 0.25
POOL_WINDOWS = (2, 4, 8, 16)
HALO = 8
FF = 2816
FT = FF // P
NOPE, ROPE, HEADS = 64, 32, 8
QK = NOPE + ROPE
NEG = -1e30
CW = 256

VECS = [("ab_b_mod", 24), ("cd_b_mod", 24), ("c", 8), ("c_ctx", 8), ("ab_pool_scale", 4),
        ("cd_q_norm", 2), ("cd_kv_norm", 1), ("ffn1_pre_g_2", 16), ("mix_pre_g_2", 16),
        ("ffn2_pre_g_2", 16)]
VOFF = {}
for _n, _k in VECS:
    VOFF[_n] = sum(k for m, k in VECS[:[n for n, _ in VECS].index(_n)])
NVEC = sum(k for _, k in VECS)


class Engine:

    def __init__(self, sem):
        self.sem, self.count, self.queue, self.seen = sem, 0, [], {}

    def wait(self, marks):
        for sem, value in marks:
            if value > self.seen.get(id(sem), 0):
                self.seen[id(sem)] = value
                self.queue.append(lambda eng, s=sem, v=value: eng.wait_ge(s, v))

    def op(self, build, after=(), mark=True):
        self.wait(after)
        if not mark:
            self.queue.append(build)
            return None
        self.count += 1
        self.queue.append(lambda eng, b=build, s=self.sem: b(eng).then_inc(s, 1))
        return (self.sem, self.count)

    def now(self):
        return [(self.sem, self.count)] if self.count else []


class Slot:

    def __init__(self, *tiles):
        self.tiles, self.free = tiles, []


class Ring:
    def __init__(self, slots):
        self.slots, self.at = slots, 0

    def take(self):
        self.at += 1
        return self.slots[(self.at - 1) % len(self.slots)]


def build(nc, A, out):
    ctx = ExitStack()
    names = [0]

    def sem(name):
        return ctx.enter_context(nc.semaphore(name))

    def sb(scope, name, shape, dt=F32):
        names[0] += 1
        return scope.enter_context(nc.sbuf_tensor(f"{name}_{names[0]}", shape, dt))

    with ctx:
        pe, act, dve, pool = (Engine(sem(n)) for n in ("pe_done", "act_done", "dve_done", "pool_done"))
        sp = Engine(None)
        dma_sems = []

        def load(dst, src, after=(), s=None):
            if s is None:
                s = [sem(f"landed_{len(dma_sems)}"), 0]
                dma_sems.append(s)
            s[1] += 16
            sp.wait(after)
            sp.queue.append(lambda eng, s0=s[0]: eng.dma_start(dst, src).then_inc(s0, 16))
            return (s[0], s[1])

        psum = ctx.enter_context(nc.psum_tensor("psum", [P, 8 * BANK], F32))
        bank_free = {b: [] for b in range(8)}

        def bank(b, n=BANK, off=0):
            return psum[:, b * BANK + off:b * BANK + off + n]

        raw_ring = Ring([Slot(sb(ctx, "raw", [P, 2048]), [sem(f"raw_landed_{i}"), 0]) for i in range(2)])
        split_ring = Ring([Slot(sb(ctx, "w_hi", [P, 2048], F32R), sb(ctx, "w_lo", [P, 2048], F32R))
                           for _ in range(2)])
        X = sb(ctx, "X", [P, NT, D])
        main_hi = sb(ctx, "h_hi", [P, KT, L], F32R)
        main_lo = sb(ctx, "h_lo", [P, KT, L], F32R)
        cols = sb(ctx, "cols", [P, NVEC])
        ident = sb(ctx, "ident", [P, P])
        ones = sb(ctx, "ones", [P, P])
        half = sb(ctx, "minus_half", [P, 8])
        work_ring = Ring([Slot(sb(ctx, "work", [P, BANK])) for _ in range(3)])
        stat_ring = Ring([Slot(sb(ctx, "stat", [P, 32])) for _ in range(8)])

        def fence():
            marks = pe.now() + act.now() + dve.now() + pool.now()
            for e in (pe, act, dve, pool, sp):
                e.wait([m for m in marks if m[0] is not e.sem])
            for e in (act, dve, pool):
                e.wait(e.now())
            return marks

        plan = []

        def kview(t, nk):
            return t[:, :].rearrange("p (k n) -> p k n", k=nk)

        def add_cols(w, c0, n, split=True):
            plan.append((w[:, c0:c0 + n].rearrange("(k p) n -> p k n", p=P), KT, n, split))

        def add_rows(w, r0):
            plan.append((w[r0:r0 + 2 * P, :].rearrange("(k p) n -> p k n", p=P), 2, D, True))

        def add_down(w, rows):
            for r in range(0, rows, 2 * P):
                add_rows(w, r)

        for c0 in range(0, 2560, CW):
            add_cols(A["ab_w_in"][0], c0, CW)
        add_down(A["ab_w_out"][0], D)
        add_down(A["ab_w_out"][0], D)
        for c0, n in ((0, 256), (256, 256), (512, 256), (768, 256), (1024, 256), (1280, 160), (1440, 256), (1696, 256)):
            add_cols(A["cd_w_in"][0], c0, n)
        for c0 in (0, 256):
            plan.append((A["cd_fnet_w"][0][:, c0:c0 + 256].rearrange("(k p) n -> p k n", p=P), 4, 256, True))
        add_down(A["cd_w_out"][0], D)
        MIX_CHUNKS = [(1920, 256), (2176, 256), (2432, 256), (2688, 256), (2944, 128), (0, 256), (256, 256), (512, 256),
                      (768, 256), (1024, 128), (1152, 256), (1408, 256), (1664, 256)]
        for layer in range(DEPTH):
            for f in (1, 2):
                if f == 2:
                    for c0, n in MIX_CHUNKS:
                        add_cols(A["w_in_2"][layer], c0, n)
                    add_down(A["w_out_2"][layer], D)
                for c0 in range(0, FF, CW):
                    add_cols(A[f"ffn{f}_w_gate_2"][layer], c0, CW)
                    add_cols(A[f"ffn{f}_w_up_2"][layer], c0, CW)
                add_down(A[f"ffn{f}_w_down_2"][layer], FF)

        class Chunk:
            pass

        raws = []
        consumed = [False] * len(plan)
        at = {"prepared": 0}
        ready_chunks, in_use = [], []

        def top_up():
            while len(raws) < len(plan) and (len(raws) < 2 or consumed[len(raws) - 2]):
                src, nk, n, _ = plan[len(raws)]
                slot = raw_ring.take()
                dst = slot.tiles[0][:, 0:nk * n].rearrange("p (k n) -> p k n", k=nk)
                raws.append((slot, load(dst, src, slot.free, slot.tiles[1])))

        def prepare_chunk():
            i = at["prepared"]
            if i >= len(plan):
                return
            at["prepared"] += 1
            _, nk, n, split = plan[i]
            raw_slot, landed = raws[i]
            raw = raw_slot.tiles[0]
            c = Chunk()
            c.index, c.nk, c.n, c.split = i, nk, n, split
            w = nk * n
            if split:
                slot = split_ring.take()
                hi, lo = slot.tiles
                made_hi = act.op(lambda e: e.activation(hi[:, 0:w], raw[:, 0:w], ACT.Copy),
                                 [landed] + slot.free)
                made_lo = dve.op(lambda e: e.tensor_tensor(lo[:, 0:w], raw[:, 0:w], hi[:, 0:w].bitcast(F32),
                                                           ALU.subtract), [landed, made_hi] + slot.free)
                raw_slot.free = [made_lo]
                consumed[i] = True
                c.slot, c.ready = slot, [made_lo, made_hi]
                c.hi = hi[:, 0:w].rearrange("p (k n) -> p k n", k=nk)
                c.lo = lo[:, 0:w].rearrange("p (k n) -> p k n", k=nk)
            else:
                c.slot, c.ready = raw_slot, [landed]
                c.raw = raw[:, 0:w].rearrange("p (k n) -> p k n", k=nk)
            top_up()
            ready_chunks.append(c)

        def release(count=None):
            for c in in_use[:count]:
                c.slot.free = pe.now() if c.split else pe.now() + dve.now()
                consumed[c.index] = True
            del in_use[:count]
            top_up()

        def next_chunk(beside=False):
            if not beside:
                release()
            if not ready_chunks:
                prepare_chunk()
            c = ready_chunks.pop(0)
            in_use.append(c)
            if not beside and not ready_chunks:
                prepare_chunk()
            return c

        rot = Ring(list(range(8)))

        def take1():
            return rot.take()

        def take2():
            if rot.at % 2:
                rot.take()
            b = rot.take()
            rot.take()
            return b

        def tokens(h, k, off, n):
            return h[0][:, k, off:off + n] if off < L else h[1][:, k, off - L:off - L + n]

        def mm(o, lhsT, rhs, start, stop, after=(), mark=False):
            return pe.op(lambda e: e.matmul(o, lhsT, rhs, start=start, stop=stop, skip_group_check=True), after, mark)

        def mm3(o, st_hi, st_lo, mv_hi, mv_lo, start, stop, after=(), mark=False):
            mm(o, st_hi, mv_hi, start, False, after)
            mm(o, st_hi, mv_lo, False, False)
            return mm(o, st_lo, mv_hi, False, stop, (), mark)

        def tt(eng, o, a, b, op, after=()):
            return eng.op(lambda e: e.tensor_tensor(o, a, b, op), after)

        def ts(o, a, s1, s2, op0, op1, after=()):
            if op1 is None:
                return dve.op(lambda e: e.tensor_scalar(o, a, s1, None, op0), after)
            return dve.op(lambda e: e.tensor_scalar(o, a, s1, s2, op0, op1), after)

        def stt(o, a, s, b, op0, op1, after=()):
            return dve.op(lambda e: e.scalar_tensor_tensor(out=o, in0=a, scalar=s, in1=b, op0=op0, op1=op1), after)

        def actv(o, a, func, after=(), **kw):
            return act.op(lambda e: e.activation(o, a, func, **kw), after)

        def split_pair(hi, lo, src, after):
            made_hi = actv(hi, src, ACT.Copy, after)
            made_lo = tt(dve, lo, src, hi.bitcast(F32), ALU.subtract, [made_hi] + list(after))
            return [made_hi, made_lo]

        def work(n=BANK):
            slot = work_ring.take()
            return slot, slot.tiles[0][:, 0:n]

        def stat():
            slot = stat_ring.take()
            return slot, slot.tiles[0]

        def rsqrt(o, a, n, scale, after, weight=1.0):
            biased = ts(a, a, scale / weight ** 2, EPS / weight ** 2, ALU.mult, ALU.add, after)
            return tt(pool, o, a, half[:, 0:n], ALU.pow, [biased, made_half])

        vec_scope = ExitStack()
        vec_rows = sb(vec_scope, "vec_rows", [NVEC, P])
        vec_landed = [sem("vectors_landed"), 0]
        for name, k in VECS:
            src = A[name]
            while len(src.shape) > 1:
                src = src.rearrange("a b -> (a b)") if len(src.shape) == 2 else src.rearrange("a b c -> (a b c)")
            vecs_in = load(vec_rows[VOFF[name]:VOFF[name] + k, :], src.rearrange("(k p) -> k p", p=P), s=vec_landed)
        ident_in = load(ident[:, :], A["k_ident"])
        made_ones = pool.op(lambda e: e.memset(ones[:, :], 1.0))
        made_half = pool.op(lambda e: e.memset(half[:, :], -0.5))
        t = pe.op(lambda e: e.transpose(bank(0, NVEC), vec_rows[:, :], ident[0:NVEC, 0:NVEC]),
                  [vecs_in, ident_in])
        cols_in = dve.op(lambda e: e.tensor_copy(cols[:, :], bank(0, NVEC)), [t])
        bank_free[0] = [cols_in]
        vec_done = fence()
        vec_scope.close()

        def col(name, k, n=1):
            return cols[:, VOFF[name] + k:VOFF[name] + k + n]

        first = ExitStack()
        silu_c = sb(first, "silu_c", [P, KT, 2])
        mod = sb(first, "mod", [P, 24, 2])
        mod_cd = sb(first, "mod_odd", [P, 24, 2])
        scale1 = sb(first, "one_plus_scale", [P, KT, 2])
        gate_rows = sb(first, "gate_rows", [P, 2, D])

        def mod_chunk(mod, bias_name, ch):
            wslot, landed = mod_loads.pop(0)
            b = take1()
            for k in range(KT):
                m = mm(psum[0:2, b * BANK:b * BANK + CW], silu_c[:, k, :], wslot.tiles[0][:, k, :], k == 0, k == KT - 1,
                       [landed] + silu_ready + bank_free[b], mark=k == KT - 1)
            wslot.free = [m]
            load_mod()
            slot, w = work(CW)
            d = actv(w[0:2, :], psum[0:2, b * BANK:b * BANK + CW], ACT.Copy, [m] + slot.free)
            bank_free[b] = [d]
            b = take1()
            for j in range(2):
                m = pe.op(lambda e, j=j: e.transpose(bank(b, 2, 2 * j), w[0:2, j * P:(j + 1) * P], ident[0:2, 0:2]),
                          [d] + bank_free[b], mark=True)
            slot.free = [m]
            d = tt(dve, mod[:, 2 * ch:2 * ch + 2, :], bank(b, 4).rearrange("p (j s) -> p j s", s=2),
                   col(bias_name, 2 * ch, 2).unsqueeze(2).broadcast_to([P, 2, 2]), ALU.add, [m])
            bank_free[b] = [d]
            return d

        def gate_row(s, after, mod):
            for h in range(2):
                b = take1()
                for j in range(4):
                    slot, diag = work(P)
                    d = ts(diag, ident[:, :], mod[:, 16 + 4 * h + j, s:s + 1], None, ALU.mult, None, list(after) + slot.free)
                    m = mm(bank(b, P, j * P), ones[:, :], diag, True, True, [d, made_ones] + bank_free[b], mark=True)
                    slot.free = [m]
                g = actv(gate_rows[:, s, h * BANK:(h + 1) * BANK], bank(b), ACT.Copy, [m])
                bank_free[b] = [g]
            return g

        def turn(src, dst_hi, dst_lo, off, scale, shift, after, banks=None):
            marks = []
            for h in range(2):
                b = banks[h] if banks else take1()
                for k in range(4):
                    m = pe.op(lambda e, k=k, h=h, b=b: e.transpose(bank(b, P, k * P), src[:, (4 * h + k) * P:(4 * h + k + 1) * P],
                                                                  ident[:, :]), list(after) + bank_free[b], mark=k == 3)
                slot, w = work()
                wv = w.rearrange("p (k n) -> p k n", k=4)
                pv = bank(b).rearrange("p (k n) -> p k n", k=4)
                if h == 0 and shift is not None:
                    for k in range(4):
                        d = actv(wv[:, k, :], pv[:, k, :], ACT.Identity, [m] + slot.free, scale=scale[:, k:k + 1], bias=shift[:, k:k + 1])
                    bank_free[b] = [d]
                    slot.free = split_pair(tokens(dst_hi, slice(0, 4), off, P), tokens(dst_lo, slice(0, 4), off, P), wv, [d])
                    marks += slot.free
                    continue
                d = tt(dve, wv, pv, scale[:, 4 * h:4 * h + 4].unsqueeze(2).broadcast_to([P, 4, P]), ALU.mult, [m] + slot.free)
                bank_free[b] = [d]
                if shift is not None:
                    d = tt(dve, wv, wv, shift[:, 4 * h:4 * h + 4].unsqueeze(2).broadcast_to([P, 4, P]), ALU.add, [d])
                ks = slice(4 * h, 4 * h + 4)
                slot.free = split_pair(tokens(dst_hi, ks, off, P), tokens(dst_lo, ks, off, P), wv, [d])
                marks += slot.free
            return marks

        def project(c, j, n, hi, lo, ranges, ready, sink, take=take1):
            for r, (off, width) in enumerate(ranges):
                b = take()
                for k in range(KT):
                    m = mm3(psum[0:n, b * BANK:b * BANK + width], c.hi[:, k, j:j + n], c.lo[:, k, j:j + n],
                            tokens(hi, k, off, width), tokens(lo, k, off, width), k == 0, k == KT - 1,
                            c.ready + list(ready) + bank_free[b], mark=k == KT - 1)
                bank_free[b] = sink(r, psum[0:n, b * BANK:b * BANK + width], m)

        def project_tokens(c, hi, lo, tiles, ready, sink, take=take1):
            for t_ in tiles:
                b = take()
                for k in range(KT):
                    m = mm3(bank(b, c.n), tokens(hi, k, t_ * P, P), tokens(lo, k, t_ * P, P),
                            c.hi[:, k, :], c.lo[:, k, :], k == 0, k == KT - 1,
                            c.ready + list(ready) + bank_free[b], mark=k == KT - 1)
                bank_free[b] = sink(t_, bank(b, c.n), m)

        def down(nk, hi, lo, offs, ready, sink, follow=None):
            def part(c, ch, i, mark):
                for h in range(2):
                    b = 2 * i + h
                    for kk in range(2):
                        k = 2 * ch + kk
                        m = mm3(bank(b), tokens(hi, k, offs[i], P), tokens(lo, k, offs[i], P),
                                c.hi[:, kk, h * BANK:(h + 1) * BANK], c.lo[:, kk, h * BANK:(h + 1) * BANK],
                                k == 0, k == nk - 1, c.ready + list(ready[i]) + bank_free[b],
                                mark=mark and h == 1 and kk == 1)
                return m
            chunks, n = nk // 2, len(offs)
            for ch in range(chunks - 2):
                c = next_chunk()
                for i in range(n):
                    part(c, ch, i, ch < 1 or i == n - 1)
            pair = [next_chunk(), next_chunk(beside=True)]
            part(pair[0], chunks - 2, 0, False)
            for i in range(n):
                if i == 0:
                    part(pair[0], chunks - 2, 1, n == 2)
                elif i > 1:
                    part(pair[0], chunks - 2, i, i == n - 1)
                if i == n - 1:
                    release(1)
                if i > 1 and follow:
                    follow(i - 2)
                if i == n - 1:
                    prepare_chunk()
                m = part(pair[1], chunks - 1, i, True)
                bank_free[2 * i] = bank_free[2 * i + 1] = sink(i, psum[:, 2 * i * BANK:(2 * i + 2) * BANK], m)
            release()
            prepare_chunk()
            rot.at = 0

        def residual_layer_norm(dst, y, grow, g_row, b_row, after):
            done = []
            for h in range(2):
                slot, w = work()
                sl = slice(h * BANK, (h + 1) * BANK)
                m = tt(dve, w, y[:, sl], grow[:, sl], ALU.mult, list(after) + slot.free)
                done.append(m)
                m = stt(dst[:, sl], dst[:, sl], ALPHA, w, ALU.mult, ALU.add, [m])
                slot.free = [m]
            slot, s_ = stat()
            for h in range(2):
                st_m = dve.op(lambda e, h=h: e.bn_stats(s_[:, 6 * h:6 * h + 6], dst[:, h * BANK:(h + 1) * BANK]), [m] + slot.free)
            agg = dve.op(lambda e: e.bn_aggr(s_[:, 12:14], s_[:, 0:12]), [st_m])
            r = rsqrt(s_[:, 14:15], s_[:, 13:14], 1, 1.0, [agg])
            nb = stt(s_[:, 15:16], s_[:, 12:13], -1.0, s_[:, 14:15], ALU.mult, ALU.mult, [r, agg])
            n = actv(dst, dst, ACT.Identity, [r, nb], scale=s_[:, 14:15], bias=s_[:, 15:16])
            slot.free = [n]
            g = tt(dve, dst, dst, g_row, ALU.mult, [n] + rows_ready)
            return done, tt(pool, dst, dst, b_row, ALU.add, [g] + rows_ready)

        ctx_scope, ab = ExitStack(), ExitStack()
        h_hi = (main_hi, sb(first, "ctx_hi", [P, KT, LC], F32R))
        h_lo = (main_lo, sb(first, "ctx_lo", [P, KT, LC], F32R))
        CTX = sb(ctx_scope, "CTX", [P, NC, D])
        mod_scope = ExitStack()
        mod_ring = Ring([Slot(sb(mod_scope, "mod_w", [P, KT, CW]), [sem(f"mod_w_landed_{i}"), 0]) for i in range(6)])
        mod_plan = [(w, c0) for w in ("ab_w_mod", "cd_w_mod") for c0 in range(0, 3 * D, CW)]
        mod_loads = []

        def load_mod():
            if mod_plan:
                w, c0 = mod_plan.pop(0)
                slot = mod_ring.take()
                src = A[w][0][:, c0:c0 + CW].rearrange("(k p) n -> p k n", p=P)
                mod_loads.append((slot, load(slot.tiles[0][:, :, :], src, slot.free + vec_done, slot.tiles[1])))

        for _ in range(6):
            load_mod()
        x_in = load(X[:, :, :], A["x"][0].rearrange("(t p) d -> p t d", p=P))
        ctx_in = load(CTX[:, :, :], A["ctx"][0].rearrange("(t p) d -> p t d", p=P))
        top_up()
        for s, name in enumerate(("c", "c_ctx")):
            silu_ready = [actv(silu_c[:, :, s], col(name, 0, 8), ACT.Silu, [cols_in])]
        for ch in range(12):
            mod_ready = [mod_chunk(mod, "ab_b_mod", ch)]
        mod_ready.append(ts(scale1[:, :, :], mod[:, 8:16, :], 1.0, None, ALU.add, None, mod_ready))
        h_ready, odd_ready = [], []
        for ch in range(12):
            odd_ready = [mod_chunk(mod_cd, "cd_b_mod", ch)]
            if ch < NT:
                h_ready += turn(X[:, ch, :], h_hi, h_lo, ch * P, scale1[:, :, 0], mod[:, 0:8, 0], [x_in] + mod_ready)
            elif ch < NT + NC:
                c_ = ch - NT
                h_ready += turn(CTX[:, c_, :], h_hi, h_lo, L + c_ * P, scale1[:, :, 1], mod[:, 0:8, 1], [ctx_in] + mod_ready)
        gates_ready = [gate_row(0, mod_ready, mod), gate_row(1, mod_ready, mod)]
        mod_scope_done = fence()
        mod_scope.close()
        pooled_in = sb(ab, "pool_in", [P, 4, HALO * 3 + LA])
        silu_ga = sb(ab, "silu_ga", [P, 4, LA])
        u_gated = sb(ab, "u_gated", [P, 4, LA])
        v_norm = sb(ab, "v_norm", [P, 6, BANK])
        pool_w = sb(ab, "pool_w", [P, 4, P])
        sgu_w = v_norm[:, 5, :].rearrange("p (h j) -> p h j", h=4)
        sgu_wT = sb(ab, "sgu_wT", [P, 4, P])
        sgu_b = sb(ab, "sgu_b", [1, 4 * P])
        RANGES = ((0, L), (L, LC))
        PAD_OFF = (HALO, 2 * HALO + L)
        pool_w_in = load(pool_w[:, :, :], A["ab_pool_w"][0].rearrange("g c d -> c g d"), mod_scope_done)
        sgu_w_in = load(sgu_w[:, :, :], A["ab_sgu_w"][0].rearrange("h i j -> i h j"))
        sgu_b_in = load(sgu_b[:, :], A["ab_sgu_b"].rearrange("a h i -> a (h i)"))
        zeroed = pool.op(lambda e: e.memset(pooled_in[:, :, :], 0.0))
        for h in range(4):
            m = pe.op(lambda e, h=h: e.transpose(bank(7, P, h * P), sgu_w[:, h, :], ident[:, :]), [sgu_w_in] + bank_free[7], mark=h == 3)
        sgu_w_ready = dve.op(lambda e: e.tensor_copy(sgu_wT[:, :, :].rearrange("p h i -> p (h i)"), bank(7)), [m])
        bank_free[7] = [sgu_w_ready]

        a_marks, ga_marks, u_marks, v_marks = [], [], [], []
        sums = sb(ab, "window_sums", [P, 2, LA + 3 * HALO])
        inv_cnt = sb(ab, "inv_count", [P, LA])
        cnt_sem = [sem("inv_count_landed"), 0]
        pooled = []

        def pool_group(g, w):
            cnt_in = load(inv_cnt[:, :], A["k_inv_count"][g].partition_broadcast(P), pooled[-1:], s=cnt_sem)
            src, width, m = pooled_in[:, g, :], LA + 3 * HALO, a_marks + pooled[-1:]
            span, side = 1, 0
            while span < w:
                width -= span
                dst = sums[:, side, :]
                m = [tt(dve, dst[:, 0:width], src[:, 0:width], src[:, span:span + width], ALU.add, m)]
                src, side, span = dst, 1 - side, 2 * span
            for r, (off, n) in enumerate(RANGES):
                o, a = PAD_OFF[r] - w // 2, pooled_in[:, g, PAD_OFF[r]:PAD_OFF[r] + n]
                d = tt(dve, src[:, o:o + n], src[:, o:o + n], inv_cnt[:, off:off + n], ALU.mult, m + [cnt_in])
                d = tt(dve, a, src[:, o:o + n], a, ALU.subtract, [d])
                m = m + [d]
            pooled.append(d)

        for ch in range(10):
            if 3 <= ch < 7:
                pool_group(ch - 3, POOL_WINDOWS[ch - 3])
            c = next_chunk()
            if ch in (6, 7):
                def v_sink(t_, ps, m, ch=ch):
                    slot, s_ = stat()
                    for j in range(2):
                        o = 20 * j
                        a = dve.op(lambda e, j=j, o=o: e.bn_stats(s_[:, o:o + 6], ps[:, j * P:(j + 1) * P]), [m] + slot.free)
                        a = dve.op(lambda e, o=o: e.bn_aggr(s_[:, o + 6:o + 8], s_[:, o:o + 6]), [a])
                        r = rsqrt(s_[:, o + 8:o + 9], s_[:, o + 7:o + 8], 1, 1.0, [a])
                        hd = 2 * (ch - 6) + j
                        d = ts(v_norm[:, t_, hd * P:(hd + 1) * P], ps[:, j * P:(j + 1) * P], s_[:, o + 6:o + 7],
                               s_[:, o + 8:o + 9], ALU.subtract, ALU.mult, [r, a])
                    slot.free = [d]
                    v_marks.append(d)
                    return [d]
                project_tokens(c, h_hi, h_lo, range(6), h_ready, v_sink)
                continue
            for j in range(2):
                g = 2 * (ch % 2) + j
                if ch < 2:
                    def sink(r, ps, m, g=g):
                        d = actv(pooled_in[:, g, PAD_OFF[r]:PAD_OFF[r] + RANGES[r][1]], ps, ACT.Copy, [m, zeroed])
                        a_marks.append(d)
                        return [d]
                elif ch < 4:
                    def sink(r, ps, m, g=g):
                        o, n = RANGES[r]
                        d = actv(silu_ga[:, g, o:o + n], ps, ACT.Silu, [m])
                        ga_marks.append(d)
                        return [d]
                elif ch < 6:
                    def sink(r, ps, m, g=g):
                        o, n = RANGES[r]
                        d = actv(u_gated[:, g, o:o + n], ps, ACT.Copy, [m])
                        u_marks.append(d)
                        return [d]
                else:
                    def sink(r, ps, m, g=g):
                        o, n = RANGES[r]
                        slot, w = work(n)
                        s_ = actv(w, ps, ACT.Silu, [m] + slot.free)
                        d = tt(dve, u_gated[:, g, o:o + n], u_gated[:, g, o:o + n], w, ALU.mult, [s_] + u_marks)
                        slot.free = [d]
                        u_marks.append(d)
                        return [s_]
                project(c, j * P, P, h_hi, h_lo, RANGES, h_ready, sink)

        h_read = pe.now()
        mix_marks = []
        for g in range(4):
            for r, (off, n) in enumerate(RANGES):
                b = take1()
                q = mm(bank(b, n), pool_w[:, g, :], pooled_in[:, g, PAD_OFF[r]:PAD_OFF[r] + n], True, True,
                       [pooled[g], pool_w_in] + bank_free[b], mark=True)
                slot, wk = work(n)
                d = stt(wk, bank(b, n), col("ab_pool_scale", g), silu_ga[:, g, off:off + n], ALU.mult, ALU.mult, [q] + ga_marks + slot.free)
                bank_free[b] = [d]
                slot.free = split_pair(tokens(h_hi, g, off, n), tokens(h_lo, g, off, n), wk, [d] + h_read)
                mix_marks += slot.free
        for hd in range(4):
            for r, (off, n) in enumerate(RANGES):
                b = take1()
                for q in range(n // P):
                    ck = off // P + q
                    mm(bank(b, P, q * P), v_norm[:, ck, hd * P:(hd + 1) * P], sgu_wT[:, hd, :], True, False,
                       v_marks + [sgu_w_ready] + bank_free[b])
                    m = mm(bank(b, P, q * P), ones[0:1, :], sgu_b[0:1, hd * P:(hd + 1) * P], False, True, [sgu_b_in], mark=True)
                slot, wk = work(n)
                d = tt(dve, wk, bank(b, n), u_gated[:, hd, off:off + n], ALU.mult, [m] + u_marks + slot.free)
                bank_free[b] = [d]
                slot.free = split_pair(tokens(h_hi, 4 + hd, off, n), tokens(h_lo, 4 + hd, off, n), wk, [d] + h_read)
                mix_marks += slot.free
        fence()
        ab.close()

        tail = ExitStack()
        g_row = sb(tail, "g_row", [P, D])
        b_row = sb(tail, "b_row", [P, D])
        row_sems = [[sem("g_row_landed"), 0], [sem("b_row_landed"), 0]]
        rows_ready = [load(g_row[:, :], A["ab_ln_g"][0].partition_broadcast(P), pe.now() + dve.now() + act.now(), s=row_sems[0]),
                      load(b_row[:, :], A["ab_ln_b"][0].partition_broadcast(P), s=row_sems[1])]
        x_marks, c_marks = [], []

        def x_sink(i, y, m):
            done, ready = residual_layer_norm(X[:, i, :], y, gate_rows[:, 0, :], g_row[:, :], b_row[:, :], [m] + gates_ready)
            x_marks.append(ready)
            return done

        scale_odd = sb(tail, "one_plus_scale_odd", [P, KT, 2])
        odd_ready.append(ts(scale_odd[:, :, :], mod_cd[:, 8:16, :], 1.0, None, ALU.add, None, odd_ready))
        h_ready = []

        def x_follow(i):
            h_ready.extend(turn(X[:, i, :], h_hi, h_lo, i * P, scale_odd[:, :, 0], mod_cd[:, 0:8, 0],
                                [x_marks[i]] + odd_ready, (2 * i, 2 * i + 1)))

        def c_follow(i):
            h_ready.extend(turn(CTX[:, i, :], h_hi, h_lo, L + i * P, scale_odd[:, :, 1], mod_cd[:, 0:8, 1],
                                [c_marks[i]] + odd_ready, (2 * i, 2 * i + 1)))

        def c_sink(i, y, m):
            done, ready = residual_layer_norm(CTX[:, i, :], y, gate_rows[:, 1, :], g_row[:, :], b_row[:, :], [m] + gates_ready)
            c_marks.append(ready)
            return done

        down(KT, h_hi, h_lo, [L + t_ * P for t_ in range(NC)], [mix_marks] * NC, c_sink)
        c_follow(0)
        c_follow(1)
        down(KT, h_hi, h_lo, [t_ * P for t_ in range(NT)], [mix_marks] * NT, x_sink, x_follow)
        x_follow(2)
        x_follow(3)
        gates_ready = [gate_row(0, odd_ready + x_marks, mod_cd)]
        fence()
        tail.close()

        ctx_scope.close()
        cd = ExitStack()
        silu_dg = sb(cd, "silu_dgate", [P, 4, L])
        cqT = sb(cd, "cqT", [P, 2, L])
        ckvT = sb(cd, "ckvT", [P, LA])
        krT = sb(cd, "krT", [P, LA])
        fourier = ExitStack()
        f_in = sb(fourier, "f_in", [P, 4, L])
        silu_fg = sb(fourier, "silu_fgate", [P, 4, L])
        dft_d = sb(fourier, "dft_d", [P, 2 * P])
        dft_l = sb(fourier, "dft_l", [P, 4, 2, L])
        f_cs = sb(fourier, "f_cs", [P, NT, 2 * P])
        spec_hi, spec_lo = main_hi[:, 4:8, :], main_lo[:, 4:8, :]
        dft_in = [load(dft_d[:, :], A["k_dft_d"], pe.now() + dve.now() + act.now()), load(dft_l[:, :, :, :], A["k_dft_l"].rearrange("(t p) s l -> p t s l", p=P))]
        f_marks, fg_marks, dg_marks, lat_marks = [], [], [], []
        nrm = ExitStack()
        for ch in range(8):
            c = next_chunk()
            if ch == 4:
                def q_sink(t_, ps, m):
                    slot, s_ = stat()
                    ws, w = work(256)
                    sq = actv(w, ps, ACT.Square, [m] + slot.free + ws.free, accum_out=s_[:, 0:1])
                    r = rsqrt(s_[:, 1:2], s_[:, 0:1], 1, 1.0 / 256, [sq])
                    d = ts(w, ps, s_[:, 1:2], None, ALU.mult, None, [r, sq])
                    slot.free = [d]
                    b = take1()
                    for k in range(2):
                        q = pe.op(lambda e, k=k: e.transpose(bank(b, P, k * P), w[:, k * P:(k + 1) * P], ident[:, :]),
                                  [d] + bank_free[b], mark=True)
                    ws.free = [q]
                    for k in range(2):
                        d2 = ts(cqT[:, k, t_ * P:(t_ + 1) * P], bank(b, P, k * P), col("cd_q_norm", k), None, ALU.mult, None, [q])
                    bank_free[b] = [d2]
                    lat_marks.append(d2)
                    return [d]
                project_tokens(c, h_hi, h_lo, range(NT), h_ready, q_sink)
                continue
            if ch == 5:
                def kv_sink(t_, ps, m):
                    slot, s_ = stat()
                    ws, w = work(160)
                    sq = actv(w[:, 0:P], ps[:, 0:P], ACT.Square, [m] + slot.free + ws.free, accum_out=s_[:, 0:1])
                    r = rsqrt(s_[:, 1:2], s_[:, 0:1], 1, 1.0 / P, [sq])
                    d = ts(w[:, 0:P], ps[:, 0:P], s_[:, 1:2], None, ALU.mult, None, [r, sq])
                    d3 = dve.op(lambda e: e.tensor_copy(w[:, P:160], ps[:, P:160]), [m])
                    slot.free = [d]
                    b = take1()
                    pe.op(lambda e: e.transpose(bank(b, P), w[:, 0:P], ident[:, :]), [d, d3] + bank_free[b], mark=False)
                    q = pe.op(lambda e: e.transpose(psum[0:QK, b * BANK + P:b * BANK + 2 * P], w[:, 64:160], ident[:, :]))
                    ws.free = [q]
                    d2 = ts(ckvT[:, t_ * P:(t_ + 1) * P], bank(b, P), col("cd_kv_norm", 0), None, ALU.mult, None, [q])
                    d4 = dve.op(lambda e: e.tensor_copy(krT[0:QK, t_ * P:(t_ + 1) * P], psum[0:QK, b * BANK + P:b * BANK + 2 * P]), [q])
                    bank_free[b] = [d4]
                    lat_marks.extend([d2, d4])
                    return [d3]
                project_tokens(c, h_hi, h_lo, range(6), h_ready, kv_sink)
                continue
            for j in range(2):
                g = 2 * (ch % 2) + j

                def sink(r, ps, m, g=g, ch=ch):
                    if ch < 2:
                        d = actv(f_in[:, g, :], ps, ACT.Copy, [m])
                        f_marks.append(d)
                    elif ch < 4:
                        d = actv(silu_fg[:, g, :], ps, ACT.Silu, [m])
                        fg_marks.append(d)
                    else:
                        d = actv(silu_dg[:, g, :], ps, ACT.Silu, [m])
                        dg_marks.append(d)
                    return [d]
                project(c, j * P, P, h_hi, h_lo, RANGES[:1], h_ready, sink)
        h_read = pe.now()

        mix_marks, spec_marks, cs_free = [], [], []
        for hd in range(4):
            cs_marks = []
            for t_ in range(NT):
                b = take1()
                m = mm(bank(b, 256), f_in[:, hd, t_ * P:(t_ + 1) * P], dft_d[:, :], True, True, f_marks + dft_in + bank_free[b], mark=True)
                d = actv(f_cs[:, t_, :], bank(b, 256), ACT.Copy, [m] + cs_free)
                bank_free[b] = [d]
                cs_marks.append(d)
            b = take1()
            for t_ in range(NT):
                for s in range(2):
                    m = mm(bank(b), f_cs[:, t_, s * P:(s + 1) * P], dft_l[:, t_, s, :], t_ == 0 and s == 0, t_ == 3 and s == 1,
                           cs_marks + bank_free[b], mark=True)
            cs_free = [m]
            bank_free[b] = split_pair(spec_hi[:, hd, :], spec_lo[:, hd, :], bank(b), [m] + h_read)
            spec_marks += bank_free[b]
        for ch in range(2):
            c = next_chunk()
            for j in range(2):
                b = take1()
                for k in range(4):
                    m = mm3(bank(b), c.hi[:, k, j * P:(j + 1) * P], c.lo[:, k, j * P:(j + 1) * P], spec_hi[:, k, :], spec_lo[:, k, :],
                            k == 0, k == 3, c.ready + spec_marks + bank_free[b], mark=k == 3)
                g = 2 * ch + j
                slot, w = work()
                d = tt(dve, w, bank(b), silu_fg[:, g, :], ALU.mult, [m] + fg_marks + slot.free)
                bank_free[b] = [d]
                slot.free = split_pair(main_hi[:, g, :], main_lo[:, g, :], w, [d] + h_read)
                mix_marks += slot.free
        f = fence()
        fourier.close()

        mla = ExitStack()
        q_up = sb(mla, "q_up", [P, 2, HEADS * QK])
        kv_up = sb(mla, "kv_up", [P, D])
        rope_c = sb(mla, "rope_cos", [QK, L])
        rope_s = sb(mla, "rope_sin", [QK, L])
        swap = sb(mla, "rope_swap", [QK, QK])
        v_all = sb(mla, "v_all", [P, 6, HEADS * 64])
        head_ring = Ring([Slot(sb(mla, "kT_head", [QK, LA]), sb(mla, "qT_head", [QK, L])) for _ in range(2)])
        p_ring = Ring([Slot(sb(mla, "probs", [P, LA])) for _ in range(2)])
        pT_ring = Ring([Slot(sb(mla, "probsT", [P, LA])) for _ in range(2)])
        o_tok = sb(mla, "o_tok", [P, NT, HEADS * 64])
        mla_in = [load(q_up[:, :, :], A["cd_w_q_up"][0].rearrange("(k p) n -> p k n", p=P), f),
                  load(kv_up[:, :], A["cd_w_kv_up"][0]), load(rope_c[:, :], A["k_rope_cos"]),
                  load(rope_s[:, :], A["k_rope_sin"]), load(swap[:, :], A["k_rope_swap"])]

        def rope(t_, after):
            b = take1()
            o = psum[0:QK, b * BANK:(b + 1) * BANK]
            m = mm(o, swap[:, :], t_[0:QK, 0:L], True, True, list(after) + mla_in + bank_free[b], mark=True)
            slot, w = work()
            d = tt(dve, w[0:QK, :], o, rope_s[:, :], ALU.mult, [m] + slot.free)
            bank_free[b] = [d]
            d2 = tt(dve, t_[0:QK, 0:L], t_[0:QK, 0:L], rope_c[:, :], ALU.mult, [m])
            d = tt(dve, t_[0:QK, 0:L], t_[0:QK, 0:L], w[0:QK, :], ALU.add, [d, d2])
            slot.free = [d]
            return d

        kr_ready = rope(krT, lat_marks)
        v_marks = []
        v_cols = kv_up[:, :].rearrange("p (h c) -> p h c", h=HEADS)[:, :, NOPE:P]
        for t_ in range(6):
            b = take1()
            m = mm(bank(b).rearrange("p (h c) -> p h c", h=HEADS), ckvT[:, t_ * P:(t_ + 1) * P], v_cols, True, True,
                   lat_marks + mla_in + bank_free[b], mark=True)
            d = actv(v_all[:, t_, :], bank(b), ACT.Copy, [m])
            bank_free[b] = [d]
            v_marks.append(d)
        SC = QK ** -0.5
        o_marks = []

        def head_keys(hd):
            slot = head_ring.take()
            kT, qT = slot.tiles
            for off, n in RANGES:
                b = take1()
                m = mm(psum[0:NOPE, b * BANK:b * BANK + n], kv_up[:, hd * P:hd * P + NOPE], ckvT[:, off:off + n], True, True,
                       lat_marks + mla_in + bank_free[b], mark=True)
                k_up = actv(kT[0:NOPE, off:off + n], psum[0:NOPE, b * BANK:b * BANK + n], ACT.Copy, [m] + slot.free)
                bank_free[b] = [k_up]
            heads[hd] = [slot, kT, qT, [k_up] + shared_keys]

        def head_queries(hd):
            slot, _, qT, ready = heads[hd]
            b = take1()
            for k in range(2):
                m = mm(psum[0:QK, b * BANK:(b + 1) * BANK], q_up[:, k, hd * QK:(hd + 1) * QK], cqT[:, k, :], k == 0, k == 1,
                       bank_free[b], mark=True)
            q = actv(qT[:, :], psum[0:QK, b * BANK:(b + 1) * BANK], ACT.Copy, [m] + slot.free)
            bank_free[b] = [q]
            ready.append(q)

        def head_rope(hd):
            heads[hd][3].append(rope(heads[hd][2], heads[hd][3][-1:]))

        heads = {}
        shared_keys = [actv(slot.tiles[0][NOPE:QK, :], krT[NOPE:QK, :], ACT.Copy, [kr_ready] + lat_marks) for slot in head_ring.slots]
        beside = {0: head_keys, 1: head_queries, 2: head_rope}
        for make in beside.values():
            make(0)

        def mla_scores(hd, t_):
            slot, kT, qT, ready = heads[hd]
            b = take2()
            for j, (off, n) in enumerate(RANGES):
                m = mm(bank(b + j, n), qT[:, t_ * P:(t_ + 1) * P], kT[:, off:off + n], True, True, ready + bank_free[b + j], mark=True)
            if t_ == NT - 1:
                slot.free = [m]
            s = psum[:, b * BANK:b * BANK + LA]
            sslot, s_ = stat()
            mx = dve.op(lambda e: e.tensor_reduce(s_[:, 0:1], s, AX.X, ALU.max), [m] + sslot.free)
            nm = ts(s_[:, 1:2], s_[:, 0:1], -SC, None, ALU.mult, None, [mx])
            ps = p_ring.take()
            pr = ps.tiles[0]
            ex = actv(pr[:, :], s, ACT.Exp, [nm] + ps.free, bias=s_[:, 1:2], scale=SC, accum_out=s_[:, 2:3])
            bank_free[b] = bank_free[b + 1] = [ex]
            return ps, pr, sslot, s_, ex

        def mla_turn(it):
            ps, pr, sslot, s_, ex = it
            b = take2()
            for k in range(6):
                bb = b + k // 4
                m = pe.op(lambda e, k=k, bb=bb: e.transpose(bank(bb, P, (k % 4) * P), pr[:, k * P:(k + 1) * P], ident[:, :]),
                          [ex] + bank_free[bb], mark=True)
            ps.free = [m]
            pt = pT_ring.take()
            c1 = actv(pt.tiles[0][:, 0:BANK], bank(b), ACT.Copy, [m] + pt.free)
            c2 = dve.op(lambda e: e.tensor_copy(pt.tiles[0][:, BANK:LA], bank(b + 1, LA - BANK)), [m] + pt.free)
            bank_free[b], bank_free[b + 1] = [c1], [c2]
            rc = dve.op(lambda e: e.reciprocal(s_[:, 3:4], s_[:, 2:3]), [ex])
            return pt, [c1, c2], sslot, s_, rc

        def mla_values(it, hd, t_):
            pt, ready, sslot, s_, rc = it
            b = take1()
            for k in range(6):
                m = mm(bank(b, 64), pt.tiles[0][:, k * P:(k + 1) * P], v_all[:, k, hd * 64:(hd + 1) * 64], k == 0, k == 5,
                       ready + v_marks + bank_free[b], mark=True)
            pt.free = [m]
            d = ts(o_tok[:, t_, hd * 64:(hd + 1) * 64], bank(b, 64), s_[:, 3:4], None, ALU.mult, None, [m, rc])
            bank_free[b] = [d]
            sslot.free = [d]
            o_marks.append(d)

        seq = [(hd, t_) for hd in range(HEADS) for t_ in range(NT)]
        a1, a2 = {}, {}
        for n in range(len(seq) + 2):
            if n < len(seq):
                a1[n] = mla_scores(*seq[n])
            if 0 <= n - 1 < len(seq):
                a2[n - 1] = mla_turn(a1.pop(n - 1))
            if 0 <= n - 2 < len(seq):
                mla_values(a2.pop(n - 2), *seq[n - 2])
            if n < len(seq) and seq[n][0] + 1 < HEADS and seq[n][1] in beside:
                beside[seq[n][1]](seq[n][0] + 1)
        for t_ in range(NT):
            b = take1()
            for k in range(4):
                m = pe.op(lambda e, k=k, b=b, t_=t_: e.transpose(bank(b, P, k * P), o_tok[:, t_, k * P:(k + 1) * P], ident[:, :]),
                          o_marks + bank_free[b], mark=True)
            slot, w = work()
            wv = w.rearrange("p (k n) -> p k n", k=4)
            d = tt(dve, wv, bank(b).rearrange("p (k n) -> p k n", k=4), silu_dg[:, :, t_ * P:(t_ + 1) * P], ALU.mult, [m] + dg_marks + slot.free)
            bank_free[b] = [d]
            slot.free = split_pair(main_hi[:, 4:8, t_ * P:(t_ + 1) * P], main_lo[:, 4:8, t_ * P:(t_ + 1) * P], wv, [d] + h_read)
            mix_marks += slot.free
        fence()
        mla.close()
        cd.close()
        tail = ExitStack()
        g_row = sb(tail, "g_row", [P, D])
        b_row = sb(tail, "b_row", [P, D])
        free = pe.now() + dve.now() + act.now()
        rows_ready = [load(g_row[:, :], A["cd_ln_g"][0].partition_broadcast(P), free, s=row_sems[0]),
                      load(b_row[:, :], A["cd_ln_b"][0].partition_broadcast(P), s=row_sems[1])]
        wide_ring = Ring([Slot(sb(tail, "wide", [P, D])) for _ in range(2)])
        HALVES = ((0, L // 2), (L // 2, L // 2))

        def rms_turn(g_name, layer, t_, x_ready, banks):
            (slot, s_), ws = stat(), wide_ring.take()
            wide = ws.tiles[0]
            sq = actv(wide[:, :], X[:, t_, :], ACT.Square, [x_ready] + ws.free + slot.free, accum_out=s_[:, 0:1])
            r = rsqrt(s_[:, 1:2], s_[:, 0:1], 1, 1.0 / D, [sq])
            diag = wide[:, 0:P]
            d = ts(diag, ident[:, :], s_[:, 1:2], None, ALU.mult, None, [r, sq])
            slot.free = [d]
            marks, at_ = [], slice(t_ * P, (t_ + 1) * P)
            for h in range(2):
                b = banks[h]
                for j in range(4):
                    k = 4 * h + j
                    m = mm(bank(b, P, j * P), X[:, t_, k * P:(k + 1) * P], diag, True, True, [d] + bank_free[b], mark=j == 3)
                for j in range(4):
                    k = 4 * h + j
                    made_hi = actv(main_hi[:, k, at_], bank(b, P, j * P), ACT.Copy, [m], scale=col(g_name, 8 * layer + k))
                for j in range(4):
                    k = 4 * h + j
                    made_lo = stt(main_lo[:, k, at_], bank(b, P, j * P), col(g_name, 8 * layer + k), main_hi[:, k, at_].bitcast(F32),
                                  ALU.mult, ALU.subtract, [m, made_hi])
                bank_free[b] = [made_lo]
                marks += [made_hi, made_lo]
            ws.free = [m]
            return marks

        def follow_with(g_name, layer, x_new, ready):
            def follow(i):
                ready[i] += rms_turn(g_name, layer, i, x_new[i], (2 * i, 2 * i + 1))
            return follow if g_name else None

        def first_groups(groups, ready, follow):
            for half in range(2):
                marks = ready[2 * half] + ready[2 * half + 1]
                for n, (c, j, sink) in enumerate(groups):
                    project(c, j, P, h_hi, h_lo, HALVES[half:half + 1], marks, sink(half))
                    if half == 0 and n in (1, 2):
                        follow(n + 1)
                    if half == 1 and n == 1:
                        release(1)
                        prepare_chunk()

        x_marks, ready = [], [[] for _ in range(NT)]
        follow = follow_with("ffn1_pre_g_2", 0, x_marks, ready)
        down(KT, h_hi, h_lo, [t_ * P for t_ in range(NT)], [mix_marks] * NT, x_sink, follow)
        tail.close()
        first.close()

        second = ExitStack()
        wide_ring = Ring([Slot(sb(second, "wide", [P, D])) for _ in range(2)])
        post_g = sb(second, "post_g", [P, D])
        post_free = pe.now() + act.now() + dve.now() + pool.now()

        def residual_rms(weight, g_ready, x_new):
            def sink(i, y, m):
                (slot, s_), ws = stat(), wide_ring.take()
                wide = ws.tiles[0]
                sq = actv(wide[:, :], y, ACT.Square, [m] + ws.free + slot.free, accum_out=s_[:, 0:1])
                r = rsqrt(s_[:, 1:2], s_[:, 0:1], 1, 1.0 / D, [sq], weight)
                d = stt(wide[:, :], y, s_[:, 1:2], post_g[:, :], ALU.mult, ALU.mult, [r, sq, g_ready])
                slot.free = [d]
                x_new[i] = tt(dve, X[:, i, :], X[:, i, :], wide[:, :], ALU.add, [d])
                ws.free = [x_new[i]]
                return [sq, d]
            return sink

        post_sem = [sem("post_g_landed"), 0]

        def ffn(f, layer, ready, follow, post_free, next_g, next_layer):
            scope = ExitStack()
            act_hi = sb(scope, "ff_hi", [P, FT, L], F32R)
            act_lo = sb(scope, "ff_lo", [P, FT, L], F32R)
            marks, gates = [], []

            def gate_sink(r, ps, m):
                slot, w = work(ps.shape[-1])
                d = actv(w, ps, ACT.Silu, [m] + slot.free)
                gates.append((slot, w, d))
                return [d]

            def up_sink(k, off, n):
                def sink(r, ps, m):
                    slot, w, s_ = gates.pop(0)
                    d = tt(dve, w, w, ps, ALU.mult, [m, s_])
                    slot.free = split_pair(act_hi[:, k, off:off + n], act_lo[:, k, off:off + n], w, [d])
                    marks.extend(slot.free)
                    return [d]
                return sink

            c, c2 = next_chunk(), next_chunk(beside=True)
            first_groups([(c, j * P, lambda half: gate_sink) for j in range(2)] +
                         [(c2, j * P, lambda half, j=j: up_sink(j, *HALVES[half])) for j in range(2)], ready, follow)
            ready = sum(ready, [])
            g_ready = load(post_g[:, :], A[f"ffn{f}_post_g_2"][layer].partition_broadcast(P), post_free, s=post_sem)
            for ch in range(1, FF // CW):
                c = next_chunk()
                for j in range(2):
                    project(c, j * P, P, h_hi, h_lo, RANGES[:1], ready, gate_sink)
                c = next_chunk()
                for j in range(2):
                    project(c, j * P, P, h_hi, h_lo, RANGES[:1], ready, up_sink(2 * ch + j, 0, L))
            new, next_ready = [None] * NT, [[] for _ in range(NT)]
            follow = follow_with(next_g, next_layer, new, next_ready)
            down(FT, (act_hi, None), (act_lo, None), [t_ * P for t_ in range(NT)], [marks] * NT, residual_rms(0.5, g_ready, new), follow)
            scope.close()
            return new, next_ready, follow, pe.now() + act.now() + dve.now()

        def mixing(layer, ready, follow, post_free):
            lam_init = 0.8 - 0.6 * math.exp(-0.3 * layer)
            sc = ExitStack()
            q_a, k_a, q_c, k_c = (sb(sc, n, [P, 3, L]) for n in ("q_a", "k_a", "q_c", "k_c"))
            q_b, k_b = (sb(sc, n, [P, 2, L]) for n in ("q_b", "k_b"))
            v_a, v_c = (sb(sc, n, [P, NT, 384]) for n in ("v_a", "v_c"))
            v_b = sb(sc, "v_b", [P, NT, 256])
            far = sb(sc, "far_bias", [P, 6])
            dist = sb(sc, "distance", [P, L])
            strict = sb(sc, "strict", [P, 2, P])
            tri = sb(sc, "suffix_tri", [P, P])
            lam = sb(sc, "lambda", [P, 4, 32])
            lam_s = sb(sc, "lambda_stats", [P, 8])
            sub_g = sb(sc, "subln_g", [P, 64])
            bias = sb(sc, "band_bias", [P, 6, 256])
            o_tok = sb(sc, "o_tok", [P, NT, 640])
            squares = sb(sc, "squares", [P, 256])
            w0, w1 = (w.tiles[0] for w in wide_ring.slots)
            a_ring = Ring([Slot(w0[:, 0:L]), Slot(w0[:, L:D])])
            map_rings = [Ring([Slot(w1[:, 0:L]), Slot(w1[:, L:D])]), Ring([Slot(sb(sc, "scores", [P, L]))])]
            turned = {"a": Ring(work_ring.slots[0:2]), "b": Ring(work_ring.slots[2:3])}
            starts = {0: 0, 1: 512, 3: 896, 2: 1024}
            SW = 1280
            stick_ring = Ring([Slot(sb(sc, "softplus", [P, SW]), sb(sc, "log_weights", [P, SW])) for _ in range(2)])
            marks = {n: [] for n in "abc"}

            def put(dst, name, scale, off=0, n=L):
                def sink(r, ps, m):
                    d = actv(dst[:, off:off + n], ps, ACT.Copy, [m], scale=scale)
                    marks[name].append(d)
                    return [d]
                return sink

            feature = {}
            for i in range(3):
                feature[i * P] = (q_a[:, i, :], "a", 0.125)
                feature[384 + i * P] = (k_a[:, i, :], "a", 1.0)
                feature[1920 + i * P] = (q_c[:, i, :], "c", 0.125)
                feature[2304 + i * P] = (k_c[:, i, :], "c", 1.0)
            for i in range(2):
                feature[1152 + i * P] = (q_b[:, i, :], "b", 1.0)
                feature[1408 + i * P] = (k_b[:, i, :], "b", 1.0)
            pair = []
            for beside, (c0, n) in enumerate(MIX_CHUNKS[:2]):
                c = next_chunk(beside=bool(beside))
                pair += [(c, j * P, lambda half, f_=feature[c0 + j * P]: put(*f_, *HALVES[half])) for j in range(n // P)]
            first_groups(pair, ready, follow)
            ready = sum(ready, [])
            g_ready = load(post_g[:, :], A["mix_post_g_2"][layer].partition_broadcast(P), post_free, s=post_sem)
            consts = [sem(f"mix_consts_{layer}"), 0]
            for dst, src in ((bias[:, :, :], A["l_band_bias"][layer].rearrange("h q k -> q h k")),
                             (far[:, :], A["l_far_bias"][layer].partition_broadcast(P)),
                             (dist[:, :], A["k_distance"]), (strict[:, :, :], A["k_strict"].rearrange("s p n -> p s n")),
                             (tri[:, :], A["k_tri"]), (sub_g[:, :], A["diff_subln_g_2"][layer].partition_broadcast(P)),
                             (lam[:, 0, :], A["diff_lambda_q1_2"][layer].partition_broadcast(P)),
                             (lam[:, 1, :], A["diff_lambda_k1_2"][layer].partition_broadcast(P)),
                             (lam[:, 2, :], A["diff_lambda_q2_2"][layer].partition_broadcast(P)),
                             (lam[:, 3, :], A["diff_lambda_k2_2"][layer].partition_broadcast(P))):
                in_ = load(dst, src, post_free, s=consts)
            masked = pool.op(lambda e: e.memset(bias[0:64, :, 192:256], NEG), [in_])
            for i in range(2):
                d = tt(dve, lam[:, 2 * i, :], lam[:, 2 * i, :], lam[:, 2 * i + 1, :], ALU.mult, [in_])
                d = dve.op(lambda e, i=i: e.tensor_reduce(lam_s[:, i:i + 1], lam[:, 2 * i, :], AX.X, ALU.add), [d])
            ex = actv(lam_s[:, 2:4], lam_s[:, 0:2], ACT.Exp, [d])
            d = tt(dve, lam_s[:, 4:5], lam_s[:, 2:3], lam_s[:, 3:4], ALU.subtract, [ex])
            lam_ready = ts(lam_s[:, 5:6], lam_s[:, 4:5], -1.0, -lam_init, ALU.mult, ALU.add, [d])
            g_scaled = ts(sub_g[:, :], sub_g[:, :], 1.0 - lam_init, None, ALU.mult, None, [in_])

            values = ((768, 1152, v_a, "a"), (1664, 1920, v_b, "b"), (2688, 3072, v_c, "c"))
            proj_banks, soft_banks, stick_banks = Ring([0, 1]), Ring([2, 3, 4]), Ring([5, 6, 7])

            def a_scores(h, t_):
                width, p0 = (t_ + 1) * P, 64 * (h % 2)
                b = soft_banks.take()
                m = mm(bank(b, width), q_a[p0:p0 + 64, h // 2, t_ * P:(t_ + 1) * P], k_a[p0:p0 + 64, h // 2, 0:width], True, True,
                       marks["a"] + bank_free[b], mark=True)
                slot, (sslot, s_) = a_ring.take(), stat()
                w = slot.tiles[0][:, 0:width]
                near = min(width, 256)
                d = tt(dve, w[:, width - near:width], bank(b, near, width - near), bias[:, h, 256 - near:256], ALU.add, [m, masked] + slot.free)
                if width > near:
                    d = ts(w[:, 0:width - near], bank(b, width - near), far[:, h:h + 1], None, ALU.add, None, [m])
                bank_free[b] = [d]
                mx = dve.op(lambda e: e.tensor_reduce(s_[:, 0:1], w, AX.X, ALU.max, negate=True), [d] + sslot.free)
                ex = actv(w, w, ACT.Exp, [mx], bias=s_[:, 0:1], accum_out=s_[:, 1:2])
                return slot, w, sslot, s_, ex

            def b_scores(h, t_):
                width = (t_ + 1) * P
                sslot, s_ = stat()
                slope, sc_ = 2.0 ** (-8.0 * (h + 1) / 4), 32 ** -0.5
                maps = []
                for mp in range(2):
                    blk = 2 * h + mp
                    p0 = 32 * (blk % 4)
                    b = soft_banks.take()
                    m = mm(bank(b, width), q_b[p0:p0 + 32, blk // 4, t_ * P:(t_ + 1) * P], k_b[p0:p0 + 32, blk // 4, 0:width], True, True,
                           marks["b"] + bank_free[b], mark=True)
                    slot, o = map_rings[mp].take(), 4 * mp
                    w = slot.tiles[0][:, 0:width]
                    d = stt(w, dist[:, L - width:L], slope / sc_, bank(b, width), ALU.mult, ALU.add, [m, in_] + slot.free)
                    bank_free[b] = [d]
                    mx = dve.op(lambda e, o=o, w=w: e.tensor_reduce(s_[:, o:o + 1], w, AX.X, ALU.max), [d] + sslot.free)
                    mx = ts(s_[:, o + 1:o + 2], s_[:, o:o + 1], -sc_, None, ALU.mult, None, [mx])
                    ex = actv(w, w, ACT.Exp, [mx], bias=s_[:, o + 1:o + 2], scale=sc_, accum_out=s_[:, o + 2:o + 3])
                    maps.append((slot, w, ex))
                return maps, sslot, s_

            def b_weights(maps, sslot, s_):
                (slot0, w0_, ex0), (slot1, w1_, ex1) = maps
                rc = [dve.op(lambda e, o=o: e.reciprocal(s_[:, o + 3:o + 4], s_[:, o + 2:o + 3]), [ex])
                      for o, ex in ((0, ex0), (4, ex1))]
                d = tt(dve, s_[:, 8:9], s_[:, 7:8], lam_s[:, 5:6], ALU.mult, rc + [lam_ready])
                d = ts(w1_, w1_, s_[:, 8:9], None, ALU.mult, None, [d, ex1])
                d = stt(w0_, w0_, s_[:, 3:4], w1_, ALU.mult, ALU.add, rc + [d, ex0])
                slot1.free, sslot.free = [d], [d]
                return slot0, d

            def turn_probs(kind, slot, t_, ready):
                b = soft_banks.take()
                for k in range(t_ + 1):
                    m = pe.op(lambda e, k=k: e.transpose(bank(b, P, k * P), slot.tiles[0][:, k * P:(k + 1) * P], ident[:, :]),
                              [ready] + bank_free[b], mark=k == t_)
                slot.free = [m]
                pt = turned[kind].take()
                width = (t_ + 1) * P
                d = actv(pt.tiles[0][:, 0:width], bank(b, width), ACT.Copy, [m] + pt.free)
                bank_free[b] = [d]
                return pt, d

            def apply_values(kind, pt, ready, h, t_):
                b = soft_banks.take()
                v = v_a if kind == "a" else v_b
                for k in range(t_ + 1):
                    m = mm(bank(b, 64), pt.tiles[0][:, k * P:(k + 1) * P], v[:, k, h * 64:(h + 1) * 64], k == 0, k == t_,
                           [ready] + marks[kind] + bank_free[b], mark=k == t_)
                pt.free = [m]
                return b, m

            o_marks = [[] for _ in range(NT)]

            def band():
                scored, turned_ = None, None
                for h, t_ in [(h, t_) for t_ in range(NT) for h in range(6)] + [(None, None)] * 2:
                    if turned_:
                        pt, d, sslot, s_, ex, h2, t2 = turned_
                        b, m = apply_values("a", pt, d, h2, t2)
                        rc = dve.op(lambda e, s_=s_: e.reciprocal(s_[:, 2:3], s_[:, 1:2]), [ex])
                        o = ts(o_tok[:, t2, h2 * 64:(h2 + 1) * 64], bank(b, 64), s_[:, 2:3], None, ALU.mult, None, [m, rc])
                        sslot.free, bank_free[b] = [o], [o]
                        o_marks[t2].append(o)
                    turned_ = scored and turn_probs("a", scored[0], scored[6], scored[4]) + scored[2:]
                    scored = None if h is None else a_scores(h, t_) + (h, t_)
                    yield

            def differential():
                scored, weighed, turned_ = None, None, None
                for h, t_ in [(h, t_) for t_ in range(NT) for h in range(4)] + [(None, None)] * 3:
                    if turned_:
                        pt, d, h3, t3 = turned_
                        b, m = apply_values("b", pt, d, h3, t3)
                        o = actv(o_tok[:, t3, 384 + h3 * 64:384 + (h3 + 1) * 64], bank(b, 64), ACT.Copy, [m])
                        bank_free[b] = [o]
                        o_marks[t3].append(o)
                    turned_ = weighed and turn_probs("b", weighed[0], weighed[3], weighed[1]) + weighed[2:]
                    weighed = scored and b_weights(*scored[:3]) + scored[3:]
                    scored = None if h is None else b_scores(h, t_) + (h, t_)
                    yield

            def stick_scores(h):
                p0 = 64 * (h % 2)
                slot = stick_ring.take()
                soft, z = slot.tiles
                copied = []
                for tiles, o, n in (((0,), 0, 512), ((1, 3), 512, 512), ((2,), 1024, 256)):
                    b = stick_banks.take()
                    for kt in tiles:
                        m = mm(bank(b, L - kt * P, starts[kt] - o), k_c[p0:p0 + 64, h // 2, kt * P:(kt + 1) * P], q_c[p0:p0 + 64, h // 2, kt * P:L],
                               True, True, marks["c"] + bank_free[b], mark=True)
                    zc = actv(z[:, o:o + n], bank(b, n), ACT.Copy, [m] + slot.free)
                    bank_free[b] = [zc]
                    copied.append(zc)
                return slot, copied + slot.free

            def stick_abs(slot, ready):
                soft, z = slot.tiles
                a_ = actv(soft[:, :], z[:, :], ACT.Abs, ready)
                return actv(soft[:, :], soft[:, :], ACT.Exp, [a_], scale=-1.0)

            def stick_log(slot, ready):
                soft = slot.tiles[0]
                return actv(soft[:, :], soft[:, :], ACT.Ln, [ready], bias=1.0)

            def stick_mask(slot, a_):
                soft, z = slot.tiles
                d = stt(soft[:, :], z[:, :], 0.0, soft[:, :], ALU.max, ALU.add, [a_])
                for kt in range(NT):
                    o = starts[kt]
                    dm = tt(dve, soft[:, o:o + P], soft[:, o:o + P], strict[:, 0, :], ALU.mult, [d, in_])
                    da = tt(dve, z[:, o:o + P], z[:, o:o + P], strict[:, 1, :], ALU.add, [d])
                return [dm, da]

            def stick_sums(slot, kt, ready):
                soft, z = slot.tiles
                width, o = L - kt * P, starts[kt]
                b = stick_banks.take()
                m = mm(bank(b, width), tri[:, :], soft[:, o:o + width], True, kt == 3, ready + bank_free[b], mark=True)
                for k2 in range(kt + 1, NT):
                    w2, o2 = L - k2 * P, starts[k2]
                    m = mm(bank(b, w2, (k2 - kt) * P), ones[:, :], soft[:, o2:o2 + w2], False, k2 == 3, mark=True)
                d = tt(dve, z[:, o:o + width], z[:, o:o + width], bank(b, width), ALU.subtract, [m] + ready)
                bank_free[b] = [d]
                return d

            def stick_values(h, slot, w_ready):
                p0, b = 64 * (h % 2), stick_banks.take()
                z = slot.tiles[1]
                for kt in range(NT):
                    width, o = L - kt * P, starts[kt]
                    m = mm(psum[p0:p0 + 64, b * BANK + kt * P:(b + 1) * BANK], v_c[:, kt, h * 64:(h + 1) * 64], z[:, o:o + width],
                           kt == 0, kt == 3, [w_ready] + marks["c"] + bank_free[b], mark=True)
                slot.free = [m]
                d = actv(q_c[p0:p0 + 64, h // 2, :], psum[p0:p0 + 64, b * BANK:(b + 1) * BANK], ACT.Copy, [m])
                bank_free[b] = [d]
                return d

            stick_marks = []

            def stick():
                slot, d = stick_scores(0)
                yield
                d = stick_abs(slot, d)
                yield
                d = stick_log(slot, d)
                yield
                masked_ = stick_mask(slot, d)
                yield
                for h in range(6):
                    d = stick_sums(slot, 0, masked_)
                    following = stick_scores(h + 1) if h < 5 else None
                    yield
                    for kt, make in ((1, stick_abs), (2, stick_log), (3, stick_mask)):
                        d = stick_sums(slot, kt, masked_)
                        if following:
                            following = (following[0], make(*following))
                        yield
                    w_ready = actv(slot.tiles[1][:, :], slot.tiles[1][:, :], ACT.Exp, [d])
                    yield
                    stick_marks.append(stick_values(h, slot, w_ready))
                    if following:
                        slot, masked_ = following
                    yield

            def projection():
                for c0, n in MIX_CHUNKS[2:]:
                    c = next_chunk()
                    v = [x for x in values if x[0] <= c0 < x[1]]
                    if v:
                        lo_, _, dst, name = v[0]

                        def v_sink(t_, ps, m, dst=dst, name=name, at_=c0 - lo_, n=n):
                            d = actv(dst[:, t_, at_:at_ + n], ps, ACT.Copy, [m])
                            marks[name].append(d)
                            return [d]
                        for t_ in range(NT):
                            project_tokens(c, h_hi, h_lo, [t_], ready, v_sink, proj_banks.take)
                            if t_ % 2:
                                yield c0
                    else:
                        for j in range(n // P):
                            project(c, j * P, P, h_hi, h_lo, RANGES[:1], ready, put(*feature[c0 + j * P]), proj_banks.take)
                            yield c0

            tile_marks = [[] for _ in range(NT)]

            def assemble():
                for t_ in range(NT):
                    while len(o_marks[t_]) < 10:
                        yield
                    sslot, s_ = stat()
                    ob = o_tok[:, t_, 384:640]
                    d = tt(dve, squares[:, :], ob, ob, ALU.mult, o_marks[t_] + sslot.free)
                    d = dve.op(lambda e, s_=s_: e.tensor_reduce(s_[:, 0:4], squares[:, :].rearrange("p (h c) -> p h c", h=4), AX.X, ALU.add), [d])
                    r = rsqrt(s_[:, 4:8], s_[:, 0:4], 4, 1.0 / 64, [d])
                    yield
                    ov = ob.rearrange("p (h c) -> p h c", h=4)
                    d = tt(dve, ov, ov, s_[:, 4:8].unsqueeze(2).broadcast_to([P, 4, 64]), ALU.mult, [r])
                    sslot.free = [d]
                    d = tt(dve, ov, ov, sub_g[:, :].unsqueeze(1).broadcast_to([P, 4, 64]), ALU.mult, [d, g_scaled])
                    for k0, k1 in ((0, 3), (3, 5)):
                        b, n = soft_banks.take(), k1 - k0
                        for k in range(k0, k1):
                            m = pe.op(lambda e, k=k, b=b, t_=t_, k0=k0: e.transpose(bank(b, P, (k - k0) * P), o_tok[:, t_, k * P:(k + 1) * P], ident[:, :]),
                                      o_marks[t_] + bank_free[b] + ([d] if k0 else []), mark=True)
                        pv = bank(b, n * P).rearrange("p (k n) -> p k n", k=n)
                        bank_free[b] = split_pair(main_hi[:, k0:k1, t_ * P:(t_ + 1) * P], main_lo[:, k0:k1, t_ * P:(t_ + 1) * P], pv, [m] + h_read)
                        tile_marks[t_] += bank_free[b]

            projecting, streams = projection(), []
            sticks, bands, differentials = stick(), band(), differential()
            starts_after = {0: sticks, 1152: bands, None: differentials}
            c0 = 0
            while c0 is not None:
                c0 = next(projecting, None)
                stream = starts_after.pop(c0, None)
                if stream:
                    streams.append(stream)
                for stream in streams + streams[1:2]:
                    next(stream, None)
            h_read = pe.now()
            assembling = assemble()
            live = streams
            stick_split = False
            while live:
                live = [s_ for s_ in live if next(s_, "over") != "over"]
                if len(stick_marks) == 6 and not stick_split:
                    stick_split = True
                    for i in range(3):
                        got = split_pair(main_hi[:, 5 + i, :], main_lo[:, 5 + i, :], q_c[:, i, :], stick_marks + h_read)
                        for tm in tile_marks:
                            tm.extend(got)
                next(assembling, None)
            for _ in assembling:
                pass
            for w in wide_ring.slots + work_ring.slots:
                w.free = pe.now() + dve.now() + act.now()
            new, next_ready = [None] * NT, [[] for _ in range(NT)]
            follow = follow_with("ffn2_pre_g_2", layer, new, next_ready)
            down(KT, h_hi, h_lo, [t_ * P for t_ in range(NT)], tile_marks, residual_rms(1.0, g_ready, new), follow)
            sc.close()
            return new, next_ready, follow, pe.now() + act.now() + dve.now()

        for layer in range(DEPTH):
            _, ready, follow, post_free = ffn(1, layer, ready, follow, post_free, "mix_pre_g_2", layer)
            _, ready, follow, post_free = mixing(layer, ready, follow, post_free)
            more = layer + 1 < DEPTH
            x_ready, ready, follow, post_free = ffn(2, layer, ready, follow, post_free, "ffn1_pre_g_2" if more else None, layer + 1)
        stored = [sem("stored"), 0]
        for t_ in range(NT):
            last = load(out[0, t_ * P:(t_ + 1) * P, :], X[:, t_, :], [x_ready[t_]], s=stored)
        sp.wait([last])
        second.close()

        block = ctx.enter_context(nc.Block())

        def play(engine, eng):
            for step in engine.queue:
                step(eng)

        block.sync(lambda e: play(sp, e))
        block.tensor(lambda e: play(pe, e))
        block.scalar(lambda e: play(act, e))
        block.vector(lambda e: play(dve, e))
        block.gpsimd(lambda e: play(pool, e))


def shape_constants():
    k = {}
    k["k_ident"] = np.eye(P)
    d = 2 * np.pi * (np.outer(np.arange(P), np.arange(P)) % P) / P
    k["k_dft_d"] = np.concatenate([np.cos(d), np.sin(d)], 1)
    a = 2 * np.pi * (np.outer(np.arange(L), np.arange(L)) % L) / L
    k["k_dft_l"] = np.stack([np.cos(a), -np.sin(a)], 1) / np.sqrt(L * P)
    tok = np.arange(L)
    inv = 10000.0 ** (-np.arange(0, 16, 2) / 16)
    ang = [np.outer(inv, tok // 64), np.outer(inv, tok % 64)]
    cos, sin = np.ones((QK, L)), np.zeros((QK, L))
    swap = np.zeros((QK, QK))
    for i in range(2):
        r = NOPE + 16 * i
        cos[r:r + 8] = cos[r + 8:r + 16] = np.cos(ang[i])
        sin[r:r + 8], sin[r + 8:r + 16] = -np.sin(ang[i]), np.sin(ang[i])
        for j in range(8):
            swap[r + 8 + j, r + j] = swap[r + j, r + 8 + j] = 1
    k["k_rope_cos"], k["k_rope_sin"], k["k_rope_swap"] = cos, sin, swap
    rows = []
    for w in POOL_WINDOWS:
        row = []
        for n in (L, LC):
            t = np.arange(n)
            row.append(1.0 / (np.clip(t + w - w // 2, 0, n) - np.clip(t - w // 2, 0, n)))
        rows.append(np.concatenate(row))
    k["k_inv_count"] = np.stack(rows)
    q, c = np.arange(P)[:, None], np.arange(L)[None]
    dist = -np.abs(q + L - P - c).astype(np.float64)
    dist[0:64, L - 64:] = NEG
    k["k_distance"] = dist
    s, t = np.arange(P)[:, None], np.arange(P)[None]
    k["k_strict"] = np.stack([(s < t) * 1.0, np.where(s < t, 0.0, NEG)])
    k["k_tri"] = (s >= t) * 1.0
    return {n: np.ascontiguousarray(v, dtype=np.float32) for n, v in k.items()}


def kernel(**inputs):
    import concourse.bacc as bacc
    from concourse.bass_utils import run_bass_kernel_spmd as run

    nc = bacc.Bacc("TRN2", target_bir_lowering=False, num_devices=1)
    arrays = {n: np.ascontiguousarray(v) for n, v in inputs.items()}
    arrays.update(shape_constants())
    rb = arrays["rel_bias_2"]
    flipped = np.concatenate([np.repeat(rb[:, :, 256:257], P - 1, axis=2), rb[:, :, :0:-1]], axis=2)
    idx = np.arange(256)[None] - np.arange(P)[:, None] + P - 1
    arrays["l_band_bias"] = np.ascontiguousarray(flipped[:, :, idx])
    arrays["l_far_bias"] = np.ascontiguousarray(rb[:, :, 256])
    A = {n: nc.dram_tensor(f"in_{n}", a.shape, mybir.dt.from_np(a.dtype), kind="ExternalInput").ap()
         for n, a in arrays.items()}
    out = nc.dram_tensor("out_x", (1, L, D), F32, kind="ExternalOutput").ap()
    build(nc, A, out)
    r = run(nc, [{f"in_{n}": a for n, a in arrays.items()}], core_ids=[0])
    return r.results[0]["out_x"]
```

```python
from contextlib import ExitStack
import math

import numpy as np

import concourse.bass as bass
from concourse import mybir

F32 = mybir.dt.float32
F32R = mybir.dt.float32r
ACT = mybir.ActivationFunctionType
ALU = mybir.AluOpType
AX = mybir.AxisListType

P = 128
D = 1024
KT = D // P
L = 512
LC = 256
LA = L + LC
NT = L // P
NC = LC // P
BANK = 512
EPS = 1e-6
DEPTH = 2
ALPHA = (2 * DEPTH) ** 0.25
POOL_WINDOWS = (2, 4, 8, 16)
HALO = 8
FF = 2816
FT = FF // P
NOPE, ROPE, HEADS = 64, 32, 8
QK = NOPE + ROPE
NEG = -1e30
CW = 256

VECS = [("ab_b_mod", 24), ("cd_b_mod", 24), ("c", 8), ("c_ctx", 8), ("ab_pool_scale", 4),
        ("cd_q_norm", 2), ("cd_kv_norm", 1), ("ffn1_pre_g_2", 16), ("mix_pre_g_2", 16),
        ("ffn2_pre_g_2", 16)]
VOFF = {}
for _n, _k in VECS:
    VOFF[_n] = sum(k for m, k in VECS[:[n for n, _ in VECS].index(_n)])
NVEC = sum(k for _, k in VECS)


class Engine:

    def __init__(self, sem):
        self.sem, self.count, self.queue, self.seen = sem, 0, [], {}

    def wait(self, marks):
        for sem, value in marks:
            if value > self.seen.get(id(sem), 0):
                self.seen[id(sem)] = value
                self.queue.append(lambda eng, s=sem, v=value: eng.wait_ge(s, v))

    def op(self, build, after=(), mark=True):
        self.wait(after)
        if not mark:
            self.queue.append(build)
            return None
        self.count += 1
        self.queue.append(lambda eng, b=build, s=self.sem: b(eng).then_inc(s, 1))
        return (self.sem, self.count)

    def now(self):
        return [(self.sem, self.count)] if self.count else []


class Slot:

    def __init__(self, *tiles):
        self.tiles, self.free = tiles, []


class Ring:
    def __init__(self, slots):
        self.slots, self.at = slots, 0

    def take(self):
        self.at += 1
        return self.slots[(self.at - 1) % len(self.slots)]


def build(nc, A, out):
    ctx = ExitStack()
    names = [0]

    def sem(name):
        return ctx.enter_context(nc.semaphore(name))

    def sb(scope, name, shape, dt=F32):
        names[0] += 1
        return scope.enter_context(nc.sbuf_tensor(f"{name}_{names[0]}", shape, dt))

    with ctx:
        pe, act, dve, pool = (Engine(sem(n)) for n in ("pe_done", "act_done", "dve_done", "pool_done"))
        sp = Engine(None)
        dma_sems = []

        def load(dst, src, after=(), s=None):
            if s is None:
                s = [sem(f"landed_{len(dma_sems)}"), 0]
                dma_sems.append(s)
            s[1] += 16
            sp.wait(after)
            sp.queue.append(lambda eng, s0=s[0]: eng.dma_start(dst, src).then_inc(s0, 16))
            return (s[0], s[1])

        psum = ctx.enter_context(nc.psum_tensor("psum", [P, 8 * BANK], F32))
        bank_free = {b: [] for b in range(8)}

        def bank(b, n=BANK, off=0):
            return psum[:, b * BANK + off:b * BANK + off + n]

        raw_ring = Ring([Slot(sb(ctx, "raw", [P, 2048]), [sem(f"raw_landed_{i}"), 0]) for i in range(2)])
        split_ring = Ring([Slot(sb(ctx, "w_hi", [P, 2048], F32R), sb(ctx, "w_lo", [P, 2048], F32R))
                           for _ in range(2)])
        X = sb(ctx, "X", [P, NT, D])
        main_hi = sb(ctx, "h_hi", [P, KT, L], F32R)
        main_lo = sb(ctx, "h_lo", [P, KT, L], F32R)
        cols = sb(ctx, "cols", [P, NVEC])
        ident = sb(ctx, "ident", [P, P])
        ones = sb(ctx, "ones", [P, P])
        half = sb(ctx, "minus_half", [P, 8])
        work_ring = Ring([Slot(sb(ctx, "work", [P, BANK])) for _ in range(3)])
        stat_ring = Ring([Slot(sb(ctx, "stat", [P, 20])) for _ in range(10)])

        def fence():
            marks = pe.now() + act.now() + dve.now() + pool.now()
            for e in (pe, act, dve, pool, sp):
                e.wait([m for m in marks if m[0] is not e.sem])
            for e in (act, dve, pool):
                e.wait(e.now())
            return marks

        plan = []

        def add_cols(w, c0, n, split=True):
            plan.append((w[:, c0:c0 + n].rearrange("(k p) n -> p k n", p=P), KT, n, split))

        def add_rows(w, r0):
            plan.append((w[r0:r0 + 2 * P, :].rearrange("(k p) n -> p k n", p=P), 2, D, True))

        def add_down(w, rows):
            for r in range(0, rows, 2 * P):
                add_rows(w, r)

        LATE_MOD = [("ab_w_mod", c0) for c0 in range(2 * D, 3 * D, CW)] + [("cd_w_mod", c0) for c0 in range(0, 3 * D, CW)]
        for ch in range(10):
            add_cols(A["ab_w_in"][0], ch * CW, CW)
            if ch > 5:
                w, c0 = LATE_MOD[6 + ch]
                add_cols(A[w][0], c0, CW, split=False)
        add_down(A["ab_w_out"][0], D)
        add_down(A["ab_w_out"][0], D)
        for c0, n in ((0, 256), (256, 256), (512, 256), (768, 256), (1024, 256), (1280, 160), (1440, 256), (1696, 256)):
            add_cols(A["cd_w_in"][0], c0, n)
        for c0 in (0, 256):
            plan.append((A["cd_fnet_w"][0][:, c0:c0 + 256].rearrange("(k p) n -> p k n", p=P), 4, 256, True))
        add_down(A["cd_w_out"][0], D)
        MIX_CHUNKS = [(1920, 256), (2176, 256), (2432, 256), (2688, 256), (2944, 128), (0, 256), (256, 256), (512, 256),
                      (768, 256), (1024, 128), (1152, 256), (1408, 256), (1664, 256)]
        for layer in range(DEPTH):
            for f in (1, 2):
                if f == 2:
                    for c0, n in MIX_CHUNKS:
                        add_cols(A["w_in_2"][layer], c0, n)
                    add_down(A["w_out_2"][layer], D)
                for c0 in range(0, FF, CW):
                    add_cols(A[f"ffn{f}_w_gate_2"][layer], c0, CW)
                    add_cols(A[f"ffn{f}_w_up_2"][layer], c0, CW)
                add_down(A[f"ffn{f}_w_down_2"][layer], FF)

        class Chunk:
            pass

        raws = []
        consumed = [False] * len(plan)
        at = {"prepared": 0}
        ready_chunks, in_use = [], []

        def top_up():
            while len(raws) < len(plan) and (len(raws) < 2 or consumed[len(raws) - 2]):
                src, nk, n, _ = plan[len(raws)]
                slot = raw_ring.take()
                dst = slot.tiles[0][:, 0:nk * n].rearrange("p (k n) -> p k n", k=nk)
                raws.append((slot, load(dst, src, slot.free, slot.tiles[1])))

        def prepare_chunk():
            i = at["prepared"]
            if i >= len(plan):
                return
            at["prepared"] += 1
            _, nk, n, split = plan[i]
            raw_slot, landed = raws[i]
            raw = raw_slot.tiles[0]
            c = Chunk()
            c.index, c.nk, c.n, c.split = i, nk, n, split
            w = nk * n
            if split:
                slot = split_ring.take()
                hi, lo = slot.tiles
                made_hi = act.op(lambda e: e.activation(hi[:, 0:w], raw[:, 0:w], ACT.Copy),
                                 [landed] + slot.free)
                made_lo = dve.op(lambda e: e.tensor_tensor(lo[:, 0:w], raw[:, 0:w], hi[:, 0:w].bitcast(F32),
                                                           ALU.subtract), [landed, made_hi] + slot.free)
                raw_slot.free = [made_lo]
                consumed[i] = True
                c.slot, c.ready = slot, [made_lo, made_hi]
                c.hi = hi[:, 0:w].rearrange("p (k n) -> p k n", k=nk)
                c.lo = lo[:, 0:w].rearrange("p (k n) -> p k n", k=nk)
            else:
                c.slot, c.ready = raw_slot, [landed]
                c.raw = raw[:, 0:w].rearrange("p (k n) -> p k n", k=nk)
            top_up()
            ready_chunks.append(c)

        def release(count=None):
            for c in in_use[:count]:
                c.slot.free = pe.now() if c.split else pe.now() + dve.now()
                consumed[c.index] = True
            del in_use[:count]
            top_up()

        def next_chunk(beside=False):
            if not beside:
                release()
            if not ready_chunks:
                prepare_chunk()
            c = ready_chunks.pop(0)
            in_use.append(c)
            if not beside and not ready_chunks:
                prepare_chunk()
            return c

        rot = Ring(list(range(8)))

        def take1():
            return rot.take()

        def take2():
            if rot.at % 2:
                rot.take()
            b = rot.take()
            rot.take()
            return b

        def tokens(h, k, off, n):
            return h[0][:, k, off:off + n] if off < L else h[1][:, k, off - L:off - L + n]

        def mm(o, lhsT, rhs, start, stop, after=(), mark=False):
            return pe.op(lambda e: e.matmul(o, lhsT, rhs, start=start, stop=stop, skip_group_check=True), after, mark)

        def mm3(o, st_hi, st_lo, mv_hi, mv_lo, start, stop, after=(), mark=False):
            mm(o, st_hi, mv_hi, start, False, after)
            mm(o, st_hi, mv_lo, False, False)
            return mm(o, st_lo, mv_hi, False, stop, (), mark)

        def tt(eng, o, a, b, op, after=()):
            return eng.op(lambda e: e.tensor_tensor(o, a, b, op), after)

        def ts(o, a, s1, s2, op0, op1, after=()):
            if op1 is None:
                return dve.op(lambda e: e.tensor_scalar(o, a, s1, None, op0), after)
            return dve.op(lambda e: e.tensor_scalar(o, a, s1, s2, op0, op1), after)

        def stt(o, a, s, b, op0, op1, after=()):
            return dve.op(lambda e: e.scalar_tensor_tensor(out=o, in0=a, scalar=s, in1=b, op0=op0, op1=op1), after)

        def actv(o, a, func, after=(), **kw):
            return act.op(lambda e: e.activation(o, a, func, **kw), after)

        def split_pair(hi, lo, src, after):
            made_hi = actv(hi, src, ACT.Copy, after)
            made_lo = tt(dve, lo, src, hi.bitcast(F32), ALU.subtract, [made_hi] + list(after))
            return [made_hi, made_lo]

        def work(n=BANK):
            slot = work_ring.take()
            return slot, slot.tiles[0][:, 0:n]

        def stat():
            slot = stat_ring.take()
            return slot, slot.tiles[0]

        def rsqrt(o, a, n, scale, after, weight=1.0):
            biased = ts(a, a, scale / weight ** 2, EPS / weight ** 2, ALU.mult, ALU.add, after)
            return tt(pool, o, a, half[:, 0:n], ALU.pow, [biased, made_half])

        vec_scope = ExitStack()
        vec_rows = sb(vec_scope, "vec_rows", [NVEC, P])
        vec_landed = [sem("vectors_landed"), 0]
        for name, k in VECS:
            src = A[name]
            while len(src.shape) > 1:
                src = src.rearrange("a b -> (a b)") if len(src.shape) == 2 else src.rearrange("a b c -> (a b c)")
            vecs_in = load(vec_rows[VOFF[name]:VOFF[name] + k, :], src.rearrange("(k p) -> k p", p=P), s=vec_landed)
        ident_in = load(ident[:, :], A["k_ident"])
        made_ones = pool.op(lambda e: e.memset(ones[:, :], 1.0))
        made_half = pool.op(lambda e: e.memset(half[:, :], -0.5))
        t = pe.op(lambda e: e.transpose(bank(0, NVEC), vec_rows[:, :], ident[0:NVEC, 0:NVEC]),
                  [vecs_in, ident_in])
        cols_in = dve.op(lambda e: e.tensor_copy(cols[:, :], bank(0, NVEC)), [t])
        bank_free[0] = [cols_in]
        vec_done = fence()
        vec_scope.close()

        def col(name, k, n=1):
            return cols[:, VOFF[name] + k:VOFF[name] + k + n]

        first = ExitStack()
        silu_c = sb(first, "silu_c", [P, KT, 2])
        mod = sb(first, "mod", [P, 24, 2])
        mod_cd = sb(first, "mod_odd", [P, 24, 2])
        scale1 = sb(first, "one_plus_scale", [P, KT, 2])
        gate_rows = sb(first, "gate_rows", [P, 2, D])

        mod_row_ring = Ring([Slot(sb(first, "mod_row", [2, CW])) for _ in range(2)])

        def mod_product(w, wait):
            b = take1()
            for k in range(KT):
                m = mm(psum[0:2, b * BANK:b * BANK + CW], silu_c[:, k, :], w[:, k, :], k == 0, k == KT - 1,
                       wait + silu_ready + bank_free[b], mark=k == KT - 1)
            slot = mod_row_ring.take()
            row = slot.tiles[0]
            d = actv(row[:, :], psum[0:2, b * BANK:b * BANK + CW], ACT.Copy, [m] + slot.free)
            bank_free[b] = [d]
            return slot, row, d, m

        def mod_turn(product, mod, bias_name, ch):
            slot, row, d, _ = product
            b = take1()
            for j in range(2):
                m = pe.op(lambda e, j=j: e.transpose(bank(b, 2, 2 * j), row[:, j * P:(j + 1) * P], ident[0:2, 0:2]),
                          [d] + bank_free[b], mark=True)
            slot.free = [m]
            d = tt(dve, mod[:, 2 * ch:2 * ch + 2, :], bank(b, 4).rearrange("p (j s) -> p j s", s=2),
                   col(bias_name, 2 * ch, 2).unsqueeze(2).broadcast_to([P, 2, 2]), ALU.add, [m])
            bank_free[b] = [d]
            return d

        open_gates = []

        def gate_diags(s, h, after, mod):
            slot, diags = work()
            for j in range(4):
                d = ts(diags[:, j * P:(j + 1) * P], ident[:, :], mod[:, 16 + 4 * h + j, s:s + 1], None, ALU.mult, None, list(after) + slot.free)
            open_gates.append((slot, diags, s, h, d))

        def gate_row():
            slot, diags, s, h, d = open_gates.pop()
            b = take1()
            m = mm(bank(b), ones[:, :], diags, True, True, [d, made_ones] + bank_free[b], mark=True)
            slot.free = [m]
            g = actv(gate_rows[:, s, h * BANK:(h + 1) * BANK], bank(b), ACT.Copy, [m])
            bank_free[b] = [g]
            gates_ready.append(g)

        def turn(src, dst_hi, dst_lo, off, scale, shift, after, banks=None):
            halves = []
            for h in range(2):
                b = banks[h] if banks else take1()
                for k in range(4):
                    m = pe.op(lambda e, k=k, h=h, b=b: e.transpose(bank(b, P, k * P), src[:, (4 * h + k) * P:(4 * h + k + 1) * P],
                                                                  ident[:, :]), list(after) + bank_free[b], mark=k == 3)
                slot, w = work()
                wv = w.rearrange("p (k n) -> p k n", k=4)
                pv = bank(b).rearrange("p (k n) -> p k n", k=4)
                if h == 0:
                    for k in range(4):
                        d = actv(wv[:, k, :], pv[:, k, :], ACT.Identity, [m] + slot.free, scale=scale[:, k:k + 1], bias=shift[:, k:k + 1])
                    bank_free[b] = [d]
                else:
                    d = tt(dve, wv, pv, scale[:, 4:8].unsqueeze(2).broadcast_to([P, 4, P]), ALU.mult, [m] + slot.free)
                    bank_free[b] = [d]
                    d = tt(dve, wv, wv, shift[:, 4:8].unsqueeze(2).broadcast_to([P, 4, P]), ALU.add, [d])
                halves.append((slot, wv, d, slice(4 * h, 4 * h + 4)))
            his = [actv(tokens(dst_hi, ks, off, P), wv, ACT.Copy, [d]) for _, wv, d, ks in halves]
            marks = []
            for (slot, wv, d, ks), made_hi in zip(halves, his):
                made_lo = tt(dve, tokens(dst_lo, ks, off, P), wv, tokens(dst_hi, ks, off, P).bitcast(F32), ALU.subtract, [made_hi, d])
                slot.free = [made_hi, made_lo]
                marks += slot.free
            return marks

        def project(c, j, n, hi, lo, ranges, ready, sink, take=take1):
            for r, (off, width) in enumerate(ranges):
                b = take()
                for k in range(KT):
                    m = mm3(psum[0:n, b * BANK:b * BANK + width], c.hi[:, k, j:j + n], c.lo[:, k, j:j + n],
                            tokens(hi, k, off, width), tokens(lo, k, off, width), k == 0, k == KT - 1,
                            c.ready + list(ready) + bank_free[b], mark=k == KT - 1)
                bank_free[b] = sink(r, psum[0:n, b * BANK:b * BANK + width], m)

        def project_tokens(c, hi, lo, tiles, ready, sink, take=take1):
            for t_ in tiles:
                b = take()
                for k in range(KT):
                    m = mm3(bank(b, c.n), tokens(hi, k, t_ * P, P), tokens(lo, k, t_ * P, P),
                            c.hi[:, k, :], c.lo[:, k, :], k == 0, k == KT - 1,
                            c.ready + list(ready) + bank_free[b], mark=k == KT - 1)
                bank_free[b] = sink(t_, bank(b, c.n), m)

        def down(nk, hi, lo, offs, ready, sink, follow=None, between=None):
            def part(c, ch, i, mark):
                for h in range(2):
                    b = 2 * i + h
                    for kk in range(2):
                        k = 2 * ch + kk
                        m = mm3(bank(b), tokens(hi, k, offs[i], P), tokens(lo, k, offs[i], P),
                                c.hi[:, kk, h * BANK:(h + 1) * BANK], c.lo[:, kk, h * BANK:(h + 1) * BANK],
                                k == 0, k == nk - 1, c.ready + list(ready(i, k)) + bank_free[b],
                                mark=mark and h == 1 and kk == 1)
                return m
            chunks, n = nk // 2, len(offs)
            for ch in range(chunks - 2):
                c = next_chunk()
                for i in range(n):
                    part(c, ch, i, ch < 1 or i == n - 1)
                if between:
                    between(ch)
            pair = [next_chunk(), next_chunk(beside=True)]
            part(pair[0], chunks - 2, 0, False)
            for i in range(n):
                if i == 0:
                    part(pair[0], chunks - 2, 1, n == 2)
                elif i > 1:
                    part(pair[0], chunks - 2, i, i == n - 1)
                if i == n - 1:
                    release(1)
                if i > 1 and follow:
                    follow(i - 2)
                if i == n - 1:
                    prepare_chunk()
                m = part(pair[1], chunks - 1, i, True)
                bank_free[2 * i] = bank_free[2 * i + 1] = sink(i, psum[:, 2 * i * BANK:(2 * i + 2) * BANK], m)
            release()
            prepare_chunk()
            rot.at = 0

        def residual_layer_norm(dst, y, grow, g_row, b_row, after):
            done = []
            for h in range(2):
                slot, w = work()
                sl = slice(h * BANK, (h + 1) * BANK)
                m = tt(dve, w, y[:, sl], grow[:, sl], ALU.mult, list(after) + slot.free)
                done.append(m)
                m = stt(dst[:, sl], dst[:, sl], ALPHA, w, ALU.mult, ALU.add, [m])
                slot.free = [m]
            slot, s_ = stat()
            for h in range(2):
                st_m = dve.op(lambda e, h=h: e.bn_stats(s_[:, 6 * h:6 * h + 6], dst[:, h * BANK:(h + 1) * BANK]), [m] + slot.free)
            agg = dve.op(lambda e: e.bn_aggr(s_[:, 12:14], s_[:, 0:12]), [st_m])
            r = rsqrt(s_[:, 14:15], s_[:, 13:14], 1, 1.0, [agg])
            nb = stt(s_[:, 15:16], s_[:, 12:13], -1.0, s_[:, 14:15], ALU.mult, ALU.mult, [r, agg])
            n = actv(dst, dst, ACT.Identity, [r, nb], scale=s_[:, 14:15], bias=s_[:, 15:16])
            slot.free = [n]
            g = tt(dve, dst, dst, g_row, ALU.mult, [n] + rows_ready)
            return done, tt(pool, dst, dst, b_row, ALU.add, [g] + rows_ready)

        ctx_scope, ab = ExitStack(), ExitStack()
        h_hi = (main_hi, sb(first, "ctx_hi", [P, KT, LC], F32R))
        h_lo = (main_lo, sb(first, "ctx_lo", [P, KT, LC], F32R))
        CTX = sb(ctx_scope, "CTX", [P, NC, D])
        mod_scope = ExitStack()
        mod_ring = Ring([Slot(sb(mod_scope, "mod_w", [P, KT, CW]), [sem(f"mod_w_landed_{i}"), 0]) for i in range(6)])
        mod_plan = [("ab_w_mod", c0) for c0 in range(0, 2 * D, CW)]
        mod_loads = []

        def load_mod():
            if mod_plan:
                w, c0 = mod_plan.pop(0)
                slot = mod_ring.take()
                src = A[w][0][:, c0:c0 + CW].rearrange("(k p) n -> p k n", p=P)
                mod_loads.append((slot, load(slot.tiles[0][:, :, :], src, slot.free + vec_done, slot.tiles[1])))

        for _ in range(6):
            load_mod()
        x_in = load(X[:, :, :], A["x"][0].rearrange("(t p) d -> p t d", p=P))
        ctx_in = load(CTX[:, :, :], A["ctx"][0].rearrange("(t p) d -> p t d", p=P))
        top_up()
        for s, name in enumerate(("c", "c_ctx")):
            silu_ready = [actv(silu_c[:, :, s], col(name, 0, 8), ACT.Silu, [cols_in])]
        product = None
        for ch in range(8):
            slot, landed = mod_loads.pop(0)
            before, product = product, mod_product(slot.tiles[0], [landed])
            slot.free = [product[3]]
            load_mod()
            if before:
                mod_turn(before, mod, "ab_b_mod", ch - 1)
        mod_ready = [mod_turn(product, mod, "ab_b_mod", 7)]
        mod_ready.append(ts(scale1[:, :, :], mod[:, 8:16, :], 1.0, None, ALU.add, None, mod_ready))
        h_ready = [[], []]
        for t_ in range(NT):
            h_ready[0] += turn(X[:, t_, :], h_hi, h_lo, t_ * P, scale1[:, :, 0], mod[:, 0:8, 0], [x_in] + mod_ready)
        mod_scope_done = fence()
        mod_scope.close()
        pooled_in = sb(ab, "pool_in", [P, 4, HALO * 3 + LA])
        silu_ga = sb(ab, "silu_ga", [P, 4, LA])
        u_gated = sb(ab, "u_gated", [P, 4, LA])
        v_norm = sb(ab, "v_norm", [P, 6, BANK])
        pool_w = sb(ab, "pool_w", [P, 4, P])
        sgu_w = v_norm[:, 5, :].rearrange("p (h j) -> p h j", h=4)
        sgu_wT = sb(ab, "sgu_wT", [P, 4, P])
        sgu_b = sb(ab, "sgu_b", [1, 4 * P])
        RANGES = ((0, L), (L, LC))
        PAD_OFF = (HALO, 2 * HALO + L)
        pool_w_in = load(pool_w[:, :, :], A["ab_pool_w"][0].rearrange("g c d -> c g d"), mod_scope_done)
        sgu_w_in = load(sgu_w[:, :, :], A["ab_sgu_w"][0].rearrange("h i j -> i h j"))
        sgu_b_in = load(sgu_b[:, :], A["ab_sgu_b"].rearrange("a h i -> a (h i)"))
        zeroed = pool.op(lambda e: e.memset(pooled_in[:, :, :], 0.0))

        a_marks, ga_marks, u_marks, v_marks = [], [], [], []
        sums = sb(ab, "window_sums", [P, 2, LA + 3 * HALO])
        inv_cnt = sb(ab, "inv_count", [P, LA])
        cnt_sem = [sem("inv_count_landed"), 0]
        pooled = []

        def pool_group(g, w):
            cnt_in = load(inv_cnt[:, :], A["k_inv_count"][g].partition_broadcast(P), pooled[-1:], s=cnt_sem)
            src, width, m = pooled_in[:, g, :], LA + 3 * HALO, a_marks + pooled[-1:]
            span, side = 1, 0
            while span < w:
                width -= span
                dst = sums[:, side, :]
                m = [tt(pool, dst[:, 0:width], src[:, 0:width], src[:, span:span + width], ALU.add, m)]
                src, side, span = dst, 1 - side, 2 * span
            for r, (off, n) in enumerate(RANGES):
                o, a = PAD_OFF[r] - w // 2, pooled_in[:, g, PAD_OFF[r]:PAD_OFF[r] + n]
                d = tt(pool, src[:, o:o + n], src[:, o:o + n], inv_cnt[:, off:off + n], ALU.mult, m + [cnt_in])
                d = tt(pool, a, src[:, o:o + n], a, ALU.subtract, [d])
                m = m + [d]
            pooled.append(d)

        late = [("ab_b_mod", mod, 8 + i) for i in range(4)] + [("cd_b_mod", mod_cd, i) for i in range(12)]
        sink_ch0, gates_ready = [], []
        open_product = []
        turned_mods = []

        def close_product():
            if open_product:
                product, (name, dst, ch) = open_product.pop()
                turned_mods.append(mod_turn(product, dst, name, ch))

        late_slots = [Slot(t[:, 0:n, :].rearrange("p a b -> p (a b)")[:, 0:KT * CW], [sem(f"late_mod_landed_{i}"), 0])
                      for i, (t, n) in enumerate(((u_gated, 3), (v_norm, 4)))]
        late_slots = [late_slots[i % 2] for i in range(8)] + late_slots[1:] * 4
        for slot in late_slots[0:2]:
            slot.free = mod_scope_done
        late_loads, late_full = [], []

        def load_late():
            n = len(late_loads)
            if n < len(late_slots) and late_slots[n] not in late_full:
                late_full.append(late_slots[n])
                w, c0 = LATE_MOD[n]
                slot = late_slots[n]
                dst = slot.tiles[0].rearrange("p (k n) -> p k n", n=CW)
                src = A[w][0][:, c0:c0 + CW].rearrange("(k p) n -> p k n", p=P)
                late_loads.append((slot, dst, load(dst, src, slot.free, slot.tiles[1])))

        def late_product(n):
            slot, dst, landed = late_loads[n]
            product = mod_product(dst, [landed])
            slot.free = [product[3]]
            late_full.remove(slot)
            close_product()
            open_product.append((product, late.pop(0)))
            load_late()

        load_late()
        load_late()
        for ch in range(10):
            if ch > 6:
                c = next_chunk()
                product = mod_product(c.raw, c.ready)
                close_product()
                open_product.append((product, late.pop(0)))
            if ch == 1:
                for h in range(4):
                    m = pe.op(lambda e, h=h: e.transpose(bank(7, P, h * P), sgu_w[:, h, :], ident[:, :]), [sgu_w_in] + bank_free[7], mark=h == 3)
                sgu_w_ready = dve.op(lambda e: e.tensor_copy(sgu_wT[:, :, :].rearrange("p h i -> p (h i)"), bank(7)), [m])
                bank_free[7] = [sgu_w_ready]
            if 2 <= ch < 6:
                pool_group(ch - 2, POOL_WINDOWS[ch - 2])
            if 4 <= ch < 8:
                gate_diags(*divmod(ch - 4, 2), turned_mods[3:4], mod)
            c = next_chunk()
            if ch in (6, 7):
                def v_sink(t_, ps, m, ch=ch):
                    slot, s_ = stat()
                    for j in range(2):
                        o = 10 * j
                        a = dve.op(lambda e, j=j, o=o: e.bn_stats(s_[:, o:o + 6], ps[:, j * P:(j + 1) * P]), [m] + slot.free)
                        a = dve.op(lambda e, o=o: e.bn_aggr(s_[:, o + 6:o + 8], s_[:, o:o + 6]), [a])
                        r = rsqrt(s_[:, o + 8:o + 9], s_[:, o + 7:o + 8], 1, 1.0, [a])
                        hd = 2 * (ch - 6) + j
                        d = ts(v_norm[:, t_, hd * P:(hd + 1) * P], ps[:, j * P:(j + 1) * P], s_[:, o + 6:o + 7],
                               s_[:, o + 8:o + 9], ALU.subtract, ALU.mult, [r, a])
                    slot.free = [d]
                    v_marks.append(d)
                    return [d]
                project_tokens(c, h_hi, h_lo, range(6), h_ready[0] + h_ready[1], v_sink)
                close_product()
                gate_row()
                continue
            for j in range(2):
                g = 2 * (ch % 2) + j
                if ch < 2:
                    def sink(r, ps, m, g=g):
                        d = actv(pooled_in[:, g, PAD_OFF[r]:PAD_OFF[r] + RANGES[r][1]], ps, ACT.Copy, [m, zeroed])
                        a_marks.append(d)
                        return [d]
                elif ch < 4:
                    def sink(r, ps, m, g=g):
                        o, n = RANGES[r]
                        d = actv(silu_ga[:, g, o:o + n], ps, ACT.Silu, [m])
                        ga_marks.append(d)
                        return [d]
                elif ch < 6:
                    def sink(r, ps, m, g=g):
                        o, n = RANGES[r]
                        d = actv(u_gated[:, g, o:o + n], ps, ACT.Copy, [m])
                        u_marks.append(d)
                        return [d]
                else:
                    def sink(r, ps, m, g=g):
                        o, n = RANGES[r]
                        slot, w = work(n)
                        s_ = actv(w, ps, ACT.Silu, [m] + slot.free)
                        d = tt(dve, u_gated[:, g, o:o + n], u_gated[:, g, o:o + n], w, ALU.mult, [s_] + u_marks)
                        slot.free = [d]
                        u_marks.append(d)
                        return [s_]
                if ch == 0:
                    sink_ch0.append(sink)
                project(c, j * P, P, h_hi, h_lo, RANGES[:1], h_ready[0], sink)
                if ch < 6:
                    late_product(2 * ch + j)
                if ch == j == 0:
                    for c_ in range(NC):
                        h_ready[1] += turn(CTX[:, c_, :], h_hi, h_lo, L + c_ * P, scale1[:, :, 1], mod[:, 0:8, 1], [ctx_in] + mod_ready)
                    continue
                if ch == 0:
                    project(c, 0, P, h_hi, h_lo, RANGES[1:], h_ready[1], lambda r, ps, m: sink_ch0[0](1, ps, m))
                project(c, j * P, P, h_hi, h_lo, RANGES[1:], h_ready[1], lambda r, ps, m, sink=sink: sink(1, ps, m))
                close_product()
                if open_gates:
                    gate_row()
        c = next_chunk()
        open_product.append((mod_product(c.raw, c.ready), late.pop(0)))
        close_product()
        odd_ready = turned_mods[-1:]

        h_read = pe.now()
        mix_marks = [[] for _ in range(KT)]
        for g in range(4):
            for r, (off, n) in enumerate(RANGES):
                b = take1()
                q = mm(bank(b, n), pool_w[:, g, :], pooled_in[:, g, PAD_OFF[r]:PAD_OFF[r] + n], True, True,
                       [pooled[g], pool_w_in] + bank_free[b], mark=True)
                slot, wk = work(n)
                d = stt(wk, bank(b, n), col("ab_pool_scale", g), silu_ga[:, g, off:off + n], ALU.mult, ALU.mult, [q] + ga_marks + slot.free)
                bank_free[b] = [d]
                slot.free = split_pair(tokens(h_hi, g, off, n), tokens(h_lo, g, off, n), wk, [d] + h_read)
                mix_marks[g] += slot.free
        for hd in range(4):
            for r, (off, n) in enumerate(RANGES):
                b = take1()
                for q in range(n // P):
                    ck = off // P + q
                    mm(bank(b, P, q * P), v_norm[:, ck, hd * P:(hd + 1) * P], sgu_wT[:, hd, :], True, False,
                       v_marks + [sgu_w_ready] + bank_free[b])
                    m = mm(bank(b, P, q * P), ones[0:1, :], sgu_b[0:1, hd * P:(hd + 1) * P], False, True, [sgu_b_in], mark=True)
                slot, wk = work(n)
                d = tt(dve, wk, bank(b, n), u_gated[:, hd, off:off + n], ALU.mult, [m] + u_marks + slot.free)
                bank_free[b] = [d]
                slot.free = split_pair(tokens(h_hi, 4 + hd, off, n), tokens(h_lo, 4 + hd, off, n), wk, [d] + h_read)
                mix_marks[4 + hd] += slot.free
        fence()
        ab.close()

        tail = ExitStack()
        g_row = sb(tail, "g_row", [P, D])
        b_row = sb(tail, "b_row", [P, D])
        row_sems = [[sem("g_row_landed"), 0], [sem("b_row_landed"), 0]]
        rows_ready = [load(g_row[:, :], A["ab_ln_g"][0].partition_broadcast(P), pe.now() + dve.now() + act.now(), s=row_sems[0]),
                      load(b_row[:, :], A["ab_ln_b"][0].partition_broadcast(P), s=row_sems[1])]
        x_marks, c_marks = [], []

        def x_sink(i, y, m):
            done, ready = residual_layer_norm(X[:, i, :], y, gate_rows[:, 0, :], g_row[:, :], b_row[:, :], [m] + gates_ready)
            x_marks.append(ready)
            return done

        scale_odd = sb(tail, "one_plus_scale_odd", [P, KT, 2])
        odd_ready.append(ts(scale_odd[:, :, :], mod_cd[:, 8:16, :], 1.0, None, ALU.add, None, odd_ready))
        h_ready = []

        def x_follow(i):
            h_ready.extend(turn(X[:, i, :], h_hi, h_lo, i * P, scale_odd[:, :, 0], mod_cd[:, 0:8, 0],
                                [x_marks[i]] + odd_ready, (2 * i, 2 * i + 1)))

        def c_follow(i):
            h_ready.extend(turn(CTX[:, i, :], h_hi, h_lo, L + i * P, scale_odd[:, :, 1], mod_cd[:, 0:8, 1],
                                [c_marks[i]] + odd_ready, (2 * i, 2 * i + 1)))

        def c_sink(i, y, m):
            done, ready = residual_layer_norm(CTX[:, i, :], y, gate_rows[:, 1, :], g_row[:, :], b_row[:, :], [m] + gates_ready)
            c_marks.append(ready)
            return done

        down(KT, h_hi, h_lo, [t_ * P for t_ in range(NT)], lambda i, k: mix_marks[k], x_sink, x_follow)
        down(KT, h_hi, h_lo, [L + t_ * P for t_ in range(NC)], lambda i, k: mix_marks[k], c_sink, between=lambda ch: x_follow(2 + ch))
        gates_ready = []
        x_done = list(x_marks)
        c_follow(0)
        c_follow(1)
        fence()
        tail.close()

        ctx_scope.close()
        cd = ExitStack()
        silu_dg = sb(cd, "silu_dgate", [P, 4, L])
        cqT = sb(cd, "cqT", [P, 2, L])
        ckvT = sb(cd, "ckvT", [P, LA])
        krT = sb(cd, "krT", [P, LA])
        q_up = sb(cd, "q_up", [P, 2, HEADS * QK])
        kv_up = sb(cd, "kv_up", [P, D])
        rope_c = sb(cd, "rope_cos", [QK, L])
        rope_s = sb(cd, "rope_sin", [QK, L])
        swap = sb(cd, "rope_swap", [QK, QK])
        fourier = ExitStack()
        f_in = sb(fourier, "f_in", [P, 4, L])
        silu_fg = sb(fourier, "silu_fgate", [P, 4, L])
        dft_d = sb(fourier, "dft_d", [P, 2 * P])
        dft_l = sb(fourier, "dft_l", [P, 4, 2, L])
        cs_ring = Ring([Slot(sb(fourier, "f_cs", [P, NT, 2 * P])) for _ in range(2)])
        spec_hi, spec_lo = main_hi[:, 4:8, :], main_lo[:, 4:8, :]
        dft_in = [load(dft_d[:, :], A["k_dft_d"], pe.now() + dve.now() + act.now()), load(dft_l[:, :, :, :], A["k_dft_l"].rearrange("(t p) s l -> p t s l", p=P))]
        f_marks, fg_marks, dg_marks, lat_marks = [], [], [], []
        mla_in = [load(q_up[:, :, :], A["cd_w_q_up"][0].rearrange("(k p) n -> p k n", p=P), pe.now() + dve.now() + act.now()),
                  load(kv_up[:, :], A["cd_w_kv_up"][0]), load(rope_c[:, :], A["k_rope_cos"]),
                  load(rope_s[:, :], A["k_rope_sin"]), load(swap[:, :], A["k_rope_swap"])]

        def rope(t_, after):
            b = take1()
            o = psum[0:QK, b * BANK:(b + 1) * BANK]
            m = mm(o, swap[:, :], t_[0:QK, 0:L], True, True, list(after) + mla_in + bank_free[b], mark=True)
            slot, w = work()
            d = tt(dve, w[0:QK, :], o, rope_s[:, :], ALU.mult, [m] + slot.free)
            bank_free[b] = [d]
            d2 = tt(dve, t_[0:QK, 0:L], t_[0:QK, 0:L], rope_c[:, :], ALU.mult, [m])
            d = tt(dve, t_[0:QK, 0:L], t_[0:QK, 0:L], w[0:QK, :], ALU.add, [d, d2])
            slot.free = [d]
            return d

        behind = []

        def turn_behind(turn_next=None):
            if behind:
                behind.pop()()
            if turn_next:
                behind.append(turn_next)

        for ch in range(8):
            c = next_chunk()
            if ch == 4:
                def q_sink(t_, ps, m):
                    slot, s_ = stat()
                    ws, w = work(256)
                    sq = actv(w, ps, ACT.Square, [m] + slot.free + ws.free, accum_out=s_[:, 0:1])
                    r = rsqrt(s_[:, 1:2], s_[:, 0:1], 1, 1.0 / 256, [sq])
                    d = ts(w, ps, s_[:, 1:2], None, ALU.mult, None, [r, sq])
                    slot.free = [d]

                    def turn_q():
                        b = take1()
                        for k in range(2):
                            q = pe.op(lambda e, k=k: e.transpose(bank(b, P, k * P), w[:, k * P:(k + 1) * P], ident[:, :]),
                                      [d] + bank_free[b], mark=True)
                        ws.free = [q]
                        for k in range(2):
                            d2 = ts(cqT[:, k, t_ * P:(t_ + 1) * P], bank(b, P, k * P), col("cd_q_norm", k), None, ALU.mult, None, [q])
                        bank_free[b] = [d2]
                        lat_marks.append(d2)
                    turn_behind(turn_q)
                    return [d]
                project_tokens(c, h_hi, h_lo, range(NT), h_ready, q_sink)
                continue
            if ch == 5:
                def kv_sink(t_, ps, m):
                    slot, s_ = stat()
                    ws, w = work(160)
                    sq = actv(w[:, 0:P], ps[:, 0:P], ACT.Square, [m] + slot.free + ws.free, accum_out=s_[:, 0:1])
                    r = rsqrt(s_[:, 1:2], s_[:, 0:1], 1, 1.0 / P, [sq])
                    d = ts(w[:, 0:P], ps[:, 0:P], s_[:, 1:2], None, ALU.mult, None, [r, sq])
                    d3 = dve.op(lambda e: e.tensor_copy(w[:, P:160], ps[:, P:160]), [m])
                    slot.free = [d]

                    def turn_kv():
                        b = take1()
                        pe.op(lambda e: e.transpose(bank(b, P), w[:, 0:P], ident[:, :]), [d, d3] + bank_free[b], mark=False)
                        q = pe.op(lambda e: e.transpose(psum[0:QK, b * BANK + P:b * BANK + 2 * P], w[:, 64:160], ident[:, :]))
                        ws.free = [q]
                        d2 = ts(ckvT[:, t_ * P:(t_ + 1) * P], bank(b, P), col("cd_kv_norm", 0), None, ALU.mult, None, [q])
                        d4 = dve.op(lambda e: e.tensor_copy(krT[0:QK, t_ * P:(t_ + 1) * P], psum[0:QK, b * BANK + P:b * BANK + 2 * P]), [q])
                        bank_free[b] = [d4]
                        lat_marks.extend([d2, d4])
                    turn_behind(turn_kv)
                    return [d3]
                project_tokens(c, h_hi, h_lo, range(6), h_ready, kv_sink)
                continue
            for j in range(2):
                g = 2 * (ch % 2) + j

                def sink(r, ps, m, g=g, ch=ch):
                    if ch < 2:
                        d = actv(f_in[:, g, :], ps, ACT.Copy, [m])
                        f_marks.append(d)
                    elif ch < 4:
                        d = actv(silu_fg[:, g, :], ps, ACT.Silu, [m])
                        fg_marks.append(d)
                    else:
                        d = actv(silu_dg[:, g, :], ps, ACT.Silu, [m])
                        dg_marks.append(d)
                    return [d]
                if ch == 1:
                    gate_diags(0, j, odd_ready + x_done, mod_cd)
                project(c, j * P, P, h_hi, h_lo, RANGES[:1], h_ready, sink)
                turn_behind()
                if ch == 1:
                    gate_row()
        h_read = pe.now()
        kr_ready = rope(krT, lat_marks)

        mix_marks, spec_marks = [[] for _ in range(4)], []
        attn_marks = [[] for _ in range(NT)]

        def over_features(hd):
            slot = cs_ring.take()
            marks = []
            for t_ in range(NT):
                b = take1()
                m = mm(bank(b, 256), f_in[:, hd, t_ * P:(t_ + 1) * P], dft_d[:, :], True, True, f_marks + dft_in + bank_free[b], mark=True)
                d = actv(slot.tiles[0][:, t_, :], bank(b, 256), ACT.Copy, [m] + slot.free)
                bank_free[b] = [d]
                marks.append(d)
            return slot, marks

        following = over_features(0)
        for hd in range(4):
            slot, cs_marks = following
            if hd < 3:
                following = over_features(hd + 1)
            f_cs = slot.tiles[0]
            b = take1()
            for t_ in range(NT):
                for s in range(2):
                    m = mm(bank(b), f_cs[:, t_, s * P:(s + 1) * P], dft_l[:, t_, s, :], t_ == 0 and s == 0, t_ == 3 and s == 1,
                           cs_marks + bank_free[b], mark=True)
            slot.free = [m]
            bank_free[b] = split_pair(spec_hi[:, hd, :], spec_lo[:, hd, :], bank(b), [m] + h_read)
            spec_marks += bank_free[b]
        for ch in range(2):
            c = next_chunk()
            for j in range(2):
                b = take1()
                for k in range(4):
                    m = mm3(bank(b), c.hi[:, k, j * P:(j + 1) * P], c.lo[:, k, j * P:(j + 1) * P], spec_hi[:, k, :], spec_lo[:, k, :],
                            k == 0, k == 3, c.ready + spec_marks + bank_free[b], mark=k == 3)
                g = 2 * ch + j
                slot, w = work()
                d = tt(dve, w, bank(b), silu_fg[:, g, :], ALU.mult, [m] + fg_marks + slot.free)
                bank_free[b] = [d]
                slot.free = split_pair(main_hi[:, g, :], main_lo[:, g, :], w, [d] + h_read)
                mix_marks[g] += slot.free
        f = fence()
        fourier.close()

        mla = ExitStack()
        v_all = sb(mla, "v_all", [P, 6, HEADS * 64])
        head_ring = Ring([Slot(sb(mla, "kT_head", [QK, LA]), sb(mla, "qT_head", [QK, L])) for _ in range(2)])
        p_ring = Ring([Slot(sb(mla, "probs", [P, LA])) for _ in range(2)])
        pT_ring = Ring([Slot(sb(mla, "probsT", [P, LA])) for _ in range(2)])
        o_tok = sb(mla, "o_tok", [P, NT, HEADS * 64])
        v_marks = []
        v_cols = kv_up[:, :].rearrange("p (h c) -> p h c", h=HEADS)[:, :, NOPE:P]
        for t_ in range(6):
            b = take1()
            m = mm(bank(b).rearrange("p (h c) -> p h c", h=HEADS), ckvT[:, t_ * P:(t_ + 1) * P], v_cols, True, True,
                   lat_marks + mla_in + bank_free[b], mark=True)
            d = actv(v_all[:, t_, :], bank(b), ACT.Copy, [m])
            bank_free[b] = [d]
            v_marks.append(d)
        SC = QK ** -0.5
        o_marks = []

        def head_keys(hd):
            slot = head_ring.take()
            kT, qT = slot.tiles
            for off, n in RANGES:
                b = take1()
                m = mm(psum[0:NOPE, b * BANK:b * BANK + n], kv_up[:, hd * P:hd * P + NOPE], ckvT[:, off:off + n], True, True,
                       lat_marks + mla_in + bank_free[b], mark=True)
                k_up = actv(kT[0:NOPE, off:off + n], psum[0:NOPE, b * BANK:b * BANK + n], ACT.Copy, [m] + slot.free)
                bank_free[b] = [k_up]
            heads[hd] = [slot, kT, qT, [k_up] + shared_keys]

        def head_queries(hd):
            slot, _, qT, ready = heads[hd]
            b = take1()
            for k in range(2):
                m = mm(psum[0:QK, b * BANK:(b + 1) * BANK], q_up[:, k, hd * QK:(hd + 1) * QK], cqT[:, k, :], k == 0, k == 1,
                       bank_free[b], mark=True)
            q = actv(qT[:, :], psum[0:QK, b * BANK:(b + 1) * BANK], ACT.Copy, [m] + slot.free)
            bank_free[b] = [q]
            ready.append(q)

        def head_rope(hd):
            heads[hd][3].append(rope(heads[hd][2], heads[hd][3][-1:]))

        heads = {}
        shared_keys = [actv(slot.tiles[0][NOPE:QK, :], krT[NOPE:QK, :], ACT.Copy, [kr_ready] + lat_marks) for slot in head_ring.slots]
        beside = {0: head_keys, 1: head_queries, 2: head_rope}
        for make in beside.values():
            make(0)

        def mla_scores(hd, t_):
            slot, kT, qT, ready = heads[hd]
            b = take2()
            for j, (off, n) in enumerate(RANGES):
                m = mm(bank(b + j, n), qT[:, t_ * P:(t_ + 1) * P], kT[:, off:off + n], True, True, ready + bank_free[b + j], mark=True)
            if t_ == NT - 1:
                slot.free = [m]
            s = psum[:, b * BANK:b * BANK + LA]
            sslot, s_ = stat()
            mx = dve.op(lambda e: e.tensor_reduce(s_[:, 0:1], s, AX.X, ALU.max), [m] + sslot.free)
            nm = ts(s_[:, 1:2], s_[:, 0:1], -SC, None, ALU.mult, None, [mx])
            ps = p_ring.take()
            pr = ps.tiles[0]
            ex = actv(pr[:, :], s, ACT.Exp, [nm] + ps.free, bias=s_[:, 1:2], scale=SC, accum_out=s_[:, 2:3])
            bank_free[b] = bank_free[b + 1] = [ex]
            return ps, pr, sslot, s_, ex

        def mla_turn(it):
            ps, pr, sslot, s_, ex = it
            b = take2()
            for k in range(6):
                bb = b + k // 4
                m = pe.op(lambda e, k=k, bb=bb: e.transpose(bank(bb, P, (k % 4) * P), pr[:, k * P:(k + 1) * P], ident[:, :]),
                          [ex] + bank_free[bb], mark=True)
            ps.free = [m]
            pt = pT_ring.take()
            c1 = actv(pt.tiles[0][:, 0:BANK], bank(b), ACT.Copy, [m] + pt.free)
            c2 = dve.op(lambda e: e.tensor_copy(pt.tiles[0][:, BANK:LA], bank(b + 1, LA - BANK)), [m] + pt.free)
            bank_free[b], bank_free[b + 1] = [c1], [c2]
            rc = dve.op(lambda e: e.reciprocal(s_[:, 3:4], s_[:, 2:3]), [ex])
            return pt, [c1, c2], sslot, s_, rc

        def mla_values(it, hd, t_):
            pt, ready, sslot, s_, rc = it
            b = take1()
            for k in range(6):
                m = mm(bank(b, 64), pt.tiles[0][:, k * P:(k + 1) * P], v_all[:, k, hd * 64:(hd + 1) * 64], k == 0, k == 5,
                       ready + v_marks + bank_free[b], mark=True)
            pt.free = [m]
            d = ts(o_tok[:, t_, hd * 64:(hd + 1) * 64], bank(b, 64), s_[:, 3:4], None, ALU.mult, None, [m, rc])
            bank_free[b] = [d]
            sslot.free = [d]
            o_marks.append(d)

        seq = [(hd, t_) for hd in range(HEADS) for t_ in range(NT)]
        a1, a2 = {}, {}
        for n in range(len(seq) + 2):
            if n < len(seq):
                a1[n] = mla_scores(*seq[n])
            if 0 <= n - 1 < len(seq):
                a2[n - 1] = mla_turn(a1.pop(n - 1))
            if 0 <= n - 2 < len(seq):
                mla_values(a2.pop(n - 2), *seq[n - 2])
            if n < len(seq) and seq[n][0] + 1 < HEADS and seq[n][1] in beside:
                beside[seq[n][1]](seq[n][0] + 1)
        for t_ in range(NT):
            b = take1()
            for k in range(4):
                m = pe.op(lambda e, k=k, b=b, t_=t_: e.transpose(bank(b, P, k * P), o_tok[:, t_, k * P:(k + 1) * P], ident[:, :]),
                          o_marks + bank_free[b], mark=True)
            slot, w = work()
            wv = w.rearrange("p (k n) -> p k n", k=4)
            d = tt(dve, wv, bank(b).rearrange("p (k n) -> p k n", k=4), silu_dg[:, :, t_ * P:(t_ + 1) * P], ALU.mult, [m] + dg_marks + slot.free)
            bank_free[b] = [d]
            slot.free = split_pair(main_hi[:, 4:8, t_ * P:(t_ + 1) * P], main_lo[:, 4:8, t_ * P:(t_ + 1) * P], wv, [d] + h_read)
            attn_marks[t_] += slot.free
        fence()
        mla.close()
        cd.close()
        tail = ExitStack()
        g_row = sb(tail, "g_row", [P, D])
        b_row = sb(tail, "b_row", [P, D])
        free = pe.now() + dve.now() + act.now()
        rows_ready = [load(g_row[:, :], A["cd_ln_g"][0].partition_broadcast(P), free, s=row_sems[0]),
                      load(b_row[:, :], A["cd_ln_b"][0].partition_broadcast(P), s=row_sems[1])]
        wide_ring = Ring([Slot(sb(tail, "wide", [P, D])) for _ in range(2)])
        HALVES = ((0, L // 2), (L // 2, L // 2))

        def rms_turn(g_name, layer, t_, x_ready, banks):
            (slot, s_), ws = stat(), wide_ring.take()
            wide = ws.tiles[0]
            sq = actv(wide[:, :], X[:, t_, :], ACT.Square, [x_ready] + ws.free + slot.free, accum_out=s_[:, 0:1])
            r = rsqrt(s_[:, 1:2], s_[:, 0:1], 1, 1.0 / D, [sq])
            diag = wide[:, 0:P]
            d = ts(diag, ident[:, :], s_[:, 1:2], None, ALU.mult, None, [r, sq])
            slot.free = [d]
            marks, at_ = [], slice(t_ * P, (t_ + 1) * P)
            for h in range(2):
                b = banks[h]
                for j in range(4):
                    k = 4 * h + j
                    m = mm(bank(b, P, j * P), X[:, t_, k * P:(k + 1) * P], diag, True, True, [d] + bank_free[b], mark=j == 3)
                for j in range(4):
                    k = 4 * h + j
                    made_hi = actv(main_hi[:, k, at_], bank(b, P, j * P), ACT.Copy, [m], scale=col(g_name, 8 * layer + k))
                for j in range(4):
                    k = 4 * h + j
                    made_lo = stt(main_lo[:, k, at_], bank(b, P, j * P), col(g_name, 8 * layer + k), main_hi[:, k, at_].bitcast(F32),
                                  ALU.mult, ALU.subtract, [m, made_hi])
                bank_free[b] = [made_lo]
                marks += [made_hi, made_lo]
            ws.free = [m]
            return marks

        def follow_with(g_name, layer, x_new, ready):
            def follow(i):
                ready[i] += rms_turn(g_name, layer, i, x_new[i], (2 * i, 2 * i + 1))
            return follow if g_name else None

        def first_groups(groups, ready, follow):
            for half in range(2):
                marks = ready[2 * half] + ready[2 * half + 1]
                for n, (c, j, sink) in enumerate(groups):
                    project(c, j, P, h_hi, h_lo, HALVES[half:half + 1], marks, sink(half))
                    if half == 0 and n in (1, 2):
                        follow(n + 1)
                    if half == 1 and n == 1:
                        release(1)
                        prepare_chunk()

        x_marks, ready = [], [[] for _ in range(NT)]
        follow = follow_with("ffn1_pre_g_2", 0, x_marks, ready)
        down(KT, h_hi, h_lo, [t_ * P for t_ in range(NT)], lambda i, k: mix_marks[k] if k < 4 else attn_marks[i], x_sink, follow)
        tail.close()
        first.close()

        second = ExitStack()
        wide_ring = Ring([Slot(sb(second, "wide", [P, D])) for _ in range(2)])
        post_g = sb(second, "post_g", [P, D])
        post_free = pe.now() + act.now() + dve.now() + pool.now()

        def residual_rms(weight, g_ready, x_new):
            def sink(i, y, m):
                (slot, s_), ws = stat(), wide_ring.take()
                wide = ws.tiles[0]
                sq = actv(wide[:, :], y, ACT.Square, [m] + ws.free + slot.free, accum_out=s_[:, 0:1])
                r = rsqrt(s_[:, 1:2], s_[:, 0:1], 1, 1.0 / D, [sq], weight)
                d = stt(wide[:, :], y, s_[:, 1:2], post_g[:, :], ALU.mult, ALU.mult, [r, sq, g_ready])
                slot.free = [d]
                x_new[i] = tt(dve, X[:, i, :], X[:, i, :], wide[:, :], ALU.add, [d])
                ws.free = [x_new[i]]
                return [sq, d]
            return sink

        post_sem = [sem("post_g_landed"), 0]

        def ffn(f, layer, ready, follow, post_free, next_g, next_layer):
            scope = ExitStack()
            act_hi = sb(scope, "ff_hi", [P, FT, L], F32R)
            act_lo = sb(scope, "ff_lo", [P, FT, L], F32R)
            marks, gates = [[] for _ in range(FT)], []

            def gate_sink(r, ps, m):
                slot, w = work(ps.shape[-1])
                d = actv(w, ps, ACT.Silu, [m] + slot.free)
                gates.append((slot, w, d))
                return [d]

            def up_sink(k, off, n):
                def sink(r, ps, m):
                    slot, w, s_ = gates.pop(0)
                    d = tt(dve, w, w, ps, ALU.mult, [m, s_])
                    slot.free = split_pair(act_hi[:, k, off:off + n], act_lo[:, k, off:off + n], w, [d])
                    marks[k].extend(slot.free)
                    return [d]
                return sink

            c, c2 = next_chunk(), next_chunk(beside=True)
            first_groups([(c, j * P, lambda half: gate_sink) for j in range(2)] +
                         [(c2, j * P, lambda half, j=j: up_sink(j, *HALVES[half])) for j in range(2)], ready, follow)
            ready = sum(ready, [])
            g_ready = load(post_g[:, :], A[f"ffn{f}_post_g_2"][layer].partition_broadcast(P), post_free, s=post_sem)
            for ch in range(1, FF // CW):
                c = next_chunk()
                for j in range(2):
                    project(c, j * P, P, h_hi, h_lo, RANGES[:1], ready, gate_sink)
                c = next_chunk()
                for j in range(2):
                    project(c, j * P, P, h_hi, h_lo, RANGES[:1], ready, up_sink(2 * ch + j, 0, L))
            new, next_ready = [None] * NT, [[] for _ in range(NT)]
            follow = follow_with(next_g, next_layer, new, next_ready)
            down(FT, (act_hi, None), (act_lo, None), [t_ * P for t_ in range(NT)], lambda i, k: marks[k], residual_rms(0.5, g_ready, new), follow)
            scope.close()
            return new, next_ready, follow, pe.now() + act.now() + dve.now()

        def mixing(layer, ready, follow, post_free):
            lam_init = 0.8 - 0.6 * math.exp(-0.3 * layer)
            sc = ExitStack()
            q_a, k_a, q_c, k_c = (sb(sc, n, [P, 3, L]) for n in ("q_a", "k_a", "q_c", "k_c"))
            q_b, k_b = (sb(sc, n, [P, 2, L]) for n in ("q_b", "k_b"))
            v_a, v_c = (sb(sc, n, [P, NT, 384]) for n in ("v_a", "v_c"))
            v_b = sb(sc, "v_b", [P, NT, 256])
            far = sb(sc, "far_bias", [P, 6])
            dist = sb(sc, "distance", [P, L])
            strict = sb(sc, "strict", [P, 2, P])
            tri = sb(sc, "suffix_tri", [P, P])
            lam = sb(sc, "lambda", [P, 4, 32])
            lam_s = sb(sc, "lambda_stats", [P, 8])
            sub_g = sb(sc, "subln_g", [P, 64])
            bias = sb(sc, "band_bias", [P, 6, 256])
            o_tok = sb(sc, "o_tok", [P, NT, 640])
            squares = sb(sc, "squares", [P, 256])
            w0, w1 = (w.tiles[0] for w in wide_ring.slots)
            a_ring = Ring([Slot(w0[:, 0:L]), Slot(w0[:, L:D])])
            map_rings = [Ring([Slot(w1[:, 0:L]), Slot(w1[:, L:D])]), Ring([Slot(sb(sc, "scores", [P, L]))])]
            turned = {"a": Ring(work_ring.slots[0:2]), "b": Ring(work_ring.slots[2:3])}
            starts = {0: 0, 1: 512, 3: 896, 2: 1024}
            SW = 1280
            stick_ring = Ring([Slot(sb(sc, "softplus", [P, SW]), sb(sc, "log_weights", [P, SW])) for _ in range(2)])
            marks = {n: [] for n in "abc"}

            def put(dst, name, scale, off=0, n=L):
                def sink(r, ps, m):
                    d = actv(dst[:, off:off + n], ps, ACT.Copy, [m], scale=scale)
                    marks[name].append(d)
                    return [d]
                return sink

            feature = {}
            for i in range(3):
                feature[i * P] = (q_a[:, i, :], "a", 0.125)
                feature[384 + i * P] = (k_a[:, i, :], "a", 1.0)
                feature[1920 + i * P] = (q_c[:, i, :], "c", 0.125)
                feature[2304 + i * P] = (k_c[:, i, :], "c", 1.0)
            for i in range(2):
                feature[1152 + i * P] = (q_b[:, i, :], "b", 1.0)
                feature[1408 + i * P] = (k_b[:, i, :], "b", 1.0)
            pair = []
            for beside, (c0, n) in enumerate(MIX_CHUNKS[:2]):
                c = next_chunk(beside=bool(beside))
                pair += [(c, j * P, lambda half, f_=feature[c0 + j * P]: put(*f_, *HALVES[half])) for j in range(n // P)]
            first_groups(pair, ready, follow)
            ready = sum(ready, [])
            g_ready = load(post_g[:, :], A["mix_post_g_2"][layer].partition_broadcast(P), post_free, s=post_sem)
            consts = [sem(f"mix_consts_{layer}"), 0]
            for dst, src in ((bias[:, :, :], A["l_band_bias"][layer].rearrange("h q k -> q h k")),
                             (far[:, :], A["l_far_bias"][layer].partition_broadcast(P)),
                             (dist[:, :], A["k_distance"]), (strict[:, :, :], A["k_strict"].rearrange("s p n -> p s n")),
                             (tri[:, :], A["k_tri"]), (sub_g[:, :], A["diff_subln_g_2"][layer].partition_broadcast(P)),
                             (lam[:, 0, :], A["diff_lambda_q1_2"][layer].partition_broadcast(P)),
                             (lam[:, 1, :], A["diff_lambda_k1_2"][layer].partition_broadcast(P)),
                             (lam[:, 2, :], A["diff_lambda_q2_2"][layer].partition_broadcast(P)),
                             (lam[:, 3, :], A["diff_lambda_k2_2"][layer].partition_broadcast(P))):
                in_ = load(dst, src, post_free, s=consts)
            masked = pool.op(lambda e: e.memset(bias[0:64, :, 192:256], NEG), [in_])
            for i in range(2):
                d = tt(dve, lam[:, 2 * i, :], lam[:, 2 * i, :], lam[:, 2 * i + 1, :], ALU.mult, [in_])
                d = dve.op(lambda e, i=i: e.tensor_reduce(lam_s[:, i:i + 1], lam[:, 2 * i, :], AX.X, ALU.add), [d])
            ex = actv(lam_s[:, 2:4], lam_s[:, 0:2], ACT.Exp, [d])
            d = tt(dve, lam_s[:, 4:5], lam_s[:, 2:3], lam_s[:, 3:4], ALU.subtract, [ex])
            lam_ready = ts(lam_s[:, 5:6], lam_s[:, 4:5], -1.0, -lam_init, ALU.mult, ALU.add, [d])
            g_scaled = ts(sub_g[:, :], sub_g[:, :], 1.0 - lam_init, None, ALU.mult, None, [in_])

            values = ((768, 1152, v_a, "a"), (1664, 1920, v_b, "b"), (2688, 3072, v_c, "c"))
            proj_banks, soft_banks, stick_banks = Ring([0, 1]), Ring([2, 3, 4]), Ring([5, 6, 7])

            def a_scores(h, t_):
                width, p0 = (t_ + 1) * P, 64 * (h % 2)
                b = soft_banks.take()
                m = mm(bank(b, width), q_a[p0:p0 + 64, h // 2, t_ * P:(t_ + 1) * P], k_a[p0:p0 + 64, h // 2, 0:width], True, True,
                       marks["a"] + bank_free[b], mark=True)
                slot, (sslot, s_) = a_ring.take(), stat()
                w = slot.tiles[0][:, 0:width]
                near = min(width, 256)
                d = tt(dve, w[:, width - near:width], bank(b, near, width - near), bias[:, h, 256 - near:256], ALU.add, [m, masked] + slot.free)
                if width > near:
                    d = ts(w[:, 0:width - near], bank(b, width - near), far[:, h:h + 1], None, ALU.add, None, [m])
                bank_free[b] = [d]
                mx = dve.op(lambda e: e.tensor_reduce(s_[:, 0:1], w, AX.X, ALU.max, negate=True), [d] + sslot.free)
                ex = actv(w, w, ACT.Exp, [mx], bias=s_[:, 0:1], accum_out=s_[:, 1:2])
                return slot, w, sslot, s_, ex

            def b_scores(h, t_):
                width = (t_ + 1) * P
                sslot, s_ = stat()
                slope, sc_ = 2.0 ** (-8.0 * (h + 1) / 4), 32 ** -0.5
                maps = []
                for mp in range(2):
                    blk = 2 * h + mp
                    p0 = 32 * (blk % 4)
                    b = soft_banks.take()
                    m = mm(bank(b, width), q_b[p0:p0 + 32, blk // 4, t_ * P:(t_ + 1) * P], k_b[p0:p0 + 32, blk // 4, 0:width], True, True,
                           marks["b"] + bank_free[b], mark=True)
                    slot, o = map_rings[mp].take(), 4 * mp
                    w = slot.tiles[0][:, 0:width]
                    d = stt(w, dist[:, L - width:L], slope / sc_, bank(b, width), ALU.mult, ALU.add, [m, in_] + slot.free)
                    bank_free[b] = [d]
                    mx = dve.op(lambda e, o=o, w=w: e.tensor_reduce(s_[:, o:o + 1], w, AX.X, ALU.max), [d] + sslot.free)
                    mx = ts(s_[:, o + 1:o + 2], s_[:, o:o + 1], -sc_, None, ALU.mult, None, [mx])
                    ex = actv(w, w, ACT.Exp, [mx], bias=s_[:, o + 1:o + 2], scale=sc_, accum_out=s_[:, o + 2:o + 3])
                    maps.append((slot, w, ex))
                return maps, sslot, s_

            def b_weights(maps, sslot, s_):
                (slot0, w0_, ex0), (slot1, w1_, ex1) = maps
                rc = [dve.op(lambda e, o=o: e.reciprocal(s_[:, o + 3:o + 4], s_[:, o + 2:o + 3]), [ex])
                      for o, ex in ((0, ex0), (4, ex1))]
                d = tt(dve, s_[:, 8:9], s_[:, 7:8], lam_s[:, 5:6], ALU.mult, rc + [lam_ready])
                d = ts(w1_, w1_, s_[:, 8:9], None, ALU.mult, None, [d, ex1])
                d = stt(w0_, w0_, s_[:, 3:4], w1_, ALU.mult, ALU.add, rc + [d, ex0])
                slot1.free, sslot.free = [d], [d]
                return slot0, d

            def turn_probs(kind, slot, t_, ready):
                b = soft_banks.take()
                for k in range(t_ + 1):
                    m = pe.op(lambda e, k=k: e.transpose(bank(b, P, k * P), slot.tiles[0][:, k * P:(k + 1) * P], ident[:, :]),
                              [ready] + bank_free[b], mark=k == t_)
                slot.free = [m]
                pt = turned[kind].take()
                width = (t_ + 1) * P
                d = actv(pt.tiles[0][:, 0:width], bank(b, width), ACT.Copy, [m] + pt.free)
                bank_free[b] = [d]
                return pt, d

            def apply_values(kind, pt, ready, h, t_):
                b = soft_banks.take()
                v = v_a if kind == "a" else v_b
                for k in range(t_ + 1):
                    m = mm(bank(b, 64), pt.tiles[0][:, k * P:(k + 1) * P], v[:, k, h * 64:(h + 1) * 64], k == 0, k == t_,
                           [ready] + marks[kind] + bank_free[b], mark=k == t_)
                pt.free = [m]
                return b, m

            o_marks = [[] for _ in range(NT)]

            def band():
                scored, turned_, before = None, None, None
                for h, t_ in [(h, t_) for t_ in range(NT) for h in range(6)] + [(None, None)] * 3:
                    if before:
                        pt, d, sslot, s_, ex, h2, t2 = before
                        b, m = apply_values("a", pt, d, h2, t2)
                        rc = dve.op(lambda e, s_=s_: e.reciprocal(s_[:, 2:3], s_[:, 1:2]), [ex])
                        o = ts(o_tok[:, t2, h2 * 64:(h2 + 1) * 64], bank(b, 64), s_[:, 2:3], None, ALU.mult, None, [m, rc])
                        sslot.free, bank_free[b] = [o], [o]
                        o_marks[t2].append(o)
                    before = turned_
                    turned_ = scored and turn_probs("a", scored[0], scored[6], scored[4]) + scored[2:]
                    scored = None if h is None else a_scores(h, t_) + (h, t_)
                    yield

            def differential():
                scored, weighed, turned_ = None, None, None
                for h, t_ in [(h, t_) for t_ in range(NT) for h in range(4)] + [(None, None)] * 3:
                    if turned_:
                        pt, d, h3, t3 = turned_
                        b, m = apply_values("b", pt, d, h3, t3)
                        o = actv(o_tok[:, t3, 384 + h3 * 64:384 + (h3 + 1) * 64], bank(b, 64), ACT.Copy, [m])
                        bank_free[b] = [o]
                        o_marks[t3].append(o)
                    turned_ = weighed and turn_probs("b", weighed[0], weighed[3], weighed[1]) + weighed[2:]
                    weighed = scored and b_weights(*scored[:3]) + scored[3:]
                    scored = None if h is None else b_scores(h, t_) + (h, t_)
                    yield

            def stick_scores(h):
                p0 = 64 * (h % 2)
                slot = stick_ring.take()
                soft, z = slot.tiles
                copied = []
                for tiles, o, n in (((0,), 0, 512), ((1, 3), 512, 512), ((2,), 1024, 256)):
                    b = stick_banks.take()
                    for kt in tiles:
                        m = mm(bank(b, L - kt * P, starts[kt] - o), k_c[p0:p0 + 64, h // 2, kt * P:(kt + 1) * P], q_c[p0:p0 + 64, h // 2, kt * P:L],
                               True, True, marks["c"] + bank_free[b], mark=True)
                    zc = actv(z[:, o:o + n], bank(b, n), ACT.Copy, [m] + slot.free)
                    bank_free[b] = [zc]
                    copied.append(zc)
                return slot, copied + slot.free

            def stick_abs(slot, ready):
                soft, z = slot.tiles
                return stt(soft[:, :], z[:, :], -1.0, z[:, :], ALU.mult, ALU.min, ready)

            def stick_log(slot, ready):
                soft = slot.tiles[0]
                a_ = actv(soft[:, :], soft[:, :], ACT.Exp, [ready])
                return actv(soft[:, :], soft[:, :], ACT.Ln, [a_], bias=1.0)

            def stick_mask(slot, a_):
                soft, z = slot.tiles
                d = stt(soft[:, :], z[:, :], 0.0, soft[:, :], ALU.max, ALU.add, [a_])
                for kt in range(NT):
                    o = starts[kt]
                    dm = tt(pool, soft[:, o:o + P], soft[:, o:o + P], strict[:, 0, :], ALU.mult, [d, in_])
                    da = tt(pool, z[:, o:o + P], z[:, o:o + P], strict[:, 1, :], ALU.add, [d])
                return [dm, da]

            def stick_sums(slot, kt, ready):
                soft, z = slot.tiles
                width, o = L - kt * P, starts[kt]
                b = stick_banks.take()
                m = mm(bank(b, width), tri[:, :], soft[:, o:o + width], True, kt == 3, ready + bank_free[b], mark=True)
                for k2 in range(kt + 1, NT):
                    w2, o2 = L - k2 * P, starts[k2]
                    m = mm(bank(b, w2, (k2 - kt) * P), ones[:, :], soft[:, o2:o2 + w2], False, k2 == 3, mark=True)
                d = tt(dve, z[:, o:o + width], z[:, o:o + width], bank(b, width), ALU.subtract, [m] + ready)
                bank_free[b] = [d]
                return d

            def stick_values(h, slot, w_ready):
                p0, b = 64 * (h % 2), stick_banks.take()
                z = slot.tiles[1]
                for kt in range(NT):
                    width, o = L - kt * P, starts[kt]
                    m = mm(psum[p0:p0 + 64, b * BANK + kt * P:(b + 1) * BANK], v_c[:, kt, h * 64:(h + 1) * 64], z[:, o:o + width],
                           kt == 0, kt == 3, [w_ready] + marks["c"] + bank_free[b], mark=True)
                slot.free = [m]
                d = actv(q_c[p0:p0 + 64, h // 2, :], psum[p0:p0 + 64, b * BANK:(b + 1) * BANK], ACT.Copy, [m])
                bank_free[b] = [d]
                return d

            stick_marks = []

            def stick():
                slot, d = stick_scores(0)
                yield
                d = stick_abs(slot, d)
                yield
                d = stick_log(slot, d)
                yield
                masked_ = stick_mask(slot, d)
                yield
                for h in range(6):
                    d = stick_sums(slot, 0, masked_)
                    following = stick_scores(h + 1) if h < 5 else None
                    yield
                    for kt, make in ((1, stick_abs), (2, stick_log), (3, stick_mask)):
                        d = stick_sums(slot, kt, masked_)
                        if following:
                            following = (following[0], make(*following))
                        yield
                    w_ready = actv(slot.tiles[1][:, :], slot.tiles[1][:, :], ACT.Exp, [d])
                    yield
                    stick_marks.append(stick_values(h, slot, w_ready))
                    if following:
                        slot, masked_ = following
                    yield

            def projection():
                for c0, n in MIX_CHUNKS[2:]:
                    c = next_chunk()
                    v = [x for x in values if x[0] <= c0 < x[1]]
                    if v:
                        lo_, _, dst, name = v[0]

                        def v_sink(t_, ps, m, dst=dst, name=name, at_=c0 - lo_, n=n):
                            d = actv(dst[:, t_, at_:at_ + n], ps, ACT.Copy, [m])
                            marks[name].append(d)
                            return [d]
                        for t_ in range(NT):
                            project_tokens(c, h_hi, h_lo, [t_], ready, v_sink, proj_banks.take)
                            if t_ % 2:
                                yield c0
                    else:
                        for j in range(n // P):
                            project(c, j * P, P, h_hi, h_lo, RANGES[:1], ready, put(*feature[c0 + j * P]), proj_banks.take)
                            yield c0

            tile_marks = [[] for _ in range(NT)]

            def assemble():
                for t_ in range(NT):
                    while len(o_marks[t_]) < 10:
                        yield
                    sslot, s_ = stat()
                    ob = o_tok[:, t_, 384:640]
                    d = tt(dve, squares[:, :], ob, ob, ALU.mult, o_marks[t_] + sslot.free)
                    d = dve.op(lambda e, s_=s_: e.tensor_reduce(s_[:, 0:4], squares[:, :].rearrange("p (h c) -> p h c", h=4), AX.X, ALU.add), [d])
                    r = rsqrt(s_[:, 4:8], s_[:, 0:4], 4, 1.0 / 64, [d])
                    yield
                    ov = ob.rearrange("p (h c) -> p h c", h=4)
                    d = tt(dve, ov, ov, s_[:, 4:8].unsqueeze(2).broadcast_to([P, 4, 64]), ALU.mult, [r])
                    sslot.free = [d]
                    d = tt(dve, ov, ov, sub_g[:, :].unsqueeze(1).broadcast_to([P, 4, 64]), ALU.mult, [d, g_scaled])
                    for k0, k1 in ((0, 3), (3, 5)):
                        b, n = soft_banks.take(), k1 - k0
                        for k in range(k0, k1):
                            m = pe.op(lambda e, k=k, b=b, t_=t_, k0=k0: e.transpose(bank(b, P, (k - k0) * P), o_tok[:, t_, k * P:(k + 1) * P], ident[:, :]),
                                      o_marks[t_] + bank_free[b] + ([d] if k0 else []), mark=True)
                        pv = bank(b, n * P).rearrange("p (k n) -> p k n", k=n)
                        bank_free[b] = split_pair(main_hi[:, k0:k1, t_ * P:(t_ + 1) * P], main_lo[:, k0:k1, t_ * P:(t_ + 1) * P], pv, [m] + h_read)
                        tile_marks[t_] += bank_free[b]

            projecting, streams = projection(), []
            sticks, bands, differentials = stick(), band(), differential()
            starts_after = {0: sticks, 1152: bands, None: differentials}
            c0 = 0
            while c0 is not None:
                c0 = next(projecting, None)
                stream = starts_after.pop(c0, None)
                if stream:
                    streams.append(stream)
                for stream in streams + streams[1:2]:
                    next(stream, None)
            h_read = pe.now()
            assembling = assemble()
            soft_banks.slots += proj_banks.slots
            live = streams
            stick_split = False
            while live:
                live = [s_ for s_ in live if next(s_, "over") != "over"]
                if len(stick_marks) == 6 and not stick_split:
                    stick_split = True
                    for i in range(3):
                        got = split_pair(main_hi[:, 5 + i, :], main_lo[:, 5 + i, :], q_c[:, i, :], stick_marks + h_read)
                        for tm in tile_marks:
                            tm.extend(got)
                next(assembling, None)
            for _ in assembling:
                pass
            for w in wide_ring.slots + work_ring.slots:
                w.free = pe.now() + dve.now() + act.now()
            new, next_ready = [None] * NT, [[] for _ in range(NT)]
            follow = follow_with("ffn2_pre_g_2", layer, new, next_ready)
            down(KT, h_hi, h_lo, [t_ * P for t_ in range(NT)], lambda i, k: tile_marks[i], residual_rms(1.0, g_ready, new), follow)
            sc.close()
            return new, next_ready, follow, pe.now() + act.now() + dve.now()

        for layer in range(DEPTH):
            _, ready, follow, post_free = ffn(1, layer, ready, follow, post_free, "mix_pre_g_2", layer)
            _, ready, follow, post_free = mixing(layer, ready, follow, post_free)
            more = layer + 1 < DEPTH
            x_ready, ready, follow, post_free = ffn(2, layer, ready, follow, post_free, "ffn1_pre_g_2" if more else None, layer + 1)
        stored = [sem("stored"), 0]
        for t_ in range(NT):
            last = load(out[0, t_ * P:(t_ + 1) * P, :], X[:, t_, :], [x_ready[t_]], s=stored)
        sp.wait([last])
        second.close()

        block = ctx.enter_context(nc.Block())

        def play(engine, eng):
            for step in engine.queue:
                step(eng)

        block.sync(lambda e: play(sp, e))
        block.tensor(lambda e: play(pe, e))
        block.scalar(lambda e: play(act, e))
        block.vector(lambda e: play(dve, e))
        block.gpsimd(lambda e: play(pool, e))


def shape_constants():
    k = {}
    k["k_ident"] = np.eye(P)
    d = 2 * np.pi * (np.outer(np.arange(P), np.arange(P)) % P) / P
    k["k_dft_d"] = np.concatenate([np.cos(d), np.sin(d)], 1)
    a = 2 * np.pi * (np.outer(np.arange(L), np.arange(L)) % L) / L
    k["k_dft_l"] = np.stack([np.cos(a), -np.sin(a)], 1) / np.sqrt(L * P)
    tok = np.arange(L)
    inv = 10000.0 ** (-np.arange(0, 16, 2) / 16)
    ang = [np.outer(inv, tok // 64), np.outer(inv, tok % 64)]
    cos, sin = np.ones((QK, L)), np.zeros((QK, L))
    swap = np.zeros((QK, QK))
    for i in range(2):
        r = NOPE + 16 * i
        cos[r:r + 8] = cos[r + 8:r + 16] = np.cos(ang[i])
        sin[r:r + 8], sin[r + 8:r + 16] = -np.sin(ang[i]), np.sin(ang[i])
        for j in range(8):
            swap[r + 8 + j, r + j] = swap[r + j, r + 8 + j] = 1
    k["k_rope_cos"], k["k_rope_sin"], k["k_rope_swap"] = cos, sin, swap
    rows = []
    for w in POOL_WINDOWS:
        row = []
        for n in (L, LC):
            t = np.arange(n)
            row.append(1.0 / (np.clip(t + w - w // 2, 0, n) - np.clip(t - w // 2, 0, n)))
        rows.append(np.concatenate(row))
    k["k_inv_count"] = np.stack(rows)
    q, c = np.arange(P)[:, None], np.arange(L)[None]
    dist = -np.abs(q + L - P - c).astype(np.float64)
    dist[0:64, L - 64:] = NEG
    k["k_distance"] = dist
    s, t = np.arange(P)[:, None], np.arange(P)[None]
    k["k_strict"] = np.stack([(s < t) * 1.0, np.where(s < t, 0.0, NEG)])
    k["k_tri"] = (s >= t) * 1.0
    return {n: np.ascontiguousarray(v, dtype=np.float32) for n, v in k.items()}


def kernel(**inputs):
    import concourse.bacc as bacc
    from concourse.bass_utils import run_bass_kernel_spmd as run

    nc = bacc.Bacc("TRN2", target_bir_lowering=False, num_devices=1)
    arrays = {n: np.ascontiguousarray(v) for n, v in inputs.items()}
    arrays.update(shape_constants())
    rb = arrays["rel_bias_2"]
    flipped = np.concatenate([np.repeat(rb[:, :, 256:257], P - 1, axis=2), rb[:, :, :0:-1]], axis=2)
    idx = np.arange(256)[None] - np.arange(P)[:, None] + P - 1
    arrays["l_band_bias"] = np.ascontiguousarray(flipped[:, :, idx])
    arrays["l_far_bias"] = np.ascontiguousarray(rb[:, :, 256])
    A = {n: nc.dram_tensor(f"in_{n}", a.shape, mybir.dt.from_np(a.dtype), kind="ExternalInput").ap()
         for n, a in arrays.items()}
    out = nc.dram_tensor("out_x", (1, L, D), F32, kind="ExternalOutput").ap()
    build(nc, A, out)
    r = run(nc, [{f"in_{n}": a for n, a in arrays.items()}], core_ids=[0])
    return r.results[0]["out_x"]
```
